# Optimizing a Trainium2 kernel written in Bass

```python
import jax, jax.numpy as jnp
from jax import lax
import numpy as np
import math

D_MODEL = 1024
BATCH = 1
SEQ = 256
DEPTH = 2

N_A_LAYERS = DEPTH // 2
N_B_LAYERS = DEPTH - N_A_LAYERS
CHUNK = 128
GMLP_WIDTH = 2 * D_MODEL
GMLP_GROUPS = 16
GMLP_GROUP_DIM = GMLP_WIDTH // GMLP_GROUPS
N_HEADS = 16
HEAD_DIM = D_MODEL // N_HEADS
Q_BLOCK = 128
FFN_HIDDEN = -(-8 * D_MODEL // (3 * 256)) * 256
EPS = 1e-6


def rms_norm(x, g):
    xf = x.astype(jnp.float32)
    y = xf * lax.rsqrt(jnp.mean(xf * xf, axis=-1, keepdims=True) + EPS)
    return (y * g.astype(jnp.float32)).astype(x.dtype)

def layer_norm(x, g, b):
    xf = x.astype(jnp.float32)
    mu = jnp.mean(xf, axis=-1, keepdims=True)
    xc = xf - mu
    y = xc * lax.rsqrt(jnp.mean(xc * xc, axis=-1, keepdims=True) + EPS)
    return (y * g.astype(jnp.float32) + b.astype(jnp.float32)).astype(x.dtype)

def modulate(h, shift, scale):
    return h * (1 + scale[:, None, :]) + shift[:, None, :]

def swiglu(h, w_gu, w_down):
    gu = h @ w_gu
    g, u = jnp.split(gu, 2, axis=-1)
    return (jax.nn.silu(g) * u) @ w_down

def gmlp_mixer(h, w_in, b_in, ln_g, ln_b, w_s, b_s, w_out):
    B, S, _ = h.shape
    z = jax.nn.gelu(h @ w_in + b_in)
    u, v = jnp.split(z, 2, axis=-1)
    v = layer_norm(v, ln_g, ln_b)
    v = v.reshape(B, S // CHUNK, CHUNK, GMLP_GROUPS, GMLP_GROUP_DIM)
    causal = jnp.tril(jnp.ones((CHUNK, CHUNK), dtype=w_s.dtype))
    ws = w_s * causal[None]
    v = jnp.einsum('gts,bnsgc->bntgc', ws, v) + b_s.T[:, :, None]
    y = u * v.reshape(B, S, GMLP_WIDTH)
    return y @ w_out

def shared_kv(x, mod_kv, kv_norm_g, kv_w, kv_b_f, k_norm_g):
    B, S, _ = x.shape
    shift, scale = jnp.split(mod_kv, 2, axis=-1)
    h = modulate(rms_norm(x, kv_norm_g), shift, scale)
    kvf = h @ kv_w
    k = kvf[..., :D_MODEL].reshape(B, S, N_HEADS, HEAD_DIM)
    k = rms_norm(k, k_norm_g).transpose(0, 2, 1, 3)
    v = kvf[..., D_MODEL:2 * D_MODEL].reshape(B, S, N_HEADS, HEAD_DIM).transpose(0, 2, 1, 3)
    f_logit = kvf[..., 2 * D_MODEL:].astype(jnp.float32) + kv_b_f.astype(jnp.float32)
    dcum = jnp.cumsum(jax.nn.log_sigmoid(f_logit), axis=1).transpose(0, 2, 1)
    return k, v, dcum

def fox_attention(q, k, v, dcum):
    B, H, S, Dh = q.shape
    nb = S // Q_BLOCK
    qb = q.reshape(B, H, nb, Q_BLOCK, Dh).transpose(2, 0, 1, 3, 4)
    db = dcum.reshape(B, H, nb, Q_BLOCK).transpose(2, 0, 1, 3)
    kpos = jnp.arange(S)
    scale = HEAD_DIM ** -0.5

    def block(args):
        qi, di, i = args
        qpos = i * Q_BLOCK + jnp.arange(Q_BLOCK)
        logits = jnp.einsum('bhqd,bhkd->bhqk', qi, k).astype(jnp.float32) * scale
        logits = logits + di[..., :, None] - dcum[..., None, :]
        logits = jnp.where(kpos[None, :] <= qpos[:, None], logits, -jnp.inf)
        p = jax.nn.softmax(logits, axis=-1)
        return jnp.einsum('bhqk,bhkd->bhqd', p.astype(v.dtype), v)

    o = lax.map(block, (qb, db, jnp.arange(nb)))
    return o.transpose(1, 2, 0, 3, 4).reshape(B, H, S, Dh)

def fox_mixer(h, w_qg, q_norm_g, w_o, k, v, dcum):
    B, S, _ = h.shape
    qg = h @ w_qg
    q = qg[..., :D_MODEL].reshape(B, S, N_HEADS, HEAD_DIM)
    q = rms_norm(q, q_norm_g).transpose(0, 2, 1, 3)
    gate = jax.nn.sigmoid(qg[..., D_MODEL:])
    o = fox_attention(q, k, v, dcum).transpose(0, 2, 1, 3).reshape(B, S, D_MODEL)
    return (o * gate) @ w_o

def first_inputs(seed: int = 0) -> dict:
    key = jax.random.key(seed)
    ks = jax.random.split(key, 26)
    D, F, GW = D_MODEL, FFN_HIDDEN, GMLP_WIDTH

    def nrm(k, shape, scale):
        return jax.random.normal(k, shape, jnp.float32) * scale

    def gain(k, shape):
        return 1.0 + nrm(k, shape, 0.05)

    return {
        "x": nrm(ks[0], (BATCH, SEQ, D), 1.0),
        "c": nrm(ks[1], (BATCH, D), 1.0),
        "ada_w": nrm(ks[2], (DEPTH, D, 6 * D), 0.5 * D ** -0.5),
        "ada_b": nrm(ks[3], (DEPTH, 6 * D), 0.01),
        "pre_mix_g": gain(ks[4], (DEPTH, D)),
        "post_mix_g": gain(ks[5], (DEPTH, D)),
        "pre_ffn_g": gain(ks[6], (DEPTH, D)),
        "post_ffn_g": gain(ks[7], (DEPTH, D)),
        "ffn_w_gu": nrm(ks[8], (DEPTH, D, 2 * F), D ** -0.5),
        "ffn_w_down": nrm(ks[9], (DEPTH, F, D), F ** -0.5),
        "a_w_in": nrm(ks[10], (N_A_LAYERS, D, 2 * GW), D ** -0.5),
        "a_b_in": nrm(ks[11], (N_A_LAYERS, 2 * GW), 0.01),
        "a_ln_g": gain(ks[12], (N_A_LAYERS, GW)),
        "a_ln_b": nrm(ks[13], (N_A_LAYERS, GW), 0.01),
        "a_w_s": nrm(ks[14], (N_A_LAYERS, GMLP_GROUPS, CHUNK, CHUNK), 0.5 * CHUNK ** -0.5),
        "a_b_s": 1.0 + nrm(ks[15], (N_A_LAYERS, GMLP_GROUPS, CHUNK), 0.1),
        "a_w_out": nrm(ks[16], (N_A_LAYERS, GW, D), GW ** -0.5),
        "kv_ada_w": nrm(ks[17], (D, 2 * D), 0.5 * D ** -0.5),
        "kv_ada_b": nrm(ks[18], (2 * D,), 0.01),
        "kv_norm_g": gain(ks[19], (D,)),
        "kv_w": nrm(ks[20], (D, 2 * D + N_HEADS), D ** -0.5),
        "kv_b_f": jax.random.uniform(ks[21], (N_HEADS,), jnp.float32, 1.0, 5.0),
        "k_norm_g": gain(ks[22], (HEAD_DIM,)),
        "b_w_qg": nrm(ks[23], (N_B_LAYERS, D, 2 * D), D ** -0.5),
        "b_q_norm_g": gain(ks[24], (N_B_LAYERS, HEAD_DIM)),
        "b_w_o": nrm(ks[25], (N_B_LAYERS, D, D), D ** -0.5),
    }

def first_block(x, c, ada_w, ada_b, pre_mix_g, post_mix_g, pre_ffn_g, post_ffn_g,
              ffn_w_gu, ffn_w_down, a_w_in, a_b_in, a_ln_g, a_ln_b, a_w_s, a_b_s,
              a_w_out, kv_ada_w, kv_ada_b, kv_norm_g, kv_w, kv_b_f, k_norm_g,
              b_w_qg, b_q_norm_g, b_w_o):
    c_act = jax.nn.silu(c)
    k = v = dcum = None
    for layer in range(DEPTH):
        mod = c_act @ ada_w[layer] + ada_b[layer]
        sh_m, sc_m, g_m, sh_f, sc_f, g_f = jnp.split(mod, 6, axis=-1)
        h = modulate(rms_norm(x, pre_mix_g[layer]), sh_m, sc_m)
        if layer < N_A_LAYERS:
            i = layer
            y = gmlp_mixer(h, a_w_in[i], a_b_in[i], a_ln_g[i], a_ln_b[i],
                           a_w_s[i], a_b_s[i], a_w_out[i])
        else:
            j = layer - N_A_LAYERS
            y = fox_mixer(h, b_w_qg[j], b_q_norm_g[j], b_w_o[j], k, v, dcum)
        x = x + g_m[:, None, :] * rms_norm(y, post_mix_g[layer])
        h = modulate(rms_norm(x, pre_ffn_g[layer]), sh_f, sc_f)
        y = swiglu(h, ffn_w_gu[layer], ffn_w_down[layer])
        x = x + g_f[:, None, :] * rms_norm(y, post_ffn_g[layer])
        if layer == N_A_LAYERS - 1:
            k, v, dcum = shared_kv(x, c_act @ kv_ada_w + kv_ada_b, kv_norm_g,
                                   kv_w, kv_b_f, k_norm_g)
    return x


CHUNK_2 = 64
HEAD_DIM_2 = 64
ROPE_THETA = 10000.0
D_FF = 2816
DSA_Q_BLOCK = 32
A_HEADS = D_MODEL // (4 * HEAD_DIM_2)
A_VDIM = 2 * HEAD_DIM_2
B_HEADS = D_MODEL // (2 * HEAD_DIM_2)
IDX_HEADS = 8
IDX_DIM = 32
TOPK_MAX = 256
C_HEADS = D_MODEL // HEAD_DIM_2
C_LEFT_CHUNKS = 8
MAX_REL = 256
REL_TABLE = MAX_REL + CHUNK_2

MIX_WIDTH = A_HEADS * A_VDIM + B_HEADS * HEAD_DIM_2
EVEN_SIZES = (2 * A_HEADS * HEAD_DIM_2, 2 * A_HEADS * HEAD_DIM_2, A_HEADS * A_VDIM,
              B_HEADS * HEAD_DIM_2, B_HEADS * HEAD_DIM_2, B_HEADS * HEAD_DIM_2,
              IDX_HEADS * IDX_DIM, IDX_DIM, IDX_HEADS)
EVEN_PROJ = sum(EVEN_SIZES)
EVEN_SPLITS = [sum(EVEN_SIZES[:i + 1]) for i in range(len(EVEN_SIZES) - 1)]


def rmsnorm(x, g):
    xf = x.astype(jnp.float32)
    y = xf * lax.rsqrt(jnp.mean(xf * xf, axis=-1, keepdims=True) + EPS)
    return (y * g.astype(jnp.float32)).astype(x.dtype)

def rope_tables(seq, dim):
    inv = ROPE_THETA ** (-jnp.arange(0, dim, 2, dtype=jnp.float32) / dim)
    ang = jnp.arange(seq, dtype=jnp.float32)[:, None] * inv[None, :]
    return jnp.cos(ang), jnp.sin(ang)

def apply_rope(x, cos, sin):
    xf = x.astype(jnp.float32)
    x1, x2 = jnp.split(xf, 2, axis=-1)
    c = cos[:, None, :]
    s = sin[:, None, :]
    return jnp.concatenate([x1 * c - x2 * s, x2 * c + x1 * s], axis=-1).astype(x.dtype)

def masked_softmax(s, mask):
    return jax.nn.softmax(jnp.where(mask, s, -jnp.inf), axis=-1)

def swiglu_2(h, wg, wu, wd):
    return (jax.nn.silu(h @ wg) * (h @ wu)) @ wd

def diff_attention(q, k, v, lam, subln, lambda_init):
    B_, S_ = q.shape[0], q.shape[1]
    nb = S_ // Q_BLOCK
    qb = q.reshape(B_, nb, Q_BLOCK, A_HEADS, 2, HEAD_DIM_2).swapaxes(0, 1)
    kf = k.astype(jnp.float32)
    vf = v.astype(jnp.float32)
    kchunk = jnp.arange(S_) // CHUNK_2
    scale = HEAD_DIM_2 ** -0.5

    def one_block(args):
        bi, qblk = args
        qpos = bi * Q_BLOCK + jnp.arange(Q_BLOCK)
        mask = kchunk[None, :] <= (qpos // CHUNK_2)[:, None]
        s = jnp.einsum('bqhcd,bkhcd->bhcqk', qblk.astype(jnp.float32), kf) * scale
        p = masked_softmax(s, mask)
        w = p[:, :, 0] - lam * p[:, :, 1]
        return jnp.einsum('bhqk,bkhe->bqhe', w, vf)

    o = lax.map(one_block, (jnp.arange(nb), qb))
    o = o.swapaxes(0, 1).reshape(B_, S_, A_HEADS, A_VDIM)
    o = rmsnorm(o, subln) * (1.0 - lambda_init)
    return o.reshape(B_, S_, A_HEADS * A_VDIM).astype(v.dtype)

def dsa_attention(q, k, v, qi, ki, wi, topk):
    B_, S_ = q.shape[0], q.shape[1]
    nb = S_ // DSA_Q_BLOCK
    qb = q.reshape(B_, nb, DSA_Q_BLOCK, B_HEADS, HEAD_DIM_2).swapaxes(0, 1)
    qib = qi.reshape(B_, nb, DSA_Q_BLOCK, IDX_HEADS, IDX_DIM).swapaxes(0, 1)
    wib = wi.reshape(B_, nb, DSA_Q_BLOCK, IDX_HEADS).swapaxes(0, 1)
    kf = k.astype(jnp.float32)
    vf = v.astype(jnp.float32)
    kif = ki.astype(jnp.float32)
    kchunk = jnp.arange(S_) // CHUNK_2
    scale = HEAD_DIM_2 ** -0.5
    gather = jax.vmap(lambda kk, ii: kk[ii])

    def one_block(args):
        bi, qblk, qiblk, wiblk = args
        qpos = bi * DSA_Q_BLOCK + jnp.arange(DSA_Q_BLOCK)
        qchunk = qpos // CHUNK_2
        rel = jax.nn.relu(jnp.einsum('bqhd,bkd->bqhk', qiblk.astype(jnp.float32), kif))
        score = jnp.einsum('bqhk,bqh->bqk', rel, wiblk.astype(jnp.float32))
        mask = kchunk[None, :] <= qchunk[:, None]
        score = jnp.where(mask[None], score, -jnp.inf)
        _, idx = lax.top_k(score, topk)
        valid = (idx // CHUNK_2) <= qchunk[None, :, None]
        kg = gather(kf, idx)
        vg = gather(vf, idx)
        s = jnp.einsum('bqhd,bqkhd->bhqk', qblk.astype(jnp.float32), kg) * scale
        p = masked_softmax(s, valid[:, None])
        return jnp.einsum('bhqk,bqkhd->bqhd', p, vg)

    o = lax.map(one_block, (jnp.arange(nb), qb, qib, wib))
    return o.swapaxes(0, 1).reshape(B_, S_, B_HEADS * HEAD_DIM_2).astype(v.dtype)

def chunk_band_attention(q, k, v, rel_bias):
    B_, S_ = q.shape[0], q.shape[1]
    nc = S_ // CHUNK_2
    left = C_LEFT_CHUNKS * CHUNK_2
    band = left + CHUNK_2
    kp = jnp.pad(k.astype(jnp.float32), ((0, 0), (left, 0), (0, 0), (0, 0)))
    vp = jnp.pad(v.astype(jnp.float32), ((0, 0), (left, 0), (0, 0), (0, 0)))
    dist = left + jnp.arange(CHUNK_2)[:, None] - jnp.arange(band)[None, :]
    bias_idx = jnp.clip(dist, -(CHUNK_2 - 1), MAX_REL) + (CHUNK_2 - 1)
    bias = rel_bias.astype(jnp.float32)[:, bias_idx]
    qc = q.reshape(B_, nc, CHUNK_2, C_HEADS, HEAD_DIM_2).swapaxes(0, 1)
    scale = HEAD_DIM_2 ** -0.5

    def one_chunk(args):
        ci, qblk = args
        kb = lax.dynamic_slice_in_dim(kp, ci * CHUNK_2, band, axis=1)
        vb = lax.dynamic_slice_in_dim(vp, ci * CHUNK_2, band, axis=1)
        valid = (ci * CHUNK_2 - left + jnp.arange(band)) >= 0
        s = jnp.einsum('bqhd,bkhd->bhqk', qblk.astype(jnp.float32), kb) * scale + bias[None]
        p = masked_softmax(s, valid[None, None, None, :])
        return jnp.einsum('bhqk,bkhd->bqhd', p, vb)

    o = lax.map(one_chunk, (jnp.arange(nc), qc))
    return o.swapaxes(0, 1).reshape(B_, S_, C_HEADS * HEAD_DIM_2).astype(v.dtype)

def even_mixer(h, w_in, w_out, lam_p, subln, rope64, rope32, lambda_init, topk):
    B_, S_ = h.shape[0], h.shape[1]
    cos64, sin64 = rope64
    cos32, sin32 = rope32
    a_q, a_k, a_v, b_q, b_k, b_v, i_q, i_k, i_w = jnp.split(h @ w_in, EVEN_SPLITS, axis=-1)
    a_q = apply_rope(a_q.reshape(B_, S_, 2 * A_HEADS, HEAD_DIM_2), cos64, sin64).reshape(B_, S_, A_HEADS, 2, HEAD_DIM_2)
    a_k = apply_rope(a_k.reshape(B_, S_, 2 * A_HEADS, HEAD_DIM_2), cos64, sin64).reshape(B_, S_, A_HEADS, 2, HEAD_DIM_2)
    a_v = a_v.reshape(B_, S_, A_HEADS, A_VDIM)
    lp = lam_p.astype(jnp.float32)
    lam = jnp.exp(jnp.sum(lp[0] * lp[1])) - jnp.exp(jnp.sum(lp[2] * lp[3])) + lambda_init
    o_a = diff_attention(a_q, a_k, a_v, lam, subln, lambda_init)
    b_q = apply_rope(b_q.reshape(B_, S_, B_HEADS, HEAD_DIM_2), cos64, sin64)
    b_k = apply_rope(b_k.reshape(B_, S_, B_HEADS, HEAD_DIM_2), cos64, sin64)
    b_v = b_v.reshape(B_, S_, B_HEADS, HEAD_DIM_2)
    i_q = apply_rope(i_q.reshape(B_, S_, IDX_HEADS, IDX_DIM), cos32, sin32)
    i_k = apply_rope(i_k.reshape(B_, S_, 1, IDX_DIM), cos32, sin32)[:, :, 0]
    i_w = i_w * (IDX_HEADS ** -0.5 * IDX_DIM ** -0.5)
    o_b = dsa_attention(b_q, b_k, b_v, i_q, i_k, i_w, topk)
    return jnp.concatenate([o_a, o_b], axis=-1) @ w_out

def odd_mixer(h, w_in, w_out, rel_bias):
    B_, S_ = h.shape[0], h.shape[1]
    q, k, v = jnp.split(h @ w_in, 3, axis=-1)
    q = q.reshape(B_, S_, C_HEADS, HEAD_DIM_2)
    k = k.reshape(B_, S_, C_HEADS, HEAD_DIM_2)
    v = v.reshape(B_, S_, C_HEADS, HEAD_DIM_2)
    return chunk_band_attention(q, k, v, rel_bias) @ w_out

def second_inputs(seed: int = 0) -> dict:
    key = jax.random.key(seed)
    ks = jax.random.split(key, 12)
    n_even = (DEPTH + 1) // 2
    n_odd = DEPTH // 2
    nrm = jax.random.normal
    f32 = jnp.float32
    return {
        "x": nrm(ks[0], (BATCH, SEQ, D_MODEL), f32),
        "norm_g": 1.0 + 0.01 * nrm(ks[1], (DEPTH, 6, D_MODEL), f32),
        "ffn_wg": nrm(ks[2], (DEPTH, 2, D_MODEL, D_FF), f32) * D_MODEL ** -0.5,
        "ffn_wu": nrm(ks[3], (DEPTH, 2, D_MODEL, D_FF), f32) * D_MODEL ** -0.5,
        "ffn_wd": nrm(ks[4], (DEPTH, 2, D_FF, D_MODEL), f32) * D_FF ** -0.5,
        "even_w_in": nrm(ks[5], (n_even, D_MODEL, EVEN_PROJ), f32) * D_MODEL ** -0.5,
        "even_w_out": nrm(ks[6], (n_even, MIX_WIDTH, D_MODEL), f32) * MIX_WIDTH ** -0.5,
        "even_lambda": 0.1 * nrm(ks[7], (n_even, 4, HEAD_DIM_2), f32),
        "even_subln": 1.0 + 0.01 * nrm(ks[8], (n_even, A_VDIM), f32),
        "odd_w_in": nrm(ks[9], (n_odd, D_MODEL, 3 * D_MODEL), f32) * D_MODEL ** -0.5,
        "odd_w_out": nrm(ks[10], (n_odd, D_MODEL, D_MODEL), f32) * D_MODEL ** -0.5,
        "odd_rel_bias": 0.1 * nrm(ks[11], (n_odd, C_HEADS, REL_TABLE), f32),
    }

def second_block(x, norm_g, ffn_wg, ffn_wu, ffn_wd, even_w_in, even_w_out, even_lambda, even_subln,
              odd_w_in, odd_w_out, odd_rel_bias):
    S_ = x.shape[1]
    topk = min(TOPK_MAX, S_ // 4)
    rope64 = rope_tables(S_, HEAD_DIM_2)
    rope32 = rope_tables(S_, IDX_DIM)
    for l in range(DEPTH):
        g = norm_g[l]
        h = rmsnorm(x, g[0])
        x = x + 0.5 * rmsnorm(swiglu_2(h, ffn_wg[l, 0], ffn_wu[l, 0], ffn_wd[l, 0]), g[1])
        h = rmsnorm(x, g[2])
        if l % 2 == 0:
            e = l // 2
            lambda_init = 0.8 - 0.6 * math.exp(-0.3 * l)
            m = even_mixer(h, even_w_in[e], even_w_out[e], even_lambda[e], even_subln[e],
                           rope64, rope32, lambda_init, topk)
        else:
            o = l // 2
            m = odd_mixer(h, odd_w_in[o], odd_w_out[o], odd_rel_bias[o])
        x = x + rmsnorm(m.astype(x.dtype), g[3])
        h = rmsnorm(x, g[4])
        x = x + 0.5 * rmsnorm(swiglu_2(h, ffn_wg[l, 1], ffn_wu[l, 1], ffn_wd[l, 1]), g[5])
    return x


def setup_inputs(seed=0):
    out = dict(first_inputs(seed))
    for name, value in second_inputs(seed + 1).items():
        if name != "x":
            out[name + "_2"] = value
    return out


def reference(
    x, c, ada_w, ada_b, pre_mix_g, post_mix_g, pre_ffn_g, post_ffn_g, ffn_w_gu, ffn_w_down,
    a_w_in, a_b_in, a_ln_g, a_ln_b, a_w_s, a_b_s, a_w_out, kv_ada_w, kv_ada_b, kv_norm_g, kv_w,
    kv_b_f, k_norm_g, b_w_qg, b_q_norm_g, b_w_o, norm_g_2, ffn_wg_2, ffn_wu_2, ffn_wd_2,
    even_w_in_2, even_w_out_2, even_lambda_2, even_subln_2, odd_w_in_2, odd_w_out_2,
    odd_rel_bias_2,
):
    x = first_block(
        x, c, ada_w, ada_b, pre_mix_g, post_mix_g, pre_ffn_g, post_ffn_g, ffn_w_gu, ffn_w_down,
        a_w_in, a_b_in, a_ln_g, a_ln_b, a_w_s, a_b_s, a_w_out, kv_ada_w, kv_ada_b, kv_norm_g,
        kv_w, kv_b_f, k_norm_g, b_w_qg, b_q_norm_g, b_w_o,
    )
    return second_block(
        x, norm_g_2, ffn_wg_2, ffn_wu_2, ffn_wd_2, even_w_in_2, even_w_out_2, even_lambda_2,
        even_subln_2, odd_w_in_2, odd_w_out_2, odd_rel_bias_2,
    )


_drawn_inputs = setup_inputs


def setup_inputs(seed=0):
    import zlib

    import numpy as np

    out = dict(_drawn_inputs(seed))
    spreads = {}
    factors = {'a_b_in': 5.176,
     'a_ln_g': 4.747,
     'a_ln_b': 52.954,
     'kv_ada_b': 2.995,
     'k_norm_g': 4.038,
     'b_q_norm_g': 3.518,
     'even_subln_2': 60.931,
     'odd_rel_bias_2': 5.204,
     'norm_g_2': 2.816}
    for name, (base, spread) in spreads.items():
        noise = np.random.default_rng([zlib.crc32(name.encode()), seed]).standard_normal(out[name].shape)
        drawn = base * np.exp(spread * noise) if base else spread * noise
        out[name] = __import__('jax').numpy.asarray(drawn.astype(out[name].dtype))
    for name, factor in factors.items():
        out[name] = (out[name] * factor).astype(out[name].dtype)
    return out
```

```python
from contextlib import ExitStack

import numpy as np

import concourse.bass as bass
from concourse import mybir

F32 = mybir.dt.float32
F32R = mybir.dt.float32r
ALU = mybir.AluOpType
ACT = mybir.ActivationFunctionType
AX_X = mybir.AxisListType.X

D = 1024
T = 256
F = 2816
EPS = 1e-6
BIG = 3e38
GONE = -3.3e38
LAMBDA_INIT = 0.8 - 0.6
MAXC = 2048
NRAW, NW = 5, 3



def cols(c0, n=512):
    return [("w", c0, c0 + n)]


def projections():
    out = []

    def add(name, src, lead, kt, groups):
        out.append((name, kt, [[(src, lead, g)] if isinstance(g, list) else g for g in groups]))

    def split(c0, n):
        return [cols(c0 + 512 * i) for i in range(n)]

    def ffn(tag, gate, up, down, lead):
        (gs, g0), (us, u0) = gate, up
        groups = []
        for i in range(5):
            groups += [((gs, lead, cols(g0 + 512 * i)),), ((us, lead, cols(u0 + 512 * i)),)]
        groups.append(((gs, lead, cols(g0 + 2560, 256)), (us, lead, cols(u0 + 2560, 256))))
        add("gu" + tag, None, None, 8, groups)
        add("dn" + tag, down, lead, 22, split(0, 2))

    add("a_v", "a_w_in", (0,), 8, split(2048, 4))
    add("a_u", "a_w_in", (0,), 8, split(0, 4))
    add("a_out", "a_w_out", (0,), 16, split(0, 2))
    ffn("0", ("ffn_w_gu", 0), ("ffn_w_gu", F), "ffn_w_down", (0,))
    add("kv_f", "kv_w", (), 8, [[("w", 2048, 2064), ("zero", 48), ("w", 2048, 2064), ("zero", 48)]])
    add("kv_k", "kv_w", (), 8, split(0, 2))
    add("kv_v", "kv_w", (), 8, split(1024, 2))
    add("q", "b_w_qg", (0,), 8, split(0, 2))
    add("gate", "b_w_qg", (0,), 8, split(1024, 2))
    add("o", "b_w_o", (0,), 8, split(0, 2))
    ffn("1", ("ffn_w_gu", 0), ("ffn_w_gu", F), "ffn_w_down", (1,))
    ffn("2", ("ffn_wg_2", 0), ("ffn_wu_2", 0), "ffn_wd_2", (0, 0))
    add("idx", "even_w_in_2", (0,), 8,
        [[("w", 3072, 3328)] + [("w", 3328, 3360)] * 4 + [("w", 3360, 3368), ("zero", 120)]])
    add("bqkv", "even_w_in_2", (0,), 8, split(1536, 3))
    add("aqkv", "even_w_in_2", (0,), 8, split(0, 3))
    add("even_out", "even_w_out_2", (0,), 8, split(0, 2))
    ffn("3", ("ffn_wg_2", 0), ("ffn_wu_2", 0), "ffn_wd_2", (0, 1))
    ffn("4", ("ffn_wg_2", 0), ("ffn_wu_2", 0), "ffn_wd_2", (1, 0))
    add("odd", "odd_w_in_2", (0,), 8, split(0, 6))
    add("odd_out", "odd_w_out_2", (0,), 8, split(0, 2))
    ffn("5", ("ffn_wg_2", 0), ("ffn_wu_2", 0), "ffn_wd_2", (1, 1))
    return out


def width(parts):
    return sum(p[1] if p[0] == "zero" else p[2] - p[1] for _, _, g in parts for p in g)


def k_pieces(kt):
    n = -(-kt // 4)
    base, more = divmod(kt, n)
    out, at = [], 0
    for i in range(n):
        k = base + (i < more)
        out.append((at, k))
        at += k
    return out


def stream():
    main = []
    for name, kt, groups in projections():
        for gi, parts in enumerate(groups):
            parts = list(parts)
            for k0, k in k_pieces(kt) if width(parts) > 128 else [(0, kt)]:
                main.append(("mm", parts, k0, k, width(parts), (name, gi)))
    ada = []
    for c in range(24):
        ada.append(("ada", [("ada_w", (0,), cols(256 * c, 256))], 0, 8, 256, c))
    for c in range(12):
        ada.append(("ada", [("ada_w", (1,), cols(256 * c, 256))], 0, 8, 256, 24 + c))
        if c < 8:
            ada.append(("ada", [("kv_ada_w", (), cols(256 * c, 256))], 0, 8, 256, 48 + c))
    for c in range(12, 24):
        ada.append(("ada", [("ada_w", (1,), cols(256 * c, 256))], 0, 8, 256, 24 + c))
    items = ada[:8]
    ada = ada[8:]
    for i, m in enumerate(main):
        items.append(m)
        if i % 3 and ada:
            items.append(ada.pop(0))
    assert not ada
    out, off = [], 0
    for kind, parts, k0, k, n, tag in items:
        out.append((kind, off, parts, k0, k, n, tag))
        off += 128 * k * n
    return out, off



COLS = [("c", 8), ("ada_b", 96), ("kv_ada_b", 16), ("pre_mix_g", 16), ("post_mix_g", 16),
        ("pre_ffn_g", 16), ("post_ffn_g", 16), ("kv_norm_g", 8), ("a_b_u", 16), ("a_ln_g", 16),
        ("a_ln_b", 16), ("norm_g", 96), ("subln", 1), ("q_norm", 1), ("k_norm", 1), ("b_f", 1), ("lam", 4)]
COL, NCOL = {}, 0
for _n, _w in COLS:
    COL[_n] = NCOL
    NCOL += _w

CSTS = [("ident", 128), ("ones", 128), ("bd64", 128), ("rot64", 128), ("rot32", 128), ("cos64", 256),
        ("sin64", 256), ("cos32", 256), ("sin32", 256), ("causal", 256), ("chunk", 256), ("tri", 128)]
CST, NCST = {}, 0
for _n, _w in CSTS:
    CST[_n] = (NCST, _w)
    NCST += _w


def constants():
    p = np.arange(128)

    def rot(d):
        m = np.zeros((128, 128), np.float32)
        for i in range(128):
            low = i % d < d // 2
            m[i + d // 2 if low else i - d // 2, i] = -1.0 if low else 1.0
        return m

    def rope(d):
        inv = np.float32(10000.0) ** (-np.arange(0, d, 2, dtype=np.float32) / np.float32(d))
        ang = np.arange(T, dtype=np.float32)[None, :] * inv.astype(np.float32)[:, None]
        rows = p % (d // 2)
        return np.cos(ang).astype(np.float32)[rows], np.sin(ang).astype(np.float32)[rows]

    causal = np.where(p[None, :] <= p[:, None], 0.0, -BIG)
    chunk = np.where(p[None, :] // 64 <= p[:, None] // 64, 0.0, -BIG)
    z = np.zeros((128, 128))
    made = {"ident": np.eye(128), "ones": np.ones((128, 128)),
            "bd64": (p[:, None] // 64 == p[None, :] // 64), "rot64": rot(64), "rot32": rot(32),
            "cos64": rope(64)[0], "sin64": rope(64)[1], "cos32": rope(32)[0], "sin32": rope(32)[1],
            "causal": np.concatenate([z, causal], 1), "chunk": np.concatenate([z, chunk], 1),
            "tri": (p[None, :] >= p[:, None])}
    return np.concatenate([np.asarray(made[n], np.float32) for n, _ in CSTS], axis=1)



class Engine:
    def __init__(self, name, sem):
        self.name, self.sem = name, sem
        self.n = 0
        self.queue = []
        self.waited = {}

    def wait(self, tokens):
        need = {}
        stack = [tokens]
        while stack:
            t = stack.pop()
            if t is None:
                continue
            if isinstance(t, list):
                stack.extend(t)
                continue
            s, v = t
            if v > need.get(s, 0):
                need[s] = v
        for s, v in need.items():
            if v > self.waited.get(s, 0):
                self.waited[s] = v
                self.queue.append(("wait", s, v))

    def op(self, fn, after=(), sig=True):
        self.wait(list(after))
        if not sig:
            self.queue.append(("op", fn, None, 0))
            return None
        self.n += 1
        self.queue.append(("op", fn, self.sem, 1))
        return (self.sem, self.n)

    def dma(self, fn, slot, after=()):
        self.wait(list(after))
        slot.count += 16
        self.queue.append(("op", fn, slot.sem, 16))
        return (slot.sem, slot.count)

    def play(self, eng):
        for x in self.queue:
            if x[0] == "wait":
                eng.wait_ge(x[1], x[2])
            else:
                ins = x[1](eng)
                if x[2] is not None:
                    ins.then_inc(x[2], x[3])


class Slot:

    def __init__(self, ap, sem=None):
        self.ap, self.sem, self.count, self.free = ap, sem, 0, []


class Ring:
    def __init__(self, slots):
        self.slots, self.i = slots, 0

    def take(self):
        s = self.slots[self.i % len(self.slots)]
        self.i += 1
        return s


def build(nc, w_d, col_d, cst_d, x_d, row_d, bs_d, ws_d, rel_d, out_d):
    ctx = ExitStack()
    with ctx:
        def sem(name):
            return ctx.enter_context(nc.semaphore(name))

        base = nc.sbuf_base
        total = (nc.sbuf_usable_end - base) // 32 * 32 - 32
        ctx.enter_context(nc.sbuf_tensor("arena", [128, total // 4], F32))
        base = (base + 31) // 32 * 32
        at = [0]

        def place(name, shape, dt, off):
            return nc.alloc_sbuf_tensor_at(name, shape, dt, offset=base + off)

        def area(nbytes):
            off = at[0]
            at[0] += (nbytes + 31) // 32 * 32
            assert at[0] <= total, (at[0], total)
            return off

        def sb(name, shape, dt=F32):
            n = 4
            for s in shape[1:]:
                n *= s
            return place(name, shape, dt, area(n))

        raw = [Slot(sb(f"raw{i}", [128, MAXC]), sem(f"s_raw{i}")) for i in range(NRAW)]
        whr = [Slot(sb(f"wh{i}", [128, MAXC], F32R)) for i in range(NW)]
        wlr = [Slot(sb(f"wl{i}", [128, MAXC], F32R)) for i in range(NW)]
        x = sb("x", [128, 8, T])
        hh = Slot(sb("hh", [128, 8, T], F32R))
        hl = Slot(sb("hl", [128, 8, T], F32R))
        ta = Ring([Slot(sb(f"ta{i}", [128, 4, T])) for i in range(2)])
        tb = Ring([Slot(sb(f"tb{i}", [128, 4, T])) for i in range(2)])
        big = area(2 * 22 * T * 4)
        hidh = Slot(place("hidh", [128, 22, T], F32R, big))
        hidl = Slot(place("hidl", [128, 22, T], F32R, big + 22 * T * 4))
        side = area(16384)
        cst = sb("cst", [128, NCST])
        col = sb("col", [128, NCOL])
        mod = sb("mod", [128, 112])
        cact = sb("cact", [128, 8])
        der = sb("der", [128, 10, 8])
        eps = sb("eps", [128, 1])
        red = Ring([Slot(sb(f"red{i}", [128, T])) for i in range(2)])
        rsq = sb("rsq", [128, T])
        rs = Slot(sb("rs", [128, T]))
        small = sb("small", [128, 64])

        def C(name):
            o, w = CST[name]
            return cst[:, o:o + w]

        def colat(name, i=0):
            return col[:, COL[name] + i:COL[name] + i + 1]

        ident, ones = C("ident"), C("ones")

        pst = [ctx.enter_context(nc.psum_tensor(f"pp{i}", [128, 2, 512], F32)) for i in range(4)]
        banks = [Slot(pst[i // 2][:, i % 2, :]) for i in range(8)]

        class Pair:
            def __init__(self, i):
                self.t = pst[i]
                self.b = (banks[2 * i], banks[2 * i + 1])
                self.tiles = self.t[:, :, :].rearrange("p b (m t) -> p (b m) t", t=T)
                self.rows = self.t[:, :, :]

            def free(self):
                return [self.b[0].free, self.b[1].free]

            def release(self, tok):
                self.b[0].free = [tok]
                self.b[1].free = [tok]

        pairs = Ring([Pair(0), Pair(1), Pair(2)])
        misc = Ring([banks[6], banks[7]])

        sp = Engine("sp", sem("s_sp"))
        act = Engine("act", sem("s_act"))
        dve = Engine("dve", sem("s_dve"))
        pe = Engine("pe", sem("s_pe"))
        pool = Engine("pool", sem("s_pool"))

        load_slot = {}

        def load(name, dst, src, after=()):
            s = Slot(None, sem("s_ld_" + name))
            load_slot[name] = pool.dma(lambda e: e.dma_start(dst, src), s, after)
            return load_slot[name]

        t_col = load("col", col[:, :], col_d)
        t_cst = load("cst", cst[:, :], cst_d)
        t_x = load("x", x[:, :, :], x_d.rearrange("(k p) t -> p k t", p=128))
        v = place("v", [128, 2, 2048], F32, big)
        wsT = place("wsT", [128, 16, 128], F32, big + 16384)
        bsb = place("bsb", [128, 16, 128], F32, big + 24576)
        binr = place("binr", [128, 2048], F32, big + 32768)
        t_ws = load("ws", wsT[:, :, :], ws_d.rearrange("s (g t) -> s g t", g=16))
        t_bin = load("bin", binr[:, :], row_d.partition_broadcast(128))
        t_bs = load("bs", bsb[:, :, :].rearrange("p g t -> p (g t)"), bs_d.partition_broadcast(128))
        t_eps = pool.op(lambda e: e.memset(eps[:, :], EPS))

        items, _ = stream()
        state = {"dma": 0, "prep": 0, "use": 0}
        landed, ready, freed = {}, {}, set()

        def start_loads(upto):
            while state["dma"] < min(upto, len(items)):
                i = state["dma"]
                if i >= NRAW and i - NRAW not in freed:
                    return
                kind, off, parts, k0, kt, n, tag = items[i]
                s = raw[i % NRAW]
                src = w_d[off:off + 128 * kt * n].rearrange("(p f) -> p f", p=128)
                landed[i] = sp.dma(lambda e, d=s.ap[:, 0:kt * n], src=src: e.dma_start(d, src), s, s.free)
                state["dma"] += 1

        mm_index = {}
        count = 0
        for i, it in enumerate(items):
            if it[0] == "mm":
                mm_index[i] = count
                count += 1

        def prepare(upto):
            while state["prep"] < min(upto, len(items)):
                i = state["prep"]
                kind, off, parts, k0, kt, n, tag = items[i]
                if kind == "mm":
                    s = raw[i % NRAW]
                    j = mm_index[i]
                    h, l = whr[j % NW], wlr[j % NW]
                    w = kt * n
                    th = act.op(lambda e, o=h.ap[:, 0:w], a=s.ap[:, 0:w]: e.activation(o, a, ACT.Copy),
                                [landed[i], h.free])
                    tl = dve.op(lambda e, o=l.ap[:, 0:w], a=s.ap[:, 0:w], b=h.ap[:, 0:w]:
                                e.tensor_tensor(o, a, b, ALU.subtract), [landed[i], th, l.free])
                    s.free = [th, tl]
                    ready[i] = (th, tl)
                    freed.add(i)
                    start_loads(i + NRAW + 1)
                state["prep"] += 1

        start_loads(NRAW)

        def mm(out, lhsT, rhs, start, stop, after=(), sig=False, **kw):
            return pe.op(lambda e: e.matmul(out, lhsT, rhs, start=start, stop=stop, skip_group_check=True, **kw),
                         after, sig)

        def transpose(out, in_, idn, after=(), sig=False):
            return pe.op(lambda e: e.transpose(out, in_, idn), after, sig)

        def activation(out, in_, func, after=(), **kw):
            return act.op(lambda e: e.activation(out, in_, func, **kw), after)

        def tt(out, a, b, op, after=()):
            return dve.op(lambda e: e.tensor_tensor(out, a, b, op), after)

        def stt(out, a, s, b, op0, op1, after=()):
            return dve.op(lambda e: e.scalar_tensor_tensor(out=out, in0=a, scalar=s, in1=b, op0=op0, op1=op1), after)

        def ts(out, a, s1, s2, op0, op1=None, after=()):
            if op1 is None:
                return dve.op(lambda e: e.tensor_scalar(out, a, s1, s2, op0), after)
            return dve.op(lambda e: e.tensor_scalar(out, a, s1, s2, op0, op1), after)

        t_cact = activation(cact[:, :], col[:, 0:8], ACT.Silu, [t_col])
        mod_tok = {}

        def ada_piece(i):
            kind, off, parts, k0, kt, n, c = items[i]
            s = raw[i % NRAW]
            w = s.ap[:, 0:2048].rearrange("p (k n) -> p k n", k=8)
            b = misc.take()
            for m in range(2):
                for k in range(8):
                    t = mm(b.ap[:, m:m + 1], w[:, k, m * 128:(m + 1) * 128], cact[:, k:k + 1], k == 0, k == 7,
                           [landed[i], t_cact, b.free] if m == 0 and k == 0 else (), sig=(m == 1 and k == 7))
            s.free = [t]
            freed.add(i)
            start_loads(i + NRAW + 1)
            bias = col[:, COL["ada_b"] + 2 * c:COL["ada_b"] + 2 * c + 2]
            b.free = [tt(mod[:, 2 * c:2 * c + 2], b.ap[:, 0:2], bias, ALU.add, [t])]
            mod_tok[c // 4] = b.free[0]

        def next_piece():
            while items[state["use"]][0] == "ada":
                i = state["use"]
                ada_piece(i)
                state["use"] += 1
                state["prep"] = max(state["prep"], state["use"])
            i = state["use"]
            j, seen = i, 0
            while j < len(items) and seen < 3:
                seen += items[j][0] == "mm"
                j += 1
            prepare(j)
            state["use"] += 1
            return i

        def group(name, gi, xh, xl, xtok, mode, pair=None):
            pair = pair or pairs.take()
            done = 0
            ktot = None
            while True:
                i = next_piece()
                kind, off, parts, k0, kt, n, tag = items[i]
                assert tag == (name, gi), (tag, name, gi)
                j = mm_index[i]
                last = i + 1 >= len(items) or all(
                    items[q][6] != tag or items[q][0] != "mm" for q in range(i + 1, min(i + 4, len(items))))
                wh = whr[j % NW].ap[:, 0:kt * n].rearrange("p (k n) -> p k n", k=kt)
                wl = wlr[j % NW].ap[:, 0:kt * n].rearrange("p (k n) -> p k n", k=kt)
                th, tl = ready[i]
                nm = n // 128 if mode == "T" else 2
                first = k0 == 0
                for m in range(nm):
                    if mode == "T":
                        out = pair.tiles[:, m, :]
                        fresh = first and m % 2 == 0
                    else:
                        out = pair.rows[:, m, 0:n]
                        fresh = first
                    for k in range(kt):
                        for q, xx in enumerate((xh, xl)):
                            a = [th, xtok[k0 + k][q]]
                            if first and k == 0 and q == 0:
                                a.append(pair.free())
                            xa = xx[:, k0 + k, :]
                            if mode == "T":
                                lh, rh = wh[:, k, m * 128:(m + 1) * 128], xa
                            else:
                                lh, rh = xa[:, m * 128:(m + 1) * 128], wh[:, k, :]
                            t = mm(out, lh, rh, fresh and k == 0 and q == 0, False, a,
                                   sig=(m == nm - 1 and k == kt - 1 and q == 1))
                whr[j % NW].free = [t, tl]
                for m in range(nm):
                    out = pair.tiles[:, m, :] if mode == "T" else pair.rows[:, m, 0:n]
                    for k in range(kt):
                        xa = xh[:, k0 + k, :]
                        if mode == "T":
                            lh, rh = wl[:, k, m * 128:(m + 1) * 128], xa
                        else:
                            lh, rh = xa[:, m * 128:(m + 1) * 128], wl[:, k, :]
                        t = mm(out, lh, rh, False, last and k == kt - 1, [tl],
                               sig=(m == nm - 1 and k == kt - 1))
                wlr[j % NW].free = [t]
                if last:
                    return pair, t

        def split(dsth, dstl, src, after, waitfree=()):
            th = activation(dsth, src, ACT.Copy, [after, waitfree])
            tl = tt(dstl, src, dsth, ALU.subtract, [th, after])
            return th, tl

        def stats(parts, n_feat):
            b = misc.take()
            for i, (src, toks) in enumerate(parts):
                a, r = ta.take(), red.take()
                t = activation(a.ap[:, :, :], src, ACT.Square, [toks, a.free])
                t = dve.op(lambda e, o=r.ap[:, :], s=a.ap[:, :, :].rearrange("p k t -> p t k"):
                           e.tensor_reduce(o, s, AX_X, ALU.add), [t, r.free])
                a.free = [t]
                tm = mm(b.ap[:, 0:T], ones, r.ap[:, :], i == 0, i == len(parts) - 1,
                        [t, t_cst, b.free if i == 0 else None], sig=True)
                r.free = [tm]
            t = activation(rsq[:, :], b.ap[:, 0:T], ACT.Sqrt, [tm, t_eps, state.get("rsq")],
                           bias=eps[:, 0:1], scale=1.0 / n_feat)
            b.free = [t]
            t = dve.op(lambda e: e.reciprocal(rs.ap[:, :], rsq[:, :]), [t, rs.free])
            state["rsq"] = t
            return t

        def bc4(ap, n=4):
            return ap.unsqueeze(1).to_broadcast([128, n, ap.shape[-1]])

        x_tok = [t_x, t_x]

        def make_h(acols, bcols, t_rs, after):
            toks = []
            last = None
            for m in range(8):
                if m % 4 == 0:
                    s = tb.take()
                o = s.ap[:, m % 4, :]
                t = stt(o, x[:, m, :], acols[:, m:m + 1], rs.ap[:, :], ALU.mult, ALU.mult,
                        [x_tok[m // 4], t_rs, after, s.free if m % 4 == 0 else None])
                if bcols is None:
                    th = activation(hh.ap[:, m, :], o, ACT.Copy, [t, hh.free])
                    tl = tt(hl.ap[:, m, :], o, hh.ap[:, m, :], ALU.subtract, [th, hl.free])
                else:
                    th = activation(hh.ap[:, m, :], o, ACT.Identity, [t, hh.free, after], bias=bcols[:, m:m + 1])
                    tl = stt(hl.ap[:, m, :], o, bcols[:, m:m + 1], hh.ap[:, m, :], ALU.add, ALU.subtract,
                             [th, hl.free])
                toks.append((th, tl))
                if m % 4 == 3:
                    s.free = [tl]
            rs.free = [tl]
            return toks

        def residual(outs, scols, after):
            t_rs = stats([(p.tiles[:, :, :], [t]) for p, t in outs], D)
            for half, (p, t0) in enumerate(outs):
                s = tb.take()
                for m in range(4):
                    t = stt(s.ap[:, m, :], p.tiles[:, m, :], scols[:, 4 * half + m:4 * half + m + 1], rs.ap[:, :],
                            ALU.mult, ALU.mult, [t0, t_rs, after, s.free if m == 0 else None])
                p.release(t)
                xa = x[:, 4 * half:4 * half + 4, :]
                t = tt(xa, xa, s.ap[:, :, :], ALU.add, [t, x_tok])
                s.free = [t]
                x_tok[half] = t
            rs.free = [t]

        def x_stats():
            return stats([(x[:, 4 * i:4 * i + 4, :], [x_tok[i]]) for i in range(2)], D)

        def both(name, xh, xl, xtok, mode="T"):
            return [group(name, g, xh, xl, xtok, mode) for g in range(2)]

        def modcols(sec):
            return mod[:, 8 * sec:8 * sec + 8]

        def pcols(name, i):
            return col[:, COL[name] + 8 * i:COL[name] + 8 * i + 8]

        ndr = [0]

        def scaled(gains, sec, add_one):
            o = der[:, ndr[0] % 10, :]
            ndr[0] += 1
            t = stt(o, modcols(sec), 1.0 if add_one else 0.0, gains, ALU.add, ALU.mult, [mod_tok[sec], t_col])
            return o, t

        def swiglu(tag, toks):
            name = "gu" + tag
            ht = []
            hidh.free, hidl.free = [hidh.free], [hidl.free]
            for i in range(6):
                nt = 4 if i < 5 else 2
                if i < 5:
                    pg, tg = group(name, 2 * i, hh.ap, hl.ap, toks, "T")
                    g_ps = pg.tiles[:, :, :]
                else:
                    pg, tg = group(name, 10, hh.ap, hl.ap, toks, "T")
                    g_ps = pg.tiles[:, 0:2, :]
                a = ta.take()
                t = activation(a.ap[:, 0:nt, :], g_ps, ACT.Silu, [tg, a.free])
                if i < 5:
                    pg.release(t)
                    pu, tu = group(name, 2 * i + 1, hh.ap, hl.ap, toks, "T")
                    u_ps = pu.tiles[:, :, :]
                else:
                    pu, tu = pg, tg
                    u_ps = pg.tiles[:, 2:4, :]
                s = tb.take()
                t = tt(s.ap[:, 0:nt, :], a.ap[:, 0:nt, :], u_ps, ALU.mult, [t, tu, s.free])
                pu.release(t)
                a.free = [t]
                th, tl = split(hidh.ap[:, 4 * i:4 * i + nt, :], hidl.ap[:, 4 * i:4 * i + nt, :],
                               s.ap[:, 0:nt, :], t, [hidh.free, hidl.free])
                s.free = [th, tl]
                ht += [(th, tl)] * nt
            hh.free = hl.free = [tu]
            outs = both("dn" + tag, hidh.ap, hidl.ap, ht)
            hidh.free = hidl.free = [outs[1][1]]
            return outs

        t_tri = tt(wsT[:, :, :], wsT[:, :, :], bc4(C("tri"), 16), ALU.mult, [t_ws, t_cst])
        while items[state["use"]][0] == "ada":
            ada_piece(state["use"])
            state["use"] += 1
            state["prep"] = max(state["prep"], state["use"])
        t_rs = x_stats()
        a0, ta0 = scaled(pcols("pre_mix_g", 0), 1, True)
        htok = make_h(a0, modcols(0), t_rs, [ta0, mod_tok[0]])

        bst = small[:, 0:48].rearrange("p (a g s) -> p a g s", a=2, g=4)
        mv = small[:, 48:52].rearrange("p (a s) -> p a s", a=2)
        rstd = small[:, 52:54]
        v_tok = []
        for g in range(4):
            p, t = group("a_v", g, hh.ap, hl.ap, htok, "N")
            s = tb.take()
            bias = binr[:, 512 * g:512 * g + 512]
            t = tt(s.ap[:, :, :].rearrange("p (a b) t -> p a (b t)", a=2), p.rows, bc4(bias, 2), ALU.add,
                   [t, t_bin, s.free])
            p.release(t)
            vg = v[:, :, 512 * g:512 * g + 512]
            t = activation(vg, s.ap[:, :, :].rearrange("p (a b) t -> p a (b t)", a=2), ACT.Gelu_apprx_tanh, [t])
            s.free = [t]
            for a in range(2):
                t = dve.op(lambda e, o=bst[:, a, g, :], i=v[:, a, 512 * g:512 * g + 512]: e.bn_stats(o, i), [t])
        for a in range(2):
            t = dve.op(lambda e, o=mv[:, a, :], i=bst[:, a, :, :].rearrange("p g s -> p (g s)"): e.bn_aggr(o, i), [t])
        t = activation(rstd, mv[:, :, 1], ACT.Sqrt, [t, t_eps], bias=eps[:, 0:1])
        t = dve.op(lambda e: e.reciprocal(rstd, rstd), [t])
        for a in range(2):
            t_v = ts(v[:, a, :], v[:, a, :], mv[:, a, 0:1], rstd[:, a:a + 1], ALU.subtract, ALU.mult, [t])

        wsf = wsT[:, :, :].rearrange("p g t -> p (g t)")
        for q in range(4):
            b = misc.take()
            t = mm(b.ap[:, :], ones, wsf[:, 512 * q:512 * q + 512], True, True, [t_tri, t_cst, b.free], sig=True)
            for g in range(4):
                gg = 4 * q + g
                t_q = stt(bsb[:, gg, :], b.ap[:, 128 * g:128 * g + 128], colat("a_ln_b", gg), bsb[:, gg, :],
                          ALU.mult, ALU.add, [t, t_bs, t_col])
            b.free = [t_q]

        spt = place("spt", [128, 16, T], F32, side)

        def gelu_u(g):
            p, tg = group("a_u", g, hh.ap, hl.ap, htok, "T")
            a = ta.take()
            for m in range(4):
                t = activation(a.ap[:, m, :], p.tiles[:, m, :], ACT.Gelu_apprx_tanh, [tg, a.free, t_col],
                               bias=colat("a_b_u", 4 * g + m))
            p.release(t)
            return a, t, tg

        u0 = gelu_u(0)
        sp_tok = []
        for q in range(4):
            p = pairs.take()
            for g in range(4):
                for n in range(2):
                    t = mm(p.tiles[:, g, 128 * n:128 * n + 128], v[:, n, 128 * (4 * q + g):128 * (4 * q + g) + 128],
                           wsT[:, 4 * q + g, :], g % 2 == 0 and n == 0, True,
                           [t_v, t_tri, p.free()], sig=(g == 3 and n == 1))
            for g in range(4):
                gg = 4 * q + g
                t2 = stt(spt[:, gg, :].rearrange("p (n t) -> p n t", n=2),
                         p.tiles[:, g, :].rearrange("p (n t) -> p n t", n=2), colat("a_ln_g", gg),
                         bc4(bsb[:, gg, :], 2), ALU.mult, ALU.add, [t, t_q])
            p.release(t2)
            sp_tok.append(t2)
            t_sp_pe = t
        hidh.free = [t_sp_pe, sp_tok[-1]]
        hidl.free = [t_sp_pe, sp_tok[-1]]
        ht = []
        for g in range(4):
            a, t, tg = u0 if g == 0 else gelu_u(g)
            s = tb.take()
            t = tt(s.ap[:, :, :], a.ap[:, :, :], spt[:, 4 * g:4 * g + 4, :], ALU.mult, [t, sp_tok[g], s.free])
            a.free = [t]
            th, tl = split(hidh.ap[:, 4 * g:4 * g + 4, :], hidl.ap[:, 4 * g:4 * g + 4, :], s.ap[:, :, :], t,
                           [hidh.free, hidl.free])
            s.free = [th, tl]
            ht += [(th, tl)] * 4
        t_side = t
        hh.free = hl.free = [tg]
        outs = both("a_out", hidh.ap, hidl.ap, ht)
        hidh.free = hidl.free = [outs[1][1]]

        def after_mix(layer):
            s1, t1 = scaled(pcols("post_mix_g", layer), 6 * layer + 2, False)
            residual(outs, s1, [t1])
            a1, t1 = scaled(pcols("pre_ffn_g", layer), 6 * layer + 4, True)
            return make_h(a1, modcols(6 * layer + 3), x_stats(), [t1, mod_tok[6 * layer + 3]])

        htok = after_mix(0)
        outs = swiglu("0", htok)
        s1, t1 = scaled(pcols("post_ffn_g", 0), 5, False)
        residual(outs, s1, [t1])

        t_rs = x_stats()
        a1, t1 = scaled(pcols("kv_norm_g", 0), 13, True)
        htok = make_h(a1, modcols(12), t_rs, [t1, mod_tok[12]])

        Sb = Ring([Slot(place(f"Sb{i}", [128, T], F32, side + 1024 * i)) for i in range(4)])
        Pb = Ring([Slot(place(f"Pb{i}", [128, T], F32, side + 4096 + 1024 * i)) for i in range(6)])
        PT = Ring([Slot(place(f"PT{i}", [128, T], F32, side + 10240 + 1024 * i)) for i in range(4)])
        st = place("st", [128, 64, 4], F32, side + 14336)
        dT = place("dT", [128, T], F32, big + 32768)
        nD = place("nD", [128, T], F32, big + 33792)
        side_free = [t_side, sp_tok]
        for ring in (Sb, Pb, PT):
            for s in ring.slots:
                s.free = [side_free]
        qT = place("qT", [128, 8, T], F32, big)
        kT = place("kT", [128, 8, T], F32, big + 8192)
        vv = place("vv", [128, 2, 1024], F32, big + 16384)
        gT = place("gT", [128, 8, T], F32, big + 24576)
        lf = [place(f"lf{i}", [128, T], F32, big + 34816 + 1024 * i) for i in range(3)]
        big_free = hidh.free

        p, t = group("kv_f", 0, hh.ap, hl.ap, htok, "T")
        t = ts(lf[0][:, :], p.tiles[:, 0, :], colat("b_f"), None, ALU.add, after=[t, big_free, t_col])
        p.release(t)
        t2 = activation(lf[1][:, :], lf[0][:, :], ACT.Abs, [t])
        t2 = activation(lf[1][:, :], lf[1][:, :], ACT.Exp, [t2], scale=-1.0)
        t2 = activation(lf[1][:, :], lf[1][:, :], ACT.Ln, [t2], bias=1.0)
        t = stt(lf[2][:, :], lf[0][:, :], 0.0, lf[1][:, :], ALU.min, ALU.subtract, [t, t2])
        t = dve.op(lambda e: e.tensor_tensor_scan(dT[:, :], ones[:, 0:1].to_broadcast([128, T]), lf[2][:, :], 0.0,
                                                  ALU.mult, ALU.add), [t])
        t_d = ts(nD[:, :], dT[:, :], -1.0, None, ALU.mult, after=[t])

        def head_norm(p, t0, gcol, dst, scale):
            a = ta.take()
            t = activation(a.ap[:, :, :], p.tiles, ACT.Square, [t0, a.free])
            q = pairs.take()
            for m in range(4):
                tm = mm(q.tiles[:, m, :], C("bd64"), a.ap[:, m, :], m % 2 == 0, True, [t, q.free()], sig=(m == 3))
            a.free = [tm]
            s = tb.take()
            t = activation(s.ap[:, :, :], q.tiles, ACT.Sqrt, [tm, s.free], bias=eps[:, 0:1], scale=1.0 / 64)
            q.release(t)
            t = dve.op(lambda e, o=s.ap[:, :, :]: e.reciprocal(o, o), [t])
            if scale != 1.0:
                t = ts(s.ap[:, :, :], s.ap[:, :, :], scale, None, ALU.mult, after=[t])
            t = stt(dst, p.tiles, gcol, s.ap[:, :, :], ALU.mult, ALU.mult, [t, t0, big_free, t_col])
            p.release(t)
            s.free = [t]
            return t

        qk_tok = []
        for g in range(2):
            p, t = group("kv_k", g, hh.ap, hl.ap, htok, "T")
            qk_tok.append(head_norm(p, t, colat("k_norm"), kT[:, 4 * g:4 * g + 4, :], 1.0))
        for g in range(2):
            p, t = group("kv_v", g, hh.ap, hl.ap, htok, "N")
            hh.free = hl.free = [t]
            t = activation(vv[:, :, 512 * g:512 * g + 512], p.rows, ACT.Copy, [t, big_free])
            p.release(t)
            t_vv = t
        a1, t1 = scaled(pcols("pre_mix_g", 1), 7, True)
        htok = make_h(a1, modcols(6), t_rs, [t1, mod_tok[6]])
        for g in range(2):
            p, t = group("q", g, hh.ap, hl.ap, htok, "T")
            qk_tok.append(head_norm(p, t, colat("q_norm"), qT[:, 4 * g:4 * g + 4, :], 0.125))
        for g in range(2):
            p, t = group("gate", g, hh.ap, hl.ap, htok, "T")
            hh.free = hl.free = [t]
            t = activation(gT[:, 4 * g:4 * g + 4, :], p.tiles, ACT.Sigmoid, [t, big_free])
            p.release(t)
            t_gate = t

        nst = [0]

        def attention(units, sbanks, tbanks, finish):
            S_r = Ring(sbanks)
            T_r = Ring(tbanks)
            O_r = Ring([banks[6], banks[7]])
            live = [dict(u) for u in units]
            o_bank = {}

            def scores(u):
                nk = u["nk"]
                u["s"] = []
                for terms in u["subs"]:
                    b = S_r.take()
                    for n, (c0, c1, l, r) in enumerate(terms):
                        t = mm(b.ap[:, c0:c1], l, r, n == 0, n == len(terms) - 1,
                               [u["after"], b.free] if n == 0 else (), sig=(n == len(terms) - 1))
                    sbuf = Sb.take()
                    k = nst[0] % 64
                    nst[0] += 1
                    if u["mask"] is None:
                        t = dve.op(lambda e, o=sbuf.ap[:, 0:nk], i=b.ap[:, 0:nk], m=st[:, k, 0:1]:
                                   e.tensor_scalar(o, i, -1.0, None, ALU.mult, ALU.min, accum_out=m),
                                   [t, sbuf.free])
                    else:
                        t = dve.op(lambda e, o=sbuf.ap[:, 0:nk], i=b.ap[:, 0:nk], m=st[:, k, 0:1], mk=u["mask"]:
                                   e.tensor_tensor_reduce(o, i, mk, -1.0, 3.4e38, ALU.add, ALU.min, m),
                                   [t, sbuf.free, t_cst, u["after"]])
                    b.free = [t]
                    u["s"].append((sbuf, k, t))

            def exps(u):
                nk = u["nk"]
                u["p"] = []
                for sbuf, k, t in u["s"]:
                    pb = Pb.take()
                    t = activation(pb.ap[:, 0:nk], sbuf.ap[:, 0:nk], ACT.Exp, [t, pb.free], scale=-1.0,
                                   bias=st[:, k, 0:1], accum_out=st[:, k, 1:2])
                    sbuf.free = [t]
                    u["p"].append((pb, k, t))

            def normalise(u):
                nk = u["nk"]
                rt = []
                for pb, k, t in u["p"]:
                    rt.append(dve.op(lambda e, o=st[:, k, 2:3], i=st[:, k, 1:2]: e.reciprocal(o, i), [t]))
                if len(rt) == 1:
                    pb, k, t = u["p"][0]
                    u["w"] = (pb, ts(pb.ap[:, 0:nk], pb.ap[:, 0:nk], st[:, k, 2:3], None, ALU.mult, after=[rt[0]]))
                else:
                    (p0, k0, _), (p1, k1, _) = u["p"]
                    t = ts(p1.ap[:, 0:nk], p1.ap[:, 0:nk], st[:, k1, 2:3], nlam, ALU.mult, ALU.mult,
                           after=[rt[1], t_lam])
                    t = stt(p0.ap[:, 0:nk], p0.ap[:, 0:nk], st[:, k0, 2:3], p1.ap[:, 0:nk], ALU.mult, ALU.add,
                            [t, rt[0]])
                    p1.free = [t]
                    u["w"] = (p0, t)

            def turn(u):
                nk = u["nk"]
                pb, t = u["w"]
                b = T_r.take()
                for kb in range(nk // 128):
                    tt_ = transpose(b.ap[:, 128 * kb:128 * kb + 128], pb.ap[:, 128 * kb:128 * kb + 128], ident,
                                    [t, b.free], sig=(kb == nk // 128 - 1))
                pb.free = [tt_]
                pt = PT.take()
                t = activation(pt.ap[:, 0:nk], b.ap[:, 0:nk], ACT.Copy, [tt_, pt.free])
                b.free = [t]
                u["pt"] = (pt, t)

            def values(u):
                pt, t = u["pt"]
                if u["tile"] not in o_bank:
                    o_bank[u["tile"]] = O_r.take()
                b = o_bank[u["tile"]]
                out = b.ap[u["rows"], 128 * u["qb"]:128 * u["qb"] + 128]
                n = u["nk"] // 128
                for kb in range(n):
                    tv = mm(out, u["v"](kb), pt.ap[:, 128 * kb:128 * kb + 128], kb == 0, kb == n - 1,
                            [t, u["vtok"], b.free], sig=(kb == n - 1))
                pt.free = [tv]
                if u["last"]:
                    finish(u["tile"], b, tv)

            for i in range(len(live) + 3):
                for stage, lag in ((scores, 0), (exps, 0), (normalise, 1), (turn, 2), (values, 3)):
                    if 0 <= i - lag < len(live):
                        stage(live[i - lag])

        def plain_units(qq, kk, vt, mask, after, extra=None, heads=16):
            us = []
            for h in range(heads):
                for qb in range(2):
                    nk = 128 * (qb + 1)
                    r = slice(64 * (h % 2), 64 * (h % 2) + 64)
                    terms = [(0, nk, qq[r, h // 2, 128 * qb:128 * qb + 128], kk[r, h // 2, 0:nk])]
                    if extra:
                        terms += extra(h, qb, nk)
                    us.append(dict(subs=[terms], nk=nk, mask=mask(qb), after=after, rows=r, tile=h // 2, qb=qb,
                                   v=(lambda kb, h=h: vt[:, kb, 64 * h:64 * h + 64]), vtok=after,
                                   last=(h % 2 == 1 and qb == 1)))
            return us

        def cmask(name):
            m = C(name)
            return lambda qb: m[:, 128:256] if qb == 0 else m

        ho = [None] * 8

        def forget_terms(h, qb, nk):
            r = slice(64 * (h % 2), 64 * (h % 2) + 64)
            c = 64 * (h % 2) + h
            one = ident[r, c:c + 1]
            return [(0, nk, dT[r, 128 * qb:128 * qb + 128], one.to_broadcast([64, nk])),
                    (0, nk, one.to_broadcast([64, 128]), nD[r, 0:nk])]

        def finish_fox(tile, b, t):
            s = tb.take()
            t = tt(s.ap[:, 0, :], b.ap[:, 0:T], gT[:, tile, :], ALU.mult, [t, t_gate, s.free])
            b.free = [t]
            th, tl = split(hh.ap[:, tile, :], hl.ap[:, tile, :], s.ap[:, 0, :], t, [hh.free, hl.free])
            s.free = [th, tl]
            ho[tile] = (th, tl)

        attention(plain_units(qT, kT, vv, cmask("causal"), [qk_tok, t_vv, t_d], forget_terms),
                  banks[0:3], banks[3:6], finish_fox)
        hidh.free = hidl.free = [ho[7][0], ho[7][1], (pe.sem, pe.n)]
        outs = both("o", hh.ap, hl.ap, list(ho))
        hh.free = hl.free = [outs[1][1]]
        htok = after_mix(1)
        outs = swiglu("1", htok)
        s1, t1 = scaled(pcols("post_ffn_g", 1), 11, False)
        residual(outs, s1, [t1])

        half_g = sb("half_g", [128, 4, 8])
        hg = {}
        for n, i in enumerate((1, 5, 7, 11)):
            hg[i] = (half_g[:, n, :], ts(half_g[:, n, :], pcols("norm_g", i), 0.5, None, ALU.mult, after=[t_col]))

        def ffn2(tag, pre, post):
            htok = make_h(pcols("norm_g", pre), None, x_stats(), [])
            outs = swiglu(tag, htok)
            residual(outs, hg[post][0], [hg[post][1]])

        def mix_h(i):
            return make_h(pcols("norm_g", i), None, x_stats(), [])

        prod = small[0:64, 56:58]
        el = small[:, 58:60]
        nlam = small[:, 60:61]
        lp = col[0:64, COL["lam"]:COL["lam"] + 4].rearrange("p (a b) -> p a b", b=2)
        t = tt(prod, lp[:, :, 0], lp[:, :, 1], ALU.mult, [t_col])
        b = misc.take()
        t = mm(b.ap[:, 0:2], ones[0:64, :], prod, True, True, [t, b.free], sig=True)
        t = activation(el, b.ap[:, 0:2], ACT.Exp, [t])
        b.free = [t]
        t_lam = stt(nlam, el[:, 1:2], LAMBDA_INIT, el[:, 0:1], ALU.subtract, ALU.subtract, [t])
        sub8 = small[:, 61:62]
        t_sub = ts(sub8, colat("subln"), 1.0 - LAMBDA_INIT, None, ALU.mult, after=[t_col])

        ffn2("2", 0, 1)
        htok = mix_h(2)

        aq = place("aq", [128, 4, T], F32, big)
        ak = place("ak", [128, 4, T], F32, big + 4096)
        av = place("av", [128, 2, 512], F32, big + 8192)
        bq = place("bq", [128, 4, T], F32, big + 12288)
        bk = place("bk", [128, 4, T], F32, big + 16384)
        bv = place("bv", [128, 2, 512], F32, big + 20480)
        ix = place("ix", [128, 3, T], F32, big + 24576)
        iw = place("iw", [128, 2, 8], F32, big + 27648)
        sc = place("sc", [128, 2, T], F32, big + 28672)
        sel = place("sel", [128, 2, T], F32, big + 30720)
        rl = Ring([Slot(place(f"rl{i}", [128, 512], F32, big + 32768 + 2048 * i)) for i in range(3)])
        oa = place("oa", [128, 4, T], F32, big + 38912)
        top8 = place("top8", [128, 2, 8], F32, big + 43008)
        big_free = hidh.free
        for s in rl.slots:
            s.free = [big_free]

        def rope(p, t0, nt, kind, dst, scale, keep=False):
            a = ta.take()
            t = activation(a.ap[:, :, :], p.tiles, ACT.Copy, [t0, a.free])
            p.release(t)
            q = pairs.take()
            for m in range(nt):
                tm = mm(q.tiles[:, m, :], C("rot" + kind), a.ap[:, m, :], m % 2 == 0, True, [t, q.free()],
                        sig=(m == nt - 1))
            s = tb.take()
            t1 = stt(dst, a.ap[:, 0:nt, :], scale, bc4(C("cos" + kind), nt), ALU.mult, ALU.mult, [t, big_free])
            t2 = stt(s.ap[:, 0:nt, :], q.tiles[:, 0:nt, :], scale, bc4(C("sin" + kind), nt), ALU.mult, ALU.mult,
                     [tm, s.free])
            q.release(t2)
            t3 = tt(dst, dst, s.ap[:, 0:nt, :], ALU.add, [t1, t2])
            s.free = [t3]
            a.free = [t1, tm]
            return (t3, a, t) if keep else t3

        p, t = group("idx", 0, hh.ap, hl.ap, htok, "T")
        t_ix, a, t_raw = rope(p, t, 3, "32", ix[:, :, :], 1.0, keep=True)
        b = misc.take()
        for n in range(2):
            t = transpose(b.ap[:, 128 * n:128 * n + 128], a.ap[:, 3, 128 * n:128 * n + 128], ident, [t_raw, b.free],
                          sig=(n == 1))
        a.free = [a.free, t]
        t_iw = ts(iw[:, :, :], b.ap[:, 0:256].rearrange("p (n c) -> p n c", n=2)[:, :, 0:8], 0.0625, None, ALU.mult,
                  after=[t, big_free])
        b.free = [t_iw]
        p, t = group("bqkv", 0, hh.ap, hl.ap, htok, "T")
        t_bq = rope(p, t, 4, "64", bq[:, :, :], 0.125)

        t_acc = None
        for qb in (1, 0):
            nk = 128 * (qb + 1)
            for jj in (0, 1):
                pp = [pairs.take(), pairs.take()]
                bk4 = [pp[0].b[0], pp[0].b[1], pp[1].b[0], pp[1].b[1]]
                for j in range(4):
                    h = 4 * jj + j
                    r = slice(32 * j, 32 * j + 32)
                    t = mm(bk4[j].ap[:, 0:nk], ix[r, jj, 128 * qb:128 * qb + 128], ix[r, 2, 0:nk], True, True,
                           [t_ix, bk4[j].free], sig=True)
                    s = rl.take()
                    t = activation(s.ap[:, 0:nk], bk4[j].ap[:, 0:nk], ACT.Relu, [t, s.free])
                    bk4[j].free = [t]
                    o = sc[:, qb, 0:nk]
                    if h == 0:
                        t = ts(o, s.ap[:, 0:nk], iw[:, qb, 0:1], None, ALU.mult, after=[t, t_iw])
                    else:
                        t = stt(o, s.ap[:, 0:nk], iw[:, qb, h:h + 1], o, ALU.mult, ALU.add, [t, t_acc])
                    s.free = [t]
                    t_acc = t
            o = sc[:, qb, 0:nk]
            t_acc = tt(o, o, cmask("chunk")(qb), ALU.add, [t_acc, t_cst])
        p, t = group("bqkv", 1, hh.ap, hl.ap, htok, "T")
        t_bk = rope(p, t, 4, "64", bk[:, :, :], 1.0)

        def top64(rounds):
            t = t_acc
            for _ in range(rounds):
                for qb in range(2):
                    nk = 128 * (qb + 1)
                    s8, o = top8[:, qb, :], sc[:, qb, 0:nk]
                    t = dve.op(lambda e, a=s8, b=o: e.max(a, b), [t])
                    t = dve.op(lambda e, a=s8, b=o: e.match_replace(b, a, b, GONE), [t])
            return t

        p, t = group("bqkv", 2, hh.ap, hl.ap, htok, "N")
        t_bv = activation(bv[:, :, :], p.rows, ACT.Copy, [t, big_free])
        p.release(t_bv)
        t_acc = top64(4)
        p, t = group("aqkv", 0, hh.ap, hl.ap, htok, "T")
        t_aq = rope(p, t, 4, "64", aq[:, :, :], 0.125)
        t_acc = top64(4)
        p, t = group("aqkv", 1, hh.ap, hl.ap, htok, "T")
        t_ak = rope(p, t, 4, "64", ak[:, :, :], 1.0)
        for qb in range(2):
            nk = 128 * (qb + 1)
            o = sel[:, qb, 0:nk]
            t = ts(o, sc[:, qb, 0:nk], -3.15e38, BIG, ALU.is_lt, ALU.mult, after=[t_acc])
            t_sel = ts(o, o, BIG, None, ALU.subtract, after=[t])
        p, t = group("aqkv", 2, hh.ap, hl.ap, htok, "N")
        hh.free = hl.free = [t]
        t_av = activation(av[:, :, :], p.rows, ACT.Copy, [t, big_free])
        p.release(t_av)

        us = []
        for h in range(4):
            for qb in range(2):
                nk = 128 * (qb + 1)
                subs = [[(0, nk, aq[r, h, 128 * qb:128 * qb + 128], ak[r, h, 0:nk])] for r in (slice(0, 64), slice(64, 128))]
                us.append(dict(subs=subs, nk=nk, mask=cmask("chunk")(qb), after=[t_aq, t_ak], rows=slice(0, 128),
                               tile=h, qb=qb, v=(lambda kb, h=h: av[:, kb, 128 * h:128 * h + 128]), vtok=[t_av],
                               last=(qb == 1)))
        oa_tok = []

        def finish_a(tile, b, t):
            t = dve.op(lambda e, o=oa[:, tile, :], i=b.ap[:, 0:T]: e.tensor_copy(o, i), [t, big_free])
            b.free = [t]
            oa_tok.append(t)

        attention(us, banks[0:4], banks[4:6], finish_a)

        ho = [None] * 8
        a = ta.take()
        t = activation(a.ap[:, :, :], oa[:, :, :], ACT.Square, [oa_tok, a.free])
        q = pairs.take()
        for m in range(4):
            tm = mm(q.tiles[:, m, :], ones, a.ap[:, m, :], m % 2 == 0, True, [t, q.free()], sig=(m == 3))
        a.free = [tm]
        s = tb.take()
        t = activation(s.ap[:, :, :], q.tiles, ACT.Sqrt, [tm, s.free], bias=eps[:, 0:1], scale=1.0 / 128)
        q.release(t)
        t = dve.op(lambda e, o=s.ap[:, :, :]: e.reciprocal(o, o), [t])
        t = stt(oa[:, :, :], oa[:, :, :], sub8, s.ap[:, :, :], ALU.mult, ALU.mult, [t, oa_tok, t_sub])
        s.free = [t]
        th, tl = split(hh.ap[:, 0:4, :], hl.ap[:, 0:4, :], oa[:, :, :], t, [hh.free, hl.free])
        ho[0:4] = [(th, tl)] * 4

        def finish_at(first):
            def f(tile, b, t):
                th, tl = split(hh.ap[:, first + tile, :], hl.ap[:, first + tile, :], b.ap[:, 0:T], t,
                               [hh.free, hl.free])
                b.free = [th, tl]
                ho[first + tile] = (th, tl)
            return f

        attention(plain_units(bq, bk, bv, lambda qb: sel[:, qb, 0:128 * (qb + 1)], [t_bq, t_bk, t_bv, t_sel],
                              heads=8), banks[0:3], banks[3:6], finish_at(4))
        hidh.free = hidl.free = [ho[3][0], ho[3][1], ho[7][0], ho[7][1], (pe.sem, pe.n)]
        outs = both("even_out", hh.ap, hl.ap, list(ho))
        hh.free = hl.free = [outs[1][1]]
        residual(outs, pcols("norm_g", 3), [])
        ffn2("3", 4, 5)
        ffn2("4", 6, 7)

        htok = mix_h(8)
        big_free = hidh.free
        oq = place("oq", [128, 8, T], F32, big)
        ok = place("ok", [128, 8, T], F32, big + 8192)
        ov = place("ov", [128, 2, 1024], F32, big + 16384)
        bT = place("bT", [128, 16, T], F32, big + 24576)
        t_rel = load("rel", bT[:, :, :], rel_d, [big_free])
        for g in range(2):
            p, t = group("odd", g, hh.ap, hl.ap, htok, "T")
            t_oq = activation(oq[:, 4 * g:4 * g + 4, :], p.tiles, ACT.Copy, [t, big_free], scale=0.125)
            p.release(t_oq)
        for g in range(2):
            p, t = group("odd", 2 + g, hh.ap, hl.ap, htok, "T")
            t_ok = dve.op(lambda e, o=ok[:, 4 * g:4 * g + 4, :], i=p.tiles: e.tensor_copy(o, i), [t, big_free])
            p.release(t_ok)
        for g in range(2):
            p, t = group("odd", 4 + g, hh.ap, hl.ap, htok, "N")
            hh.free = hl.free = [t]
            t_ov = activation(ov[:, :, 512 * g:512 * g + 512], p.rows, ACT.Copy, [t, big_free])
            p.release(t_ov)

        ho = [None] * 8

        def bias_terms(h, qb, nk):
            return [(128 * kb, 128 * kb + 128, bT[:, h, 128 * (qb - kb):128 * (qb - kb) + 128], ident)
                    for kb in range(qb + 1)]

        us = plain_units(oq, ok, ov, lambda qb: None, [t_oq, t_ok, t_ov, t_rel], bias_terms)
        attention(us, banks[0:3], banks[3:6], finish_at(0))
        hidh.free = hidl.free = [ho[7][0], ho[7][1], (pe.sem, pe.n)]
        outs = both("odd_out", hh.ap, hl.ap, list(ho))
        hh.free = hl.free = [outs[1][1]]
        residual(outs, pcols("norm_g", 9), [])
        ffn2("5", 10, 11)

        s_out = Slot(None, sem("s_out"))
        ov_d = out_d.rearrange("(k p) t -> p k t", p=128)
        for i in range(2):
            t = sp.dma(lambda e, i=i: e.dma_start(ov_d[:, 4 * i:4 * i + 4, :], x[:, 4 * i:4 * i + 4, :]), s_out,
                       [x_tok[i]])
        sp.wait([t])
        assert state["use"] == len(items)

        block = ctx.enter_context(nc.Block())

        @block.sync
        def _(e):
            sp.play(e)

        @block.gpsimd
        def _(e):
            pool.play(e)

        @block.scalar
        def _(e):
            act.play(e)

        @block.vector
        def _(e):
            dve.play(e)

        @block.tensor
        def _(e):
            pe.play(e)



def pack_stream(inputs):
    items, total = stream()
    out = np.empty((total,), np.float32)
    for kind, off, parts, k0, kt, n, tag in items:
        blocks = []
        for src, lead, g in parts:
            a = inputs[src]
            for i in lead:
                a = a[i]
            a = a[128 * k0:128 * (k0 + kt)]
            for p in g:
                if p[0] == "zero":
                    blocks.append(np.zeros((128 * kt, p[1]), np.float32))
                else:
                    blocks.append(a[:, p[1]:p[2]])
        w = blocks[0] if len(blocks) == 1 else np.concatenate(blocks, axis=1)
        out[off:off + 128 * kt * n] = w.reshape(kt, 128, n).transpose(1, 0, 2).reshape(-1)
    return out


def pack_columns(inputs):
    def c(a):
        return np.asarray(a).reshape(-1, 128).T

    f16 = inputs["kv_b_f"]
    z = np.zeros((48,), np.float32)
    lam = inputs["even_lambda_2"][0].T
    made = {
        "c": c(inputs["c"]), "ada_b": c(inputs["ada_b"]), "kv_ada_b": c(inputs["kv_ada_b"]),
        "pre_mix_g": c(inputs["pre_mix_g"]), "post_mix_g": c(inputs["post_mix_g"]),
        "pre_ffn_g": c(inputs["pre_ffn_g"]), "post_ffn_g": c(inputs["post_ffn_g"]),
        "kv_norm_g": c(inputs["kv_norm_g"]), "a_b_u": c(inputs["a_b_in"][0, :2048]),
        "a_ln_g": c(inputs["a_ln_g"]), "a_ln_b": c(inputs["a_ln_b"]), "norm_g": c(inputs["norm_g_2"]),
        "subln": c(inputs["even_subln_2"]), "q_norm": c(np.tile(inputs["b_q_norm_g"][0], 2)),
        "k_norm": c(np.tile(inputs["k_norm_g"], 2)), "b_f": c(np.concatenate([f16, z, f16, z])),
        "lam": np.concatenate([lam, np.zeros((64, 4), np.float32)], axis=0),
    }
    return np.ascontiguousarray(np.concatenate([made[n] for n, _ in COLS], axis=1))


def lay_out_bias(rel):
    k, q = np.arange(128)[:, None], np.arange(T)[None, :]
    out = rel[:, np.maximum(q - k + 63, 0)].transpose(1, 0, 2)
    return np.ascontiguousarray(np.where((k // 64 <= q // 64)[:, None, :], out, np.float32(-BIG)))


def kernel(**inputs):
    import concourse.bacc as _bacc
    from concourse.bass_utils import run_bass_kernel_spmd as _run

    inputs = {k: np.asarray(a) for k, a in inputs.items()}
    arrays = {
        "w": pack_stream(inputs), "cols": pack_columns(inputs), "csts": constants(),
        "xT": np.ascontiguousarray(inputs["x"][0].T),
        "bin": np.ascontiguousarray(inputs["a_b_in"][0, 2048:]),
        "bs": np.ascontiguousarray(inputs["a_b_s"][0].reshape(-1)),
        "ws": np.ascontiguousarray(inputs["a_w_s"][0].transpose(2, 0, 1).reshape(128, 2048)),
        "rel": lay_out_bias(inputs["odd_rel_bias_2"][0]),
    }
    nc = _bacc.Bacc("TRN2", target_bir_lowering=False, num_devices=1)
    aps = {n: nc.dram_tensor("in_" + n, a.shape, F32, kind="ExternalInput").ap() for n, a in arrays.items()}
    out = nc.dram_tensor("out_T", (D, T), F32, kind="ExternalOutput").ap()
    build(nc, aps["w"], aps["cols"], aps["csts"], aps["xT"], aps["bin"], aps["bs"], aps["ws"], aps["rel"], out)
    r = _run(nc, [{"in_" + n: a for n, a in arrays.items()}], core_ids=[0])
    return np.ascontiguousarray(r.results[0]["out_T"].T)[None]
```

```python
from contextlib import ExitStack

import numpy as np

import concourse.bass as bass
from concourse import mybir

F32 = mybir.dt.float32
F32R = mybir.dt.float32r
ALU = mybir.AluOpType
ACT = mybir.ActivationFunctionType
AX_X = mybir.AxisListType.X

D = 1024
T = 256
F = 2816
EPS = 1e-6
BIG = 3e38
GONE = -3.3e38
LAMBDA_INIT = 0.8 - 0.6
MAXC = 2048
NRAW, NW = 5, 3



def cols(c0, n=512):
    return [("w", c0, c0 + n)]


def projections():
    out = []

    def add(name, src, lead, kt, groups):
        out.append((name, kt, [[(src, lead, g)] if isinstance(g, list) else g for g in groups]))

    def split(c0, n):
        return [cols(c0 + 512 * i) for i in range(n)]

    def ffn(tag, gate, up, down, lead):
        (gs, g0), (us, u0) = gate, up
        groups = []
        for i in range(5):
            groups += [((gs, lead, cols(g0 + 512 * i)),), ((us, lead, cols(u0 + 512 * i)),)]
        groups.append(((gs, lead, cols(g0 + 2560, 256)), (us, lead, cols(u0 + 2560, 256))))
        add("gu" + tag, None, None, 8, groups)
        add("dn" + tag, down, lead, 22, split(0, 2))

    add("a_v", "a_w_in", (0,), 8, split(2048, 4))
    add("a_u", "a_w_in", (0,), 8, split(0, 4))
    add("a_out", "a_w_out", (0,), 16, split(0, 2))
    ffn("0", ("ffn_w_gu", 0), ("ffn_w_gu", F), "ffn_w_down", (0,))
    add("kv_f", "kv_w", (), 8, [[("w", 2048, 2064)] * 8])
    add("kv_k", "kv_w", (), 8, split(0, 2))
    add("kv_v", "kv_w", (), 8, split(1024, 2))
    add("q", "b_w_qg", (0,), 8, split(0, 2))
    add("gate", "b_w_qg", (0,), 8, split(1024, 2))
    add("o", "b_w_o", (0,), 8, split(0, 2))
    ffn("1", ("ffn_w_gu", 0), ("ffn_w_gu", F), "ffn_w_down", (1,))
    ffn("2", ("ffn_wg_2", 0), ("ffn_wu_2", 0), "ffn_wd_2", (0, 0))
    add("idx", "even_w_in_2", (0,), 8,
        [[("w", 3072, 3328)] + [("w", 3328, 3360)] * 4 + [("w", 3360, 3368), ("zero", 120)]])
    add("bqkv", "even_w_in_2", (0,), 8, split(1536, 3))
    add("aqkv", "even_w_in_2", (0,), 8, split(0, 3))
    add("even_out", "even_w_out_2", (0,), 8, split(0, 2))
    ffn("3", ("ffn_wg_2", 0), ("ffn_wu_2", 0), "ffn_wd_2", (0, 1))
    ffn("4", ("ffn_wg_2", 0), ("ffn_wu_2", 0), "ffn_wd_2", (1, 0))
    add("odd", "odd_w_in_2", (0,), 8, split(0, 6))
    add("odd_out", "odd_w_out_2", (0,), 8, split(0, 2))
    ffn("5", ("ffn_wg_2", 0), ("ffn_wu_2", 0), "ffn_wd_2", (1, 1))
    return out


def width(parts):
    return sum(p[1] if p[0] == "zero" else p[2] - p[1] for _, _, g in parts for p in g)


def k_pieces(kt):
    n = -(-kt // 4)
    base, more = divmod(kt, n)
    out, at = [], 0
    for i in range(n):
        k = base + (i < more)
        out.append((at, k))
        at += k
    return out


def stream():
    main = []
    for name, kt, groups in projections():
        for gi, parts in enumerate(groups):
            parts = list(parts)
            for k0, k in k_pieces(kt) if width(parts) > 128 else [(0, kt)]:
                main.append(("mm", parts, k0, k, width(parts), (name, gi)))
    def piece(src, lead, c, at):
        return ("ada", [(src, lead, cols(256 * c, 256))], 0, 8, 256, at + c)

    ada = [piece("ada_w", (0,), c, 0) for c in range(24)]
    ada += [piece("kv_ada_w", (), c, 48) for c in range(8)]
    ada += [piece("ada_w", (1,), c, 24) for c in range(24)]
    items = [ada[4], ada[0], ada[5], ada[1], main[0], ada[6], ada[2], ada[7], ada[3], main[1]]
    ada, main = ada[8:], main[2:]
    marks = [(0, 0), (22, 12), (56, 26), (62, 32), (72, 44), (100, 48)]
    given = 0
    for i, m in enumerate(main):
        items.append(m)
        for (a0, b0), (a1, b1) in zip(marks, marks[1:]):
            if a0 <= i < a1 and given < b0 + -(-(i + 1 - a0) * (b1 - b0) // (a1 - a0)):
                items.append(ada.pop(0))
                given += 1
    assert not ada
    out, off = [], 0
    for kind, parts, k0, k, n, tag in items:
        out.append((kind, off, parts, k0, k, n, tag))
        off += 128 * k * n
    return out, off



COLS = [("ada_b", 96), ("kv_ada_b", 16), ("pre_mix_g", 16), ("post_mix_g", 16),
        ("pre_ffn_g", 16), ("post_ffn_g", 16), ("kv_norm_g", 8), ("a_b_u", 16), ("a_ln_g", 16),
        ("a_ln_b", 16), ("norm_g", 96), ("subln", 1), ("q_norm", 1), ("k_norm", 1), ("b_f", 1), ("lam", 4)]
COL, NCOL = {}, 0
for _n, _w in COLS:
    COL[_n] = NCOL
    NCOL += _w

CSTS = [("ident", 128), ("bd64", 128), ("rot64", 128), ("rot32", 128), ("cos64", 256),
        ("sin64", 256), ("cos32", 256), ("sin32", 256), ("causal", 256), ("chunk", 256), ("tri", 128), ("forget", 10)]
CST, NCST = {}, 0
for _n, _w in CSTS:
    CST[_n] = (NCST, _w)
    NCST += _w


def constants():
    p = np.arange(128)

    def rot(d):
        m = np.zeros((128, 128), np.float32)
        for i in range(128):
            low = i % d < d // 2
            m[i + d // 2 if low else i - d // 2, i] = -1.0 if low else 1.0
        return m

    def rope(d):
        inv = np.float32(10000.0) ** (-np.arange(0, d, 2, dtype=np.float32) / np.float32(d))
        ang = np.arange(T, dtype=np.float32)[None, :] * inv.astype(np.float32)[:, None]
        rows = p % (d // 2)
        return np.cos(ang).astype(np.float32)[rows], np.sin(ang).astype(np.float32)[rows]

    causal = np.where(p[None, :] <= p[:, None], 0.0, -BIG)
    chunk = np.where(p[None, :] // 64 <= p[:, None] // 64, 0.0, -BIG)
    z = np.zeros((128, 128))
    forget = np.zeros((128, 10))
    forget[:, 0] = p % 32 < 16
    forget[:, 1] = p % 32 >= 16
    for j in range(4):
        for g in range(4):
            forget[32 * g + 16 + 4 * j + g, 2 + j] = -1.0
            forget[32 * g + 4 * j + g, 6 + j] = 1.0
    made = {"ident": np.eye(128),
            "bd64": (p[:, None] // 64 == p[None, :] // 64), "rot64": rot(64), "rot32": rot(32),
            "cos64": rope(64)[0], "sin64": rope(64)[1], "cos32": rope(32)[0], "sin32": rope(32)[1],
            "causal": np.concatenate([z, causal], 1), "chunk": np.concatenate([z, chunk], 1),
            "tri": (p[None, :] >= p[:, None]), "forget": forget}
    return np.concatenate([np.asarray(made[n], np.float32) for n, _ in CSTS], axis=1)



class Engine:
    def __init__(self, name, sem):
        self.name, self.sem = name, sem
        self.n = 0
        self.queue = []
        self.waited = {}

    def wait(self, tokens):
        need = {}
        stack = [tokens]
        while stack:
            t = stack.pop()
            if t is None:
                continue
            if isinstance(t, list):
                stack.extend(t)
                continue
            s, v = t
            if v > need.get(s, 0):
                need[s] = v
        for s, v in need.items():
            if v > self.waited.get(s, 0):
                self.waited[s] = v
                self.queue.append(("wait", s, v))

    def op(self, fn, after=(), sig=True):
        self.wait(list(after))
        if not sig:
            self.queue.append(("op", fn, None, 0))
            return None
        self.n += 1
        self.queue.append(("op", fn, self.sem, 1))
        return (self.sem, self.n)

    def dma(self, fn, slot, after=()):
        self.wait(list(after))
        slot.count += 16
        self.queue.append(("op", fn, slot.sem, 16))
        return (slot.sem, slot.count)

    def play(self, eng):
        for x in self.queue:
            if x[0] == "wait":
                eng.wait_ge(x[1], x[2])
            else:
                ins = x[1](eng)
                if x[2] is not None:
                    ins.then_inc(x[2], x[3])


class Slot:

    def __init__(self, ap, sem=None):
        self.ap, self.sem, self.count, self.free = ap, sem, 0, []


class Ring:
    def __init__(self, slots):
        self.slots, self.i = slots, 0

    def take(self):
        s = self.slots[self.i % len(self.slots)]
        self.i += 1
        return s


def build(nc, c_d, w_d, col_d, cst_d, x_d, row_d, bs_d, ws_d, rel_d, out_d):
    ctx = ExitStack()
    with ctx:
        def sem(name):
            return ctx.enter_context(nc.semaphore(name))

        base = nc.sbuf_base
        total = (nc.sbuf_usable_end - base) // 32 * 32 - 32
        ctx.enter_context(nc.sbuf_tensor("arena", [128, total // 4], F32))
        base = (base + 31) // 32 * 32
        at = [0]

        def place(name, shape, dt, off):
            return nc.alloc_sbuf_tensor_at(name, shape, dt, offset=base + off)

        def area(nbytes):
            off = at[0]
            at[0] += (nbytes + 31) // 32 * 32
            assert at[0] <= total, (at[0], total)
            return off

        def sb(name, shape, dt=F32):
            n = 4
            for s in shape[1:]:
                n *= s
            return place(name, shape, dt, area(n))

        raw = [Slot(sb(f"raw{i}", [128, MAXC]), sem(f"s_raw{i}")) for i in range(NRAW)]
        whr = [Slot(sb(f"wh{i}", [128, MAXC], F32R)) for i in range(NW)]
        wlr = [Slot(sb(f"wl{i}", [128, MAXC], F32R)) for i in range(NW)]
        x = sb("x", [128, 8, T])
        hh = Slot(sb("hh", [128, 8, T], F32R))
        hl = Slot(sb("hl", [128, 8, T], F32R))
        ta = Ring([Slot(sb(f"ta{i}", [128, 4, T])) for i in range(2)])
        tb = Ring([Slot(sb(f"tb{i}", [128, 4, T])) for i in range(2)])
        big = area(2 * 22 * T * 4)
        hidh = Slot(place("hidh", [128, 22, T], F32R, big))
        hidl = Slot(place("hidl", [128, 22, T], F32R, big + 22 * T * 4))
        side = area(16384)
        cst = sb("cst", [128, NCST])
        col = sb("col", [128, NCOL])
        mod = sb("mod", [128, 112])
        cact = sb("cact", [128, D])
        ones = sb("ones", [128, 128])[:, :]
        der = sb("der", [128, 10, 8])
        eps = sb("eps", [128, 1])
        lnv = sb("lnv", [128, T])
        rsx = Slot(sb("rsx", [128, T]))
        rsy = Slot(sb("rsy", [128, T]))
        e2 = Slot(sb("e2", [1, T]))
        eps2 = sb("eps2", [1, 1])
        warm = sb("warm", [1, 1])
        small = sb("small", [128, 64])

        def C(name):
            o, w = CST[name]
            return cst[:, o:o + w]

        def colat(name, i=0):
            return col[:, COL[name] + i:COL[name] + i + 1]

        ident = C("ident")

        pst = [ctx.enter_context(nc.psum_tensor(f"pp{i}", [128, 2, 512], F32)) for i in range(4)]
        banks = [Slot(pst[i // 2][:, i % 2, :]) for i in range(8)]

        class Pair:
            def __init__(self, i):
                self.t = pst[i]
                self.b = (banks[2 * i], banks[2 * i + 1])
                self.tiles = self.t[:, :, :].rearrange("p b (m t) -> p (b m) t", t=T)
                self.rows = self.t[:, :, :]

            def free(self):
                return [self.b[0].free, self.b[1].free]

            def release(self, tok):
                self.b[0].free = [tok]
                self.b[1].free = [tok]

        pairs = Ring([Pair(0), Pair(1), Pair(2)])
        misc = Ring([banks[6], banks[7]])

        sp = Engine("sp", sem("s_sp"))
        act = Engine("act", sem("s_act"))
        dve = Engine("dve", sem("s_dve"))
        pe = Engine("pe", sem("s_pe"))
        pool = Engine("pool", sem("s_pool"))

        load_slot = {}

        def load(name, dst, src, after=(), queue=None):
            s = Slot(None, sem("s_ld_" + name))
            load_slot[name] = (queue or pool).dma(lambda e: e.dma_start(dst, src), s, after)
            return load_slot[name]

        t_ones = pool.op(lambda e: e.memset(ones, 1.0))
        v = place("v", [128, 2, 2048], F32, big)
        wsT = place("wsT", [128, 16, 128], F32, big + 16384)
        bsb = place("bsb", [128, 16, 128], F32, big + 24576)
        binr = place("binr", [128, 2048], F32, big + 32768)
        pool.op(lambda e: e.memset(eps2[:, :], D * EPS * EPS))
        t_eps = pool.op(lambda e: e.memset(eps[:, :], EPS))

        items, _ = stream()
        state = {"dma": 0, "prep": 0, "use": 0}
        landed, ready, freed = {}, {}, set()

        def start_loads(upto):
            while state["dma"] < min(upto, len(items)):
                i = state["dma"]
                if i >= NRAW and i - NRAW not in freed:
                    return
                kind, off, parts, k0, kt, n, tag = items[i]
                s = raw[i % NRAW]
                src = w_d[off:off + 128 * kt * n].rearrange("(p f) -> p f", p=128)
                landed[i] = sp.dma(lambda e, d=s.ap[:, 0:kt * n], src=src: e.dma_start(d, src), s, s.free)
                state["dma"] += 1

        mm_index = {}
        count = 0
        for i, it in enumerate(items):
            if it[0] == "mm":
                mm_index[i] = count
                count += 1

        def prepare(upto):
            while state["prep"] < min(upto, len(items)):
                i = state["prep"]
                kind, off, parts, k0, kt, n, tag = items[i]
                if kind == "mm":
                    s = raw[i % NRAW]
                    j = mm_index[i]
                    h, l = whr[j % NW], wlr[j % NW]
                    w = kt * n
                    th = act.op(lambda e, o=h.ap[:, 0:w], a=s.ap[:, 0:w]: e.activation(o, a, ACT.Copy),
                                [landed[i], h.free])
                    tl = dve.op(lambda e, o=l.ap[:, 0:w], a=s.ap[:, 0:w], b=h.ap[:, 0:w]:
                                e.tensor_tensor(o, a, b, ALU.subtract), [landed[i], th, l.free])
                    s.free = [th, tl]
                    ready[i] = (th, tl)
                    freed.add(i)
                    start_loads(i + NRAW + 1)
                else:
                    ada_piece(i)
                state["prep"] += 1

        t_c = load("c", cact[:, :], c_d.partition_broadcast(128), queue=sp)
        t_col = load("col", col[:, :], col_d, queue=sp)
        start_loads(2)
        t_x = load("x", x[:, :, :], x_d.rearrange("(k p) t -> p k t", p=128), queue=sp)
        start_loads(NRAW)

        late = [landed[NRAW - 1]]
        t_cst = [load("cst", cst[:, :], cst_d, late), t_ones]
        t_ws = load("ws", wsT[:, :, :], ws_d.rearrange("s (g t) -> s g t", g=16), late)
        t_bin = load("bin", binr[:, :], row_d.partition_broadcast(128), late)
        t_bs = load("bs", bsb[:, :, :].rearrange("p g t -> p (g t)"), bs_d.partition_broadcast(128), late)

        def mm(out, lhsT, rhs, start, stop, after=(), sig=False, **kw):
            return pe.op(lambda e: e.matmul(out, lhsT, rhs, start=start, stop=stop, skip_group_check=True, **kw),
                         after, sig)

        def transpose(out, in_, idn, after=(), sig=False):
            return pe.op(lambda e: e.transpose(out, in_, idn), after, sig)

        def activation(out, in_, func, after=(), **kw):
            return act.op(lambda e: e.activation(out, in_, func, **kw), after)

        def tt(out, a, b, op, after=()):
            return dve.op(lambda e: e.tensor_tensor(out, a, b, op), after)

        def stt(out, a, s, b, op0, op1, after=()):
            return dve.op(lambda e: e.scalar_tensor_tensor(out=out, in0=a, scalar=s, in1=b, op0=op0, op1=op1), after)

        def ts(out, a, s1, s2, op0, op1=None, after=()):
            if op1 is None:
                return dve.op(lambda e: e.tensor_scalar(out, a, s1, s2, op0), after)
            return dve.op(lambda e: e.tensor_scalar(out, a, s1, s2, op0, op1), after)

        t_cact = activation(cact[:, :], cact[:, :], ACT.Silu, [t_c])
        mod_tok = {}

        def ada_piece(i):
            kind, off, parts, k0, kt, n, c = items[i]
            s = raw[i % NRAW]
            for m in range(2):
                w = s.ap[:, 1024 * m:1024 * m + 1024]
                o = mod[:, 2 * c + m:2 * c + m + 1]
                t = dve.op(lambda e, w=w, o=o: e.tensor_tensor_reduce(w, w, cact[:, :], 1.0, 0.0, ALU.mult, ALU.add, o),
                           [landed[i], t_cact])
            s.free = [t]
            o = mod[:, 2 * c:2 * c + 2]
            bias = col[:, COL["ada_b"] + 2 * c:COL["ada_b"] + 2 * c + 2]
            mod_tok[c // 4] = tt(o, o, bias, ALU.add, [t, t_col])
            freed.add(i)
            start_loads(i + NRAW + 1)

        def next_piece(ahead=3):
            while items[state["use"]][0] == "ada":
                state["use"] += 1
            i = state["use"]
            j, seen = i, 0
            while j < len(items) and seen < ahead:
                seen += items[j][0] == "mm"
                j += 1
            prepare(j)
            state["use"] += 1
            return i

        def group(name, gi, xh, xl, xtok, mode, between=None, ahead=3):
            pair = pairs.take()
            n_done = 0
            while True:
                if between and n_done == 1:
                    between()
                i = next_piece(ahead if n_done == 0 else 3)
                n_done += 1
                kind, off, parts, k0, kt, n, tag = items[i]
                assert tag == (name, gi), (tag, name, gi)
                j = mm_index[i]
                last = i + 1 >= len(items) or all(
                    items[q][6] != tag or items[q][0] != "mm" for q in range(i + 1, min(i + 6, len(items))))
                wh = whr[j % NW].ap[:, 0:kt * n].rearrange("p (k n) -> p k n", k=kt)
                wl = wlr[j % NW].ap[:, 0:kt * n].rearrange("p (k n) -> p k n", k=kt)
                th, tl = ready[i]
                nm = n // 128 if mode == "T" else 2
                first = k0 == 0

                def product(m, k, w, xx, after, stop=False, sig=False):
                    wa, xa = w[:, k, :], xx[:, k0 + k, :]
                    if mode == "T":
                        out, lh, rh = pair.tiles[:, m, :], wa[:, m * 128:(m + 1) * 128], xa
                    else:
                        out, lh, rh = pair.rows[:, m, 0:n], xa[:, m * 128:(m + 1) * 128], wa
                    fresh = first and k == 0 and w is wh and xx is xh and (mode == "N" or m % 2 == 0)
                    return mm(out, lh, rh, fresh, stop, after, sig)

                if last:
                    toks = []
                    for m in range(nm):
                        for k in range(kt):
                            xt = xtok[k0 + k]
                            product(m, k, wh, xh, [th, xt[0], pair.free() if first and k == 0 else None])
                            product(m, k, wh, xl, [xt[1]])
                            t = product(m, k, wl, xh, [tl], k == kt - 1, k == kt - 1)
                        toks.append(t)
                    whr[j % NW].free = [t, tl]
                    wlr[j % NW].free = [t]
                    pair.toks = [toks[min(m | 1, nm - 1)] for m in range(len(toks))]
                    return pair, t
                for k in range(kt):
                    xt = xtok[k0 + k]
                    for m in range(nm):
                        product(m, k, wh, xh, [th, xt[0], pair.free() if first and k == 0 else None])
                        t = product(m, k, wh, xl, [xt[1]], sig=(m == nm - 1 and k == kt - 1))
                whr[j % NW].free = [t, tl]
                for k in range(kt):
                    for m in range(nm):
                        t = product(m, k, wl, xh, [tl], sig=(m == nm - 1 and k == kt - 1))
                wlr[j % NW].free = [t]

        def split(dsth, dstl, src, after, waitfree=()):
            th = activation(dsth, src, ACT.Copy, [after, waitfree])
            tl = tt(dstl, src, dsth, ALU.subtract, [th, after])
            return th, tl

        def root_tables():
            activation(warm[:, :], eps[0:1, :], ACT.Ln, [t_eps])

        class Stats:

            def __init__(self, dst, extra=None):
                self.b, self.i, self.dst, self.tm, self.todo = misc.take(), 0, dst, None, []
                if extra:
                    row, t = extra
                    self.tm = mm(self.b.ap[:, 0:T], ones[0:1, :], row, True, False, [t, t_ones, self.b.free], sig=True)
                    e2.free = [self.tm]

            def add(self, src, toks, now=True):
                if self.i % 4 == 0:
                    self.a = ta.take()
                sq = self.a.ap[:, self.i % 4, :]
                t = activation(sq, src, ACT.Square, [toks, self.a.free if self.i % 4 == 0 else None])
                self.todo.append((self.i, self.a, sq, t))
                self.i += 1
                if now:
                    self.sum()

            def sum(self):
                for i, a, sq, t in self.todo:
                    self.tm = mm(self.b.ap[:, 0:T], ones, sq, self.tm is None, i == 7,
                                 [t, t_ones, self.b.free if i == 0 else None], sig=True)
                    if i % 4 == 3:
                        a.free = [self.tm]
                self.todo = []

            def done(self):
                t = activation(lnv[:, :], self.b.ap[:, 0:T], ACT.Ln, [self.tm, t_eps, state.get("lnv")],
                               bias=eps[:, 0:1], scale=1.0 / D)
                state["lnv"] = t = activation(self.dst.ap[:, :], lnv[:, :], ACT.Exp, [t, self.dst.free], scale=-0.5)
                self.b.free = [t]
                return t

            def times_eps(self):
                t = activation(e2.ap[:, :], self.b.ap[0:1, 0:T], ACT.Identity, [self.tm, t_eps, e2.free],
                               bias=eps2[:, 0:1], scale=EPS)
                self.b.free = [t]
                return (e2.ap[:, :], t)

        def bc4(ap, n=4):
            return ap.unsqueeze(1).to_broadcast([128, n, ap.shape[-1]])

        x_tok = [t_x] * 8

        def make_h(acols, bcols, t_rs, after, tiles=range(8)):
            toks = []
            for m in tiles:
                if m % 4 == 0 or m == tiles[0]:
                    s = tb.take()
                o = s.ap[:, m % 4, :]
                t = stt(o, x[:, m, :], acols[:, m:m + 1], rsx.ap[:, :], ALU.mult, ALU.mult,
                        [x_tok[m], t_rs, after, s.free if m % 4 == 0 else None])
                th = activation(hh.ap[:, m, :], o, ACT.Identity, [t, hh.free, after], bias=bcols[:, m:m + 1])
                tl = stt(hl.ap[:, m, :], o, bcols[:, m:m + 1], hh.ap[:, m, :], ALU.add, ALU.subtract,
                         [th, hl.free])
                toks.append((th, tl))
                s.free = [tl]
            rsx.free = [tl]
            return toks

        def residual(outs, scols, after, extra=None, nxt=None, more=True):
            y = Stats(rsy, extra)
            for half, (p, _) in enumerate(outs):
                for m in range(4):
                    y.add(p.tiles[:, m, :], p.toks[m])
            t_rs = y.done()
            nx = Stats(rsx) if more else None
            toks = []
            for half, (p, _) in enumerate(outs):
                s = tb.take()
                for m in range(4):
                    k = 4 * half + m
                    t = stt(s.ap[:, m, :], p.tiles[:, m, :], scols[:, k:k + 1], rsy.ap[:, :],
                            ALU.mult, ALU.mult, [p.toks[m], t_rs, after, s.free if m == 0 else None])
                    if m == 3:
                        p.release(t)
                    x_tok[k] = tt(x[:, k, :], x[:, k, :], s.ap[:, m, :], ALU.add, [t, x_tok[k]])
                    if nxt is not None:
                        g = nxt[:, k:k + 1]
                        th = activation(hh.ap[:, k, :], x[:, k, :], ACT.Copy, [x_tok[k], hh.free], scale=g)
                        toks.append(th)
                        if k:
                            toks[k - 1] = (toks[k - 1], low_part(nxt, k - 1, toks[k - 1]))
                    if more:
                        nx.add(x[:, k, :], [x_tok[k]], nxt is None)
                s.free = [x_tok[k]]
            rsy.free = [t]
            if nxt is not None:
                toks[7] = (toks[7], low_part(nxt, 7, toks[7]))
            state["x"] = nx.done() if more and nxt is None else nx
            return toks

        def late_stats():
            nx = state["x"]
            nx.sum()
            state["x"] = nx.done()
            state["e2"] = nx.times_eps()

        def low_part(nxt, k, th):
            return stt(hl.ap[:, k, :], x[:, k, :], nxt[:, k:k + 1], hh.ap[:, k, :], ALU.mult, ALU.subtract,
                       [th, hl.free])

        def both(name, xh, xl, xtok, mode="T"):
            root_tables()
            return [group(name, g, xh, xl, xtok, mode) for g in range(2)]

        def modcols(sec):
            return mod[:, 8 * sec:8 * sec + 8]

        def pcols(name, i):
            return col[:, COL[name] + 8 * i:COL[name] + 8 * i + 8]

        ndr = [0]

        def scaled(gains, sec, add_one):
            o = der[:, ndr[0] % 10, :]
            ndr[0] += 1
            t = stt(o, modcols(sec), 1.0 if add_one else 0.0, gains, ALU.add, ALU.mult, [mod_tok[sec], t_col])
            return o, t

        def swiglu(tag, toks, late=False):
            name = "gu" + tag
            ht = []
            hidh.free, hidl.free = [hidh.free], [hidl.free]
            for i in range(6):
                nt = 4 if i < 5 else 2
                if i < 5:
                    pg, tg = group(name, 2 * i, hh.ap, hl.ap, toks, "T", late_stats if late and i == 0 else None)
                    g_ps = pg.tiles[:, :, :]
                else:
                    pg, tg = group(name, 10, hh.ap, hl.ap, toks, "T")
                    g_ps = pg.tiles[:, 0:2, :]
                a = ta.take()
                if late:
                    t = tt(a.ap[:, 0:nt, :], g_ps, bc4(rsx.ap[:, :], nt), ALU.mult, [tg, a.free, state["x"]])
                    if i < 5:
                        pg.release(t)
                    rsx.free = [t]
                    t = activation(a.ap[:, 0:nt, :], a.ap[:, 0:nt, :], ACT.Silu, [t])
                else:
                    t = activation(a.ap[:, 0:nt, :], g_ps, ACT.Silu, [tg, a.free])
                    if i < 5:
                        pg.release(t)
                if i < 5:
                    pu, tu = group(name, 2 * i + 1, hh.ap, hl.ap, toks, "T")
                    u_ps = pu.tiles[:, :, :]
                else:
                    pu, tu = pg, tg
                    u_ps = pg.tiles[:, 2:4, :]
                s = tb.take()
                t = tt(s.ap[:, 0:nt, :], a.ap[:, 0:nt, :], u_ps, ALU.mult, [t, tu, s.free])
                pu.release(t)
                a.free = [t]
                th, tl = split(hidh.ap[:, 4 * i:4 * i + nt, :], hidl.ap[:, 4 * i:4 * i + nt, :],
                               s.ap[:, 0:nt, :], t, [hidh.free, hidl.free])
                s.free = [th, tl]
                ht += [(th, tl)] * nt
            hh.free = hl.free = [tu]
            outs = both("dn" + tag, hidh.ap, hidl.ap, ht)
            hidh.free = hidl.free = [outs[1][1]]
            return outs

        root_tables()
        sx = Stats(rsx)
        for k in range(8):
            sx.add(x[:, k, :], [t_x])
        t_rs = sx.done()
        sx.b.free = [t_rs]
        htok = []

        def first_h(j):
            prepare([2, 4, 7, 9][j])
            c = slice(2 * j, 2 * j + 2)
            o = der[:, 0, c]
            t = stt(o, modcols(1)[:, c], 1.0, pcols("pre_mix_g", 0)[:, c], ALU.add, ALU.mult, [mod_tok[0], mod_tok[1]])
            htok.extend(make_h(der[:, 0, :], modcols(0), t_rs, [t], range(2 * j, 2 * j + 2)))

        def second_half():
            first_h(2)
            first_h(3)

        first_h(0)
        first_h(1)
        ndr[0] = 1

        bst = small[:, 0:48].rearrange("p (a g s) -> p a g s", a=2, g=4)
        mv = small[:, 48:52].rearrange("p (a s) -> p a s", a=2)
        rstd = small[:, 52:54]
        v_tok = []
        for g in range(4):
            p, t = group("a_v", g, hh.ap, hl.ap, htok, "N",
                         *((second_half, 1) if g == 0 else ()))
            s = tb.take()
            bias = binr[:, 512 * g:512 * g + 512]
            t = tt(s.ap[:, :, :].rearrange("p (a b) t -> p a (b t)", a=2), p.rows, bc4(bias, 2), ALU.add,
                   [t, t_bin, s.free])
            p.release(t)
            vg = v[:, :, 512 * g:512 * g + 512]
            t = activation(vg, s.ap[:, :, :].rearrange("p (a b) t -> p a (b t)", a=2), ACT.Gelu_apprx_tanh, [t])
            s.free = [t]
            if g == 0:
                t_tri = tt(wsT[:, :, :], wsT[:, :, :], bc4(C("tri"), 16), ALU.mult, [t_ws, t_cst])
            for a in range(2):
                t = dve.op(lambda e, o=bst[:, a, g, :], i=v[:, a, 512 * g:512 * g + 512]: e.bn_stats(o, i), [t])
        for a in range(2):
            t = dve.op(lambda e, o=mv[:, a, :], i=bst[:, a, :, :].rearrange("p g s -> p (g s)"): e.bn_aggr(o, i), [t])
        t = activation(rstd, mv[:, :, 1], ACT.Sqrt, [t, t_eps], bias=eps[:, 0:1])
        t = dve.op(lambda e: e.reciprocal(rstd, rstd), [t])
        for a in range(2):
            t_v = ts(v[:, a, :], v[:, a, :], mv[:, a, 0:1], rstd[:, a:a + 1], ALU.subtract, ALU.mult, [t])

        wsf = wsT[:, :, :].rearrange("p g t -> p (g t)")
        for q in range(4):
            b = misc.take()
            t = mm(b.ap[:, :], ones, wsf[:, 512 * q:512 * q + 512], True, True, [t_tri, t_cst, b.free], sig=True)
            for g in range(4):
                gg = 4 * q + g
                t_q = stt(bsb[:, gg, :], b.ap[:, 128 * g:128 * g + 128], colat("a_ln_b", gg), bsb[:, gg, :],
                          ALU.mult, ALU.add, [t, t_bs, t_col])
            b.free = [t_q]

        spt = place("spt", [128, 16, T], F32, side)

        def gelu_u(g):
            p, tg = group("a_u", g, hh.ap, hl.ap, htok, "T")
            a = ta.take()
            for m in range(4):
                t = activation(a.ap[:, m, :], p.tiles[:, m, :], ACT.Gelu_apprx_tanh, [tg, a.free, t_col],
                               bias=colat("a_b_u", 4 * g + m))
            p.release(t)
            return a, t, tg

        u0 = gelu_u(0)
        sp_tok = []
        for q in range(4):
            p = pairs.take()
            for g in range(4):
                for n in range(2):
                    t = mm(p.tiles[:, g, 128 * n:128 * n + 128], v[:, n, 128 * (4 * q + g):128 * (4 * q + g) + 128],
                           wsT[:, 4 * q + g, :], g % 2 == 0 and n == 0, True,
                           [t_v, t_tri, p.free()], sig=(g == 3 and n == 1))
            for g in range(4):
                gg = 4 * q + g
                t2 = stt(spt[:, gg, :].rearrange("p (n t) -> p n t", n=2),
                         p.tiles[:, g, :].rearrange("p (n t) -> p n t", n=2), colat("a_ln_g", gg),
                         bc4(bsb[:, gg, :], 2), ALU.mult, ALU.add, [t, t_q])
            p.release(t2)
            sp_tok.append(t2)
            t_sp_pe = t
        hidh.free = [t_sp_pe, sp_tok[-1]]
        hidl.free = [t_sp_pe, sp_tok[-1]]
        ht = []
        for g in range(4):
            a, t, tg = u0 if g == 0 else gelu_u(g)
            s = tb.take()
            t = tt(s.ap[:, :, :], a.ap[:, :, :], spt[:, 4 * g:4 * g + 4, :], ALU.mult, [t, sp_tok[g], s.free])
            a.free = [t]
            th, tl = split(hidh.ap[:, 4 * g:4 * g + 4, :], hidl.ap[:, 4 * g:4 * g + 4, :], s.ap[:, :, :], t,
                           [hidh.free, hidl.free])
            s.free = [th, tl]
            ht += [(th, tl)] * 4
        t_side = t
        hh.free = hl.free = [tg]
        outs = both("a_out", hidh.ap, hidl.ap, ht)
        hidh.free = hidl.free = [outs[1][1]]

        def after_mix(layer, outs):
            s1, t1 = scaled(pcols("post_mix_g", layer), 6 * layer + 2, False)
            a1, t2 = scaled(pcols("pre_ffn_g", layer), 6 * layer + 4, True)
            residual(outs, s1, [t1])
            return make_h(a1, modcols(6 * layer + 3), state["x"], [t2, mod_tok[6 * layer + 3]])

        htok = after_mix(0, outs)
        outs = swiglu("0", htok)
        s1, t1 = scaled(pcols("post_ffn_g", 0), 5, False)
        a1, t2 = scaled(pcols("kv_norm_g", 0), 13, True)
        residual(outs, s1, [t1])

        t_rs = state["x"]
        htok = make_h(a1, modcols(12), t_rs, [t2, mod_tok[12]])

        Sb = Ring([Slot(place(f"Sb{i}", [128, T], F32, side + 1024 * i)) for i in range(4)])
        Pb = Ring([Slot(place(f"Pb{i}", [128, T], F32, side + 4096 + 1024 * i)) for i in range(6)])
        PT = Ring([Slot(place(f"PT{i}", [128, T], F32, side + 10240 + 1024 * i)) for i in range(4)])
        st = place("st", [128, 64, 4], F32, side + 14336)
        dT = place("dT", [128, T], F32, big + 32768)
        dL = place("dL", [128, T], F32, big + 33792)
        dR = place("dR", [128, 4, T], F32, big + 38912)
        side_free = [t_side, sp_tok]
        for ring in (Sb, Pb, PT):
            for s in ring.slots:
                s.free = [side_free]
        qT = place("qT", [128, 8, T], F32, big)
        kT = place("kT", [128, 8, T], F32, big + 8192)
        vv = place("vv", [128, 2, 1024], F32, big + 16384)
        gT = place("gT", [128, 8, T], F32, big + 24576)
        lf = [place(f"lf{i}", [128, T], F32, big + 34816 + 1024 * i) for i in range(3)]
        big_free = hidh.free

        p, t = group("kv_f", 0, hh.ap, hl.ap, htok, "T")
        t = ts(lf[0][:, :], p.tiles[:, 0, :], colat("b_f"), None, ALU.add, after=[t, big_free, t_col])
        p.release(t)
        t2 = activation(lf[1][:, :], lf[0][:, :], ACT.Abs, [t])
        t2 = activation(lf[1][:, :], lf[1][:, :], ACT.Exp, [t2], scale=-1.0)
        t2 = activation(lf[1][:, :], lf[1][:, :], ACT.Ln, [t2], bias=1.0)
        t = stt(lf[2][:, :], lf[0][:, :], 0.0, lf[1][:, :], ALU.min, ALU.subtract, [t, t2])
        t = dve.op(lambda e: e.tensor_tensor_scan(dT[:, :], ones[:, 0:1].to_broadcast([128, T]), lf[2][:, :], 0.0,
                                                  ALU.mult, ALU.add), [t])
        fc = C("forget")
        t_d = t = ts(dL[:, :], dT[:, :], fc[:, 0:1], fc[:, 1:2], ALU.mult, ALU.add, after=[t, t_cst])
        for j in range(4):
            t_d = ts(dR[:, j, :], dT[:, :], fc[:, 2 + j:3 + j], fc[:, 6 + j:7 + j], ALU.mult, ALU.add, after=[t])

        def head_norm(p, t0, gcol, dst, toks):
            a = ta.take()
            ts_ = [activation(a.ap[:, 2 * n:2 * n + 2, :], p.tiles[:, 2 * n:2 * n + 2, :], ACT.Square, [t0, a.free])
                   for n in range(2)]

            def rest():
                s = tb.take()
                for n in range(2):
                    b = misc.take()
                    for m in range(2):
                        tm = mm(b.ap[:, 256 * m:256 * m + 256], C("bd64"), a.ap[:, 2 * n + m, :], m == 0, True,
                                [ts_[n], t_cst, b.free], sig=(m == 1))
                    o = s.ap[:, 2 * n:2 * n + 2, :]
                    t = activation(o, b.ap.rearrange("p (m t) -> p m t", m=2), ACT.Ln, [tm, s.free],
                                   bias=eps[:, 0:1], scale=1.0 / 64)
                    b.free = [t]
                    t = activation(o, o, ACT.Exp, [t], scale=-0.5)
                    t = stt(dst[:, 2 * n:2 * n + 2, :], p.tiles[:, 2 * n:2 * n + 2, :], gcol, o, ALU.mult, ALU.mult,
                            [t, t0, big_free, t_col])
                a.free = [tm]
                p.release(t)
                s.free = [t]
                toks.append(t)
            return rest

        qg = small[:, 62:63]
        t_qg = ts(qg, colat("q_norm"), 0.125, None, ALU.mult, after=[t_col])
        qk_tok = [t_qg]
        rest = None
        for g in range(2):
            p, t = group("kv_k", g, hh.ap, hl.ap, htok, "T", rest)
            rest = head_norm(p, t, colat("k_norm"), kT[:, 4 * g:4 * g + 4, :], qk_tok)
        for g in range(2):
            p, t = group("kv_v", g, hh.ap, hl.ap, htok, "N", rest)
            rest = None
            hh.free = hl.free = [t]
            t = activation(vv[:, :, 512 * g:512 * g + 512], p.rows, ACT.Copy, [t, big_free])
            p.release(t)
            t_vv = t
        a1, t1 = scaled(pcols("pre_mix_g", 1), 7, True)
        htok = make_h(a1, modcols(6), t_rs, [t1, mod_tok[6]])
        for g in range(2):
            p, t = group("q", g, hh.ap, hl.ap, htok, "T", rest)
            rest = head_norm(p, t, qg, qT[:, 4 * g:4 * g + 4, :], qk_tok)
        for g in range(2):
            p, t = group("gate", g, hh.ap, hl.ap, htok, "T", rest)
            rest = None
            hh.free = hl.free = [t]
            t = activation(gT[:, 4 * g:4 * g + 4, :], p.tiles, ACT.Sigmoid, [t, big_free])
            p.release(t)
            t_gate = t

        nst = [0]

        def attention(units, sbanks, tbanks, finish):
            S_r = Ring(sbanks)
            T_r = Ring(tbanks)
            O_r = Ring([banks[6], banks[7]])
            live = [dict(u) for u in units]
            o_bank = {}

            def scores(u):
                nk = u["nk"]
                u["s"] = []
                for terms in u["subs"]:
                    b = S_r.take()
                    for n, (c0, c1, l, r) in enumerate(terms):
                        t = mm(b.ap[:, c0:c1], l, r, n == 0, n == len(terms) - 1,
                               [u["after"], b.free] if n == 0 else (), sig=(n == len(terms) - 1))
                    sbuf = Sb.take()
                    k = nst[0] % 64
                    nst[0] += 1
                    if u["mask"] is None:
                        t = dve.op(lambda e, o=sbuf.ap[:, 0:nk], i=b.ap[:, 0:nk], m=st[:, k, 0:1]:
                                   e.tensor_scalar(o, i, -1.0, None, ALU.mult, ALU.min, accum_out=m),
                                   [t, sbuf.free])
                    else:
                        t = dve.op(lambda e, o=sbuf.ap[:, 0:nk], i=b.ap[:, 0:nk], m=st[:, k, 0:1], mk=u["mask"]:
                                   e.tensor_tensor_reduce(o, i, mk, -1.0, 3.4e38, ALU.add, ALU.min, m),
                                   [t, sbuf.free, t_cst, u["after"]])
                    b.free = [t]
                    u["s"].append((sbuf, k, t))

            def exps(u):
                nk = u["nk"]
                u["p"] = []
                for sbuf, k, t in u["s"]:
                    pb = Pb.take()
                    t = activation(pb.ap[:, 0:nk], sbuf.ap[:, 0:nk], ACT.Exp, [t, pb.free], scale=-1.0,
                                   bias=st[:, k, 0:1], accum_out=st[:, k, 1:2])
                    sbuf.free = [t]
                    u["p"].append((pb, k, t))

            def normalise(u):
                nk = u["nk"]
                rt = []
                for pb, k, t in u["p"]:
                    rt.append(dve.op(lambda e, o=st[:, k, 2:3], i=st[:, k, 1:2]: e.reciprocal(o, i), [t]))
                if len(rt) == 1:
                    pb, k, t = u["p"][0]
                    u["w"] = (pb, ts(pb.ap[:, 0:nk], pb.ap[:, 0:nk], st[:, k, 2:3], None, ALU.mult, after=[rt[0]]))
                else:
                    (p0, k0, _), (p1, k1, _) = u["p"]
                    t = ts(p1.ap[:, 0:nk], p1.ap[:, 0:nk], st[:, k1, 2:3], nlam, ALU.mult, ALU.mult,
                           after=[rt[1], t_lam])
                    t = stt(p0.ap[:, 0:nk], p0.ap[:, 0:nk], st[:, k0, 2:3], p1.ap[:, 0:nk], ALU.mult, ALU.add,
                            [t, rt[0]])
                    p1.free = [t]
                    u["w"] = (p0, t)

            def turn(u):
                nk = u["nk"]
                pb, t = u["w"]
                b = T_r.take()
                for kb in range(nk // 128):
                    tt_ = transpose(b.ap[:, 128 * kb:128 * kb + 128], pb.ap[:, 128 * kb:128 * kb + 128], ident,
                                    [t, b.free], sig=(kb == nk // 128 - 1))
                pb.free = [tt_]
                pt = PT.take()
                t = activation(pt.ap[:, 0:nk], b.ap[:, 0:nk], ACT.Copy, [tt_, pt.free])
                b.free = [t]
                u["pt"] = (pt, t)

            def values(u):
                pt, t = u["pt"]
                if u["tile"] not in o_bank:
                    o_bank[u["tile"]] = O_r.take()
                b = o_bank[u["tile"]]
                out = b.ap[u["rows"], 128 * u["qb"]:128 * u["qb"] + 128]
                n = u["nk"] // 128
                for kb in range(n):
                    tv = mm(out, u["v"](kb), pt.ap[:, 128 * kb:128 * kb + 128], kb == 0, kb == n - 1,
                            [t, u["vtok"], b.free], sig=(kb == n - 1))
                pt.free = [tv]
                if u["last"]:
                    finish(u["tile"], b, tv)

            for i in range(len(live) + 4):
                for stage, lag in ((scores, 0), (exps, 1), (normalise, 2), (turn, 3), (values, 4)):
                    if 0 <= i - lag < len(live):
                        stage(live[i - lag])

        def plain_units(qq, kk, vt, mask, after, extra=None, heads=16):
            us = []
            for h in range(heads):
                for qb in range(2):
                    nk = 128 * (qb + 1)
                    r = slice(64 * (h % 2), 64 * (h % 2) + 64)
                    terms = [(0, nk, qq[r, h // 2, 128 * qb:128 * qb + 128], kk[r, h // 2, 0:nk])]
                    if extra:
                        terms += extra(h, qb, nk)
                    us.append(dict(subs=[terms], nk=nk, mask=mask(qb), after=after, rows=r, tile=h // 2, qb=qb,
                                   v=(lambda kb, h=h: vt[:, kb, 64 * h:64 * h + 64]), vtok=after,
                                   last=(h % 2 == 1 and qb == 1)))
            return us

        def cmask(name):
            m = C(name)
            return lambda qb: m[:, 128:256] if qb == 0 else m

        ho = [None] * 8

        def forget_terms(h, qb, nk):
            r = slice(32 * (h % 4), 32 * (h % 4) + 32)
            return [(0, nk, dL[r, 128 * qb:128 * qb + 128], dR[r, h // 4, 0:nk])]

        def finish_fox(tile, b, t):
            s = tb.take()
            t = tt(s.ap[:, 0, :], b.ap[:, 0:T], gT[:, tile, :], ALU.mult, [t, t_gate, s.free])
            b.free = [t]
            th, tl = split(hh.ap[:, tile, :], hl.ap[:, tile, :], s.ap[:, 0, :], t, [hh.free, hl.free])
            s.free = [th, tl]
            ho[tile] = (th, tl)

        attention(plain_units(qT, kT, vv, cmask("causal"), [qk_tok, t_vv, t_d], forget_terms),
                  banks[0:3], banks[3:6], finish_fox)
        hidh.free = hidl.free = [ho[7][0], ho[7][1], (pe.sem, pe.n)]
        outs = both("o", hh.ap, hl.ap, list(ho))
        hh.free = hl.free = [outs[1][1]]
        half_g = sb("half_g", [128, 4, 8])
        hg = {}
        for n, i in enumerate((1, 5, 7, 11)):
            hg[i] = (half_g[:, n, :], ts(half_g[:, n, :], pcols("norm_g", i), 0.5, None, ALU.mult, after=[t_col]))

        prod = small[0:64, 56:58]
        el = small[:, 58:60]
        nlam = small[:, 60:61]
        lp = col[0:64, COL["lam"]:COL["lam"] + 4].rearrange("p (a b) -> p a b", b=2)
        t = tt(prod, lp[:, :, 0], lp[:, :, 1], ALU.mult, [t_col])
        b = misc.take()
        t = mm(b.ap[:, 0:2], ones[0:64, :], prod, True, True, [t, b.free], sig=True)
        t = activation(el, b.ap[:, 0:2], ACT.Exp, [t])
        b.free = [t]
        t_lam = stt(nlam, el[:, 1:2], LAMBDA_INIT, el[:, 0:1], ALU.subtract, ALU.subtract, [t])
        sub8 = small[:, 61:62]
        t_sub = ts(sub8, colat("subln"), 1.0 - LAMBDA_INIT, None, ALU.mult, after=[t_col])

        htok = after_mix(1, outs)
        outs = swiglu("1", htok)
        s1, t1 = scaled(pcols("post_ffn_g", 1), 11, False)
        htok = residual(outs, s1, [t1], nxt=pcols("norm_g", 0))

        def ffn2(tag, htok, post, nxt):
            outs = swiglu(tag, htok, True)
            return residual(outs, hg[post][0], [hg[post][1]], state["e2"], nxt, nxt is not None)

        rcol = small[:, 62:64]

        def rs_column():
            b = misc.take()
            for n in range(2):
                t = mm(b.ap[:, n:n + 1], rsx.ap[0:1, 128 * n:128 * n + 128], ones[0:1, 0:1], True, True,
                       [state["x"], b.free], sig=(n == 1))
            b.free = [dve.op(lambda e: e.tensor_copy(rcol, b.ap[:, 0:2]), [t])]
            return b.free[0]

        def scaled_rows(dst, p, after):
            for n in range(2):
                t = activation(dst[:, n, :], p.rows[:, n, :], ACT.Copy, after, scale=rcol[:, n:n + 1])
            p.release(t)
            return t

        htok = ffn2("2", htok, 1, pcols("norm_g", 2))

        aq = place("aq", [128, 4, T], F32, big)
        ak = place("ak", [128, 4, T], F32, big + 4096)
        av = place("av", [128, 2, 512], F32, big + 8192)
        bq = place("bq", [128, 4, T], F32, big + 12288)
        bk = place("bk", [128, 4, T], F32, big + 16384)
        bv = place("bv", [128, 2, 512], F32, big + 20480)
        ix = place("ix", [128, 3, T], F32, big + 24576)
        iw = place("iw", [128, 2, 8], F32, big + 27648)
        sc = place("sc", [128, 2, T], F32, big + 28672)
        sel = place("sel", [128, 2, T], F32, big + 30720)
        rl = Ring([Slot(place(f"rl{i}", [128, 512], F32, big + 32768 + 2048 * i)) for i in range(3)])
        oa = place("oa", [128, 4, T], F32, big + 38912)
        top8 = place("top8", [128, 2, 8], F32, big + 43008)
        big_free = hidh.free
        for s in rl.slots:
            s.free = [big_free]

        tables = {}
        p, t = group("idx", 0, hh.ap, hl.ap, htok, "T", late_stats)
        for n, name in enumerate(("cos32", "sin32", "cos64", "sin64")):
            o = Sb.slots[n]
            tables[name] = (o.ap[:, :], tt(o.ap[:, :], C(name), rsx.ap[:, :], ALU.mult, [state["x"], o.free, t_cst]))
        t_rc = rs_column()

        def rope(p, t0, nt, kind, dst, scale, keep=False):
            (cos, tc), (sin, tn) = tables["cos" + kind], tables["sin" + kind]
            a = ta.take()
            t = activation(a.ap[:, :, :], p.tiles, ACT.Copy, [t0, a.free])
            p.release(t)
            q = pairs.take()
            for m in range(nt):
                tm = mm(q.tiles[:, m, :], C("rot" + kind), a.ap[:, m, :], m % 2 == 0, True, [t, q.free()],
                        sig=(m == nt - 1))
            s = tb.take()
            t1 = stt(dst, a.ap[:, 0:nt, :], scale, bc4(cos, nt), ALU.mult, ALU.mult, [t, tc, big_free])
            t2 = stt(s.ap[:, 0:nt, :], q.tiles[:, 0:nt, :], scale, bc4(sin, nt), ALU.mult, ALU.mult,
                     [tm, tn, s.free])
            q.release(t2)
            t3 = tt(dst, dst, s.ap[:, 0:nt, :], ALU.add, [t1, t2])
            s.free = [t3]
            a.free = [t1, tm]
            return (t3, a, t) if keep else t3

        t_ix, a, t_raw = rope(p, t, 3, "32", ix[:, :, :], 1.0, keep=True)
        b = misc.take()
        for n in range(2):
            t = transpose(b.ap[:, 128 * n:128 * n + 128], a.ap[:, 3, 128 * n:128 * n + 128], ident, [t_raw, b.free],
                          sig=(n == 1))
        a.free = [a.free, t]
        for n in range(2):
            t_iw = ts(iw[:, n, :], b.ap[:, 128 * n:128 * n + 8], rcol[:, n:n + 1], 0.0625, ALU.mult, ALU.mult,
                      after=[t, t_rc, big_free])
        b.free = [t_iw]
        p, t = group("bqkv", 0, hh.ap, hl.ap, htok, "T")
        t_bq = rope(p, t, 4, "64", bq[:, :, :], 0.125)

        t_acc = None
        for qb in (1, 0):
            nk = 128 * (qb + 1)
            for jj in (0, 1):
                pp = [pairs.take(), pairs.take()]
                bk4 = [pp[0].b[0], pp[0].b[1], pp[1].b[0], pp[1].b[1]]
                for j in range(4):
                    h = 4 * jj + j
                    r = slice(32 * j, 32 * j + 32)
                    t = mm(bk4[j].ap[:, 0:nk], ix[r, jj, 128 * qb:128 * qb + 128], ix[r, 2, 0:nk], True, True,
                           [t_ix, bk4[j].free], sig=True)
                    s = rl.take()
                    t = activation(s.ap[:, 0:nk], bk4[j].ap[:, 0:nk], ACT.Relu, [t, s.free])
                    bk4[j].free = [t]
                    o = sc[:, qb, 0:nk]
                    if h == 0:
                        t = ts(o, s.ap[:, 0:nk], iw[:, qb, 0:1], None, ALU.mult, after=[t, t_iw])
                    else:
                        t = stt(o, s.ap[:, 0:nk], iw[:, qb, h:h + 1], o, ALU.mult, ALU.add, [t, t_acc])
                    s.free = [t]
                    t_acc = t
            o = sc[:, qb, 0:nk]
            t_acc = tt(o, o, cmask("chunk")(qb), ALU.add, [t_acc, t_cst])
        p, t = group("bqkv", 1, hh.ap, hl.ap, htok, "T")
        t_bk = rope(p, t, 4, "64", bk[:, :, :], 1.0)

        def top64(rounds):
            t = t_acc
            for _ in range(rounds):
                for qb in range(2):
                    nk = 128 * (qb + 1)
                    s8, o = top8[:, qb, :], sc[:, qb, 0:nk]
                    t = dve.op(lambda e, a=s8, b=o: e.max(a, b), [t])
                    t = dve.op(lambda e, a=s8, b=o: e.match_replace(b, a, b, GONE), [t])
            return t

        p, t = group("bqkv", 2, hh.ap, hl.ap, htok, "N")
        t_bv = scaled_rows(bv, p, [t, t_rc, big_free])
        t_acc = top64(4)
        p, t = group("aqkv", 0, hh.ap, hl.ap, htok, "T")
        t_aq = rope(p, t, 4, "64", aq[:, :, :], 0.125)
        t_acc = top64(4)
        p, t = group("aqkv", 1, hh.ap, hl.ap, htok, "T")
        t_ak = rope(p, t, 4, "64", ak[:, :, :], 1.0)
        for qb in range(2):
            nk = 128 * (qb + 1)
            o = sel[:, qb, 0:nk]
            t = ts(o, sc[:, qb, 0:nk], -3.15e38, BIG, ALU.is_lt, ALU.mult, after=[t_acc])
            t_sel = ts(o, o, BIG, None, ALU.subtract, after=[t])
        p, t = group("aqkv", 2, hh.ap, hl.ap, htok, "N")
        hh.free = hl.free = [t]
        t_av = scaled_rows(av, p, [t, t_rc, big_free])
        for o in Sb.slots:
            o.free = [o.free, t_ak]
        rsx.free = [t_rc]

        us = []
        for h in range(4):
            for qb in range(2):
                nk = 128 * (qb + 1)
                subs = [[(0, nk, aq[r, h, 128 * qb:128 * qb + 128], ak[r, h, 0:nk])] for r in (slice(0, 64), slice(64, 128))]
                us.append(dict(subs=subs, nk=nk, mask=cmask("chunk")(qb), after=[t_aq, t_ak], rows=slice(0, 128),
                               tile=h, qb=qb, v=(lambda kb, h=h: av[:, kb, 128 * h:128 * h + 128]), vtok=[t_av],
                               last=(qb == 1)))
        oa_tok = []

        def finish_a(tile, b, t):
            t = dve.op(lambda e, o=oa[:, tile, :], i=b.ap[:, 0:T]: e.tensor_copy(o, i), [t, big_free])
            b.free = [t]
            oa_tok.append(t)

        attention(us, banks[0:4], banks[4:6], finish_a)

        ho = [None] * 8
        a = ta.take()
        t = activation(a.ap[:, :, :], oa[:, :, :], ACT.Square, [oa_tok, a.free])
        q = pairs.take()
        for m in range(4):
            tm = mm(q.tiles[:, m, :], ones, a.ap[:, m, :], m % 2 == 0, True, [t, q.free()], sig=(m == 3))
        a.free = [tm]
        s = tb.take()
        t = activation(s.ap[:, :, :], q.tiles, ACT.Ln, [tm, s.free], bias=eps[:, 0:1], scale=1.0 / 128)
        q.release(t)
        t = activation(s.ap[:, :, :], s.ap[:, :, :], ACT.Exp, [t], scale=-0.5)
        t = stt(oa[:, :, :], oa[:, :, :], sub8, s.ap[:, :, :], ALU.mult, ALU.mult, [t, oa_tok, t_sub])
        s.free = [t]
        th, tl = split(hh.ap[:, 0:4, :], hl.ap[:, 0:4, :], oa[:, :, :], t, [hh.free, hl.free])
        ho[0:4] = [(th, tl)] * 4

        def finish_at(first):
            def f(tile, b, t):
                th, tl = split(hh.ap[:, first + tile, :], hl.ap[:, first + tile, :], b.ap[:, 0:T], t,
                               [hh.free, hl.free])
                b.free = [th, tl]
                ho[first + tile] = (th, tl)
            return f

        attention(plain_units(bq, bk, bv, lambda qb: sel[:, qb, 0:128 * (qb + 1)], [t_bq, t_bk, t_bv, t_sel],
                              heads=8), banks[0:3], banks[3:6], finish_at(4))
        hidh.free = hidl.free = [ho[3][0], ho[3][1], ho[7][0], ho[7][1], (pe.sem, pe.n)]
        outs = both("even_out", hh.ap, hl.ap, list(ho))
        hh.free = hl.free = [outs[1][1]]
        htok = residual(outs, pcols("norm_g", 3), [], nxt=pcols("norm_g", 4))
        htok = ffn2("3", htok, 5, pcols("norm_g", 6))
        htok = ffn2("4", htok, 7, pcols("norm_g", 8))

        big_free = hidh.free
        oq = place("oq", [128, 8, T], F32, big)
        ok = place("ok", [128, 8, T], F32, big + 8192)
        ov = place("ov", [128, 2, 1024], F32, big + 16384)
        bT = place("bT", [128, 16, T], F32, big + 24576)
        t_rel = load("rel", bT[:, :, :], rel_d, [big_free])
        for g in range(2):
            p, t = group("odd", g, hh.ap, hl.ap, htok, "T", late_stats if g == 0 else None)
            if g == 0:
                t_rc = rs_column()
            t_oq = stt(oq[:, 4 * g:4 * g + 4, :], p.tiles, 0.125, bc4(rsx.ap[:, :]), ALU.mult, ALU.mult,
                       [t, state["x"], big_free])
            p.release(t_oq)
        for g in range(2):
            p, t = group("odd", 2 + g, hh.ap, hl.ap, htok, "T")
            t_ok = tt(ok[:, 4 * g:4 * g + 4, :], p.tiles, bc4(rsx.ap[:, :]), ALU.mult, [t, big_free])
            p.release(t_ok)
        for g in range(2):
            p, t = group("odd", 4 + g, hh.ap, hl.ap, htok, "N")
            hh.free = hl.free = [t]
            t_ov = scaled_rows(ov[:, :, 512 * g:512 * g + 512], p, [t, t_rc, big_free])
        rsx.free = [t_ok, t_rc]

        ho = [None] * 8

        us = plain_units(oq, ok, ov, lambda qb: None, [t_oq, t_ok, t_ov, t_rel])
        for n, u in enumerate(us):
            u["mask"] = bT[:, n // 2, 256 - u["nk"]:256]
        attention(us, banks[0:3], banks[3:6], finish_at(0))
        hidh.free = hidl.free = [ho[7][0], ho[7][1], (pe.sem, pe.n)]
        outs = both("odd_out", hh.ap, hl.ap, list(ho))
        hh.free = hl.free = [outs[1][1]]
        htok = residual(outs, pcols("norm_g", 9), [], nxt=pcols("norm_g", 10))
        ffn2("5", htok, 11, None)

        s_out = Slot(None, sem("s_out"))
        ov_d = out_d.rearrange("(k p) t -> p k t", p=128)
        for i in range(2):
            t = sp.dma(lambda e, i=i: e.dma_start(ov_d[:, 4 * i:4 * i + 4, :], x[:, 4 * i:4 * i + 4, :]), s_out,
                       [x_tok[4 * i:4 * i + 4]])
        sp.wait([t])
        assert state["use"] == len(items)

        block = ctx.enter_context(nc.Block())

        @block.sync
        def _(e):
            sp.play(e)

        @block.gpsimd
        def _(e):
            pool.play(e)

        @block.scalar
        def _(e):
            act.play(e)

        @block.vector
        def _(e):
            dve.play(e)

        @block.tensor
        def _(e):
            pe.play(e)



def pack_stream(inputs):
    items, total = stream()
    out = np.empty((total,), np.float32)
    for kind, off, parts, k0, kt, n, tag in items:
        blocks = []
        for src, lead, g in parts:
            a = inputs[src]
            for i in lead:
                a = a[i]
            a = a[128 * k0:128 * (k0 + kt)]
            for p in g:
                if p[0] == "zero":
                    blocks.append(np.zeros((128 * kt, p[1]), np.float32))
                else:
                    blocks.append(a[:, p[1]:p[2]])
        w = blocks[0] if len(blocks) == 1 else np.concatenate(blocks, axis=1)
        if kind == "ada":
            w = w.reshape(1024, 2, 128).transpose(2, 1, 0)
        else:
            w = w.reshape(kt, 128, n).transpose(1, 0, 2)
        out[off:off + 128 * kt * n] = w.reshape(-1)
    return out


def pack_columns(inputs):
    def c(a):
        return np.asarray(a).reshape(-1, 128).T

    f16 = inputs["kv_b_f"]
    lam = inputs["even_lambda_2"][0].T
    made = {
        "ada_b": c(inputs["ada_b"]), "kv_ada_b": c(inputs["kv_ada_b"]),
        "pre_mix_g": c(inputs["pre_mix_g"]), "post_mix_g": c(inputs["post_mix_g"]),
        "pre_ffn_g": c(inputs["pre_ffn_g"]), "post_ffn_g": c(inputs["post_ffn_g"]),
        "kv_norm_g": c(inputs["kv_norm_g"]), "a_b_u": c(inputs["a_b_in"][0, :2048]),
        "a_ln_g": c(inputs["a_ln_g"]), "a_ln_b": c(inputs["a_ln_b"]), "norm_g": c(inputs["norm_g_2"]),
        "subln": c(inputs["even_subln_2"]), "q_norm": c(np.tile(inputs["b_q_norm_g"][0], 2)),
        "k_norm": c(np.tile(inputs["k_norm_g"], 2)), "b_f": c(np.tile(f16, 8)),
        "lam": np.concatenate([lam, np.zeros((64, 4), np.float32)], axis=0),
    }
    return np.ascontiguousarray(np.concatenate([made[n] for n, _ in COLS], axis=1))


def lay_out_bias(rel):
    q, k = np.arange(128)[:, None] + 128, np.arange(T)[None, :]
    out = rel[:, np.maximum(q - k + 63, 0)].transpose(1, 0, 2)
    return np.ascontiguousarray(np.where((k // 64 <= q // 64)[:, None, :], out, np.float32(-BIG)))


def kernel(**inputs):
    import concourse.bacc as _bacc
    from concourse.bass_utils import run_bass_kernel_spmd as _run

    inputs = {k: np.asarray(a) for k, a in inputs.items()}
    arrays = {
        "c": np.ascontiguousarray(inputs["c"].reshape(-1)),
        "w": pack_stream(inputs), "cols": pack_columns(inputs), "csts": constants(),
        "xT": np.ascontiguousarray(inputs["x"][0].T),
        "bin": np.ascontiguousarray(inputs["a_b_in"][0, 2048:]),
        "bs": np.ascontiguousarray(inputs["a_b_s"][0].reshape(-1)),
        "ws": np.ascontiguousarray(inputs["a_w_s"][0].transpose(2, 0, 1).reshape(128, 2048)),
        "rel": lay_out_bias(inputs["odd_rel_bias_2"][0]),
    }
    nc = _bacc.Bacc("TRN2", target_bir_lowering=False, num_devices=1)
    aps = {n: nc.dram_tensor("in_" + n, a.shape, F32, kind="ExternalInput").ap() for n, a in arrays.items()}
    out = nc.dram_tensor("out_T", (D, T), F32, kind="ExternalOutput").ap()
    build(nc, aps["c"], aps["w"], aps["cols"], aps["csts"], aps["xT"], aps["bin"], aps["bs"], aps["ws"], aps["rel"], out)
    r = _run(nc, [{"in_" + n: a for n, a in arrays.items()}], core_ids=[0])
    return np.ascontiguousarray(r.results[0]["out_T"].T)[None]
```

```python
from contextlib import ExitStack

import numpy as np

import concourse.bass as bass
from concourse import mybir

F32 = mybir.dt.float32
F32R = mybir.dt.float32r
ALU = mybir.AluOpType
ACT = mybir.ActivationFunctionType
AX_X = mybir.AxisListType.X

D = 1024
T = 256
F = 2816
EPS = 1e-6
BIG = 3e38
GONE = -3.3e38
LAMBDA_INIT = 0.8 - 0.6
MAXC = 2048
NRAW, NW = 5, 3



def cols(c0, n=512):
    return [("w", c0, c0 + n)]


def projections():
    out = []

    def add(name, src, lead, kt, groups):
        out.append((name, kt, [[(src, lead, g)] if isinstance(g, list) else g for g in groups]))

    def split(c0, n):
        return [cols(c0 + 512 * i) for i in range(n)]

    def ffn(tag, gate, up, down, lead):
        (gs, g0), (us, u0) = gate, up
        groups = []
        for i in range(5):
            groups += [((gs, lead, cols(g0 + 512 * i)),), ((us, lead, cols(u0 + 512 * i)),)]
        groups.append(((gs, lead, cols(g0 + 2560, 256)), (us, lead, cols(u0 + 2560, 256))))
        add("gu" + tag, None, None, 8, groups)
        add("dn" + tag, down, lead, 22, split(0, 2))

    add("a_v", "a_w_in", (0,), 8, split(2048, 4))
    add("a_u", "a_w_in", (0,), 8, split(0, 4))
    add("a_out", "a_w_out", (0,), 16, split(0, 2))
    ffn("0", ("ffn_w_gu", 0), ("ffn_w_gu", F), "ffn_w_down", (0,))
    add("kv_f", "kv_w", (), 8, [[("w", 2048, 2064)] * 8])
    add("kv_k", "kv_w", (), 8, split(0, 2))
    add("kv_v", "kv_w", (), 8, split(1024, 2))
    add("q", "b_w_qg", (0,), 8, split(0, 1))
    add("gate", "b_w_qg", (0,), 8, split(1024, 1))
    add("q1", "b_w_qg", (0,), 8, split(512, 1))
    add("gate1", "b_w_qg", (0,), 8, split(1536, 1))
    add("o", "b_w_o", (0,), 8, split(0, 2))
    ffn("1", ("ffn_w_gu", 0), ("ffn_w_gu", F), "ffn_w_down", (1,))
    ffn("2", ("ffn_wg_2", 0), ("ffn_wu_2", 0), "ffn_wd_2", (0, 0))
    add("idx", "even_w_in_2", (0,), 8,
        [[("w", 3072, 3328)] + [("w", 3328, 3360)] * 4 + [("w", 3360, 3368), ("zero", 120)]])
    add("aqkv", "even_w_in_2", (0,), 8, split(0, 3))
    add("bqkv", "even_w_in_2", (0,), 8, split(1536, 3))
    add("even_out", "even_w_out_2", (0,), 8, split(0, 2))
    ffn("3", ("ffn_wg_2", 0), ("ffn_wu_2", 0), "ffn_wd_2", (0, 1))
    ffn("4", ("ffn_wg_2", 0), ("ffn_wu_2", 0), "ffn_wd_2", (1, 0))
    add("odd", "odd_w_in_2", (0,), 8, [cols(1024 * i + 512 * g) for g in range(2) for i in range(3)])
    add("odd_out", "odd_w_out_2", (0,), 8, split(0, 2))
    ffn("5", ("ffn_wg_2", 0), ("ffn_wu_2", 0), "ffn_wd_2", (1, 1))
    return out


def width(parts):
    return sum(p[1] if p[0] == "zero" else p[2] - p[1] for _, _, g in parts for p in g)


def k_pieces(kt):
    n = -(-kt // 4)
    base, more = divmod(kt, n)
    out, at = [], 0
    for i in range(n):
        k = base + (i < more)
        out.append((at, k))
        at += k
    return out


def stream():
    main = []
    for name, kt, groups in projections():
        for gi, parts in enumerate(groups):
            parts = list(parts)
            for k0, k in k_pieces(kt) if width(parts) > 128 else [(0, kt)]:
                main.append(("mm", parts, k0, k, width(parts), (name, gi)))
    def piece(src, lead, c, at):
        return ("ada", [(src, lead, cols(256 * c, 256))], 0, 8, 256, at + c)

    ada = [piece("ada_w", (0,), c, 0) for c in range(24)]
    ada += [piece("kv_ada_w", (), c, 48) for c in range(8)]
    ada += [piece("ada_w", (1,), c, 24) for c in range(24)]
    items = [ada[4], ada[0], ada[5], ada[1], main[0], ada[6], ada[2], ada[7], ada[3], main[1]]
    ada, main = ada[8:], main[2:]
    marks = [(0, 0), (4, 0), (22, 12), (56, 32), (74, 44), (100, 48)]
    given = 0
    for i, m in enumerate(main):
        items.append(m)
        for (a0, b0), (a1, b1) in zip(marks, marks[1:]):
            if a0 <= i < a1 and given < b0 + -(-(i + 1 - a0) * (b1 - b0) // (a1 - a0)):
                items.append(ada.pop(0))
                given += 1
    assert not ada
    out, off = [], 0
    for kind, parts, k0, k, n, tag in items:
        out.append((kind, off, parts, k0, k, n, tag))
        off += 128 * k * n
    return out, off



COLS = [("ada_b", 96), ("kv_ada_b", 16), ("pre_mix_g", 16), ("post_mix_g", 16),
        ("pre_ffn_g", 16), ("post_ffn_g", 16), ("kv_norm_g", 8), ("a_b_u", 16), ("a_ln_g", 16),
        ("a_ln_b", 16), ("norm_g", 96), ("subln", 1), ("q_norm", 1), ("k_norm", 1), ("b_f", 1), ("lam", 4)]
COL, NCOL = {}, 0
for _n, _w in COLS:
    COL[_n] = NCOL
    NCOL += _w

CSTS = [("ident", 128), ("bd64", 128), ("rot64", 128), ("rot32", 128), ("cos64", 256),
        ("sin64", 256), ("cos32", 256), ("sin32", 256), ("causal", 256), ("chunk", 256), ("tri", 128), ("forget", 10)]
CST, NCST = {}, 0
for _n, _w in CSTS:
    CST[_n] = (NCST, _w)
    NCST += _w


def constants():
    p = np.arange(128)

    def rot(d):
        m = np.zeros((128, 128), np.float32)
        for i in range(128):
            low = i % d < d // 2
            m[i + d // 2 if low else i - d // 2, i] = -1.0 if low else 1.0
        return m

    def rope(d):
        inv = np.float32(10000.0) ** (-np.arange(0, d, 2, dtype=np.float32) / np.float32(d))
        ang = np.arange(T, dtype=np.float32)[None, :] * inv.astype(np.float32)[:, None]
        rows = p % (d // 2)
        return np.cos(ang).astype(np.float32)[rows], np.sin(ang).astype(np.float32)[rows]

    causal = np.where(p[None, :] <= p[:, None], 0.0, -BIG)
    chunk = np.where(p[None, :] // 64 <= p[:, None] // 64, 0.0, -BIG)
    z = np.zeros((128, 128))
    forget = np.zeros((128, 10))
    forget[:, 0] = p % 32 < 16
    forget[:, 1] = p % 32 >= 16
    for j in range(4):
        for g in range(4):
            forget[32 * g + 16 + 4 * j + g, 2 + j] = -1.0
            forget[32 * g + 4 * j + g, 6 + j] = 1.0
    made = {"ident": np.eye(128),
            "bd64": (p[:, None] // 64 == p[None, :] // 64), "rot64": rot(64), "rot32": rot(32),
            "cos64": rope(64)[0], "sin64": rope(64)[1], "cos32": rope(32)[0], "sin32": rope(32)[1],
            "causal": np.concatenate([z, causal], 1), "chunk": np.concatenate([z, chunk], 1),
            "tri": (p[None, :] >= p[:, None]), "forget": forget}
    return np.concatenate([np.asarray(made[n], np.float32) for n, _ in CSTS], axis=1)



class Engine:
    def __init__(self, name, sem):
        self.name, self.sem = name, sem
        self.n = 0
        self.queue = []
        self.waited = {}

    def wait(self, tokens):
        need = {}
        stack = [tokens]
        while stack:
            t = stack.pop()
            if t is None:
                continue
            if isinstance(t, list):
                stack.extend(t)
                continue
            s, v = t
            if v > need.get(s, 0):
                need[s] = v
        for s, v in need.items():
            if v > self.waited.get(s, 0):
                self.waited[s] = v
                self.queue.append(("wait", s, v))

    def op(self, fn, after=(), sig=True):
        self.wait(list(after))
        if not sig:
            self.queue.append(("op", fn, None, 0))
            return None
        self.n += 1
        self.queue.append(("op", fn, self.sem, 1))
        return (self.sem, self.n)

    def dma(self, fn, slot, after=()):
        self.wait(list(after))
        slot.count += 16
        self.queue.append(("op", fn, slot.sem, 16))
        return (slot.sem, slot.count)

    def play(self, eng):
        for x in self.queue:
            if x[0] == "wait":
                eng.wait_ge(x[1], x[2])
            else:
                ins = x[1](eng)
                if x[2] is not None:
                    ins.then_inc(x[2], x[3])


class Slot:

    def __init__(self, ap, sem=None):
        self.ap, self.sem, self.count, self.free = ap, sem, 0, []


class Ring:
    def __init__(self, slots):
        self.slots, self.i = slots, 0

    def take(self):
        s = self.slots[self.i % len(self.slots)]
        self.i += 1
        return s


def build(nc, c_d, w_d, col_d, cst_d, x_d, row_d, bs_d, ws_d, rel_d, out_d):
    ctx = ExitStack()
    with ctx:
        def sem(name):
            return ctx.enter_context(nc.semaphore(name))

        base = nc.sbuf_base
        total = (nc.sbuf_usable_end - base) // 32 * 32 - 32
        ctx.enter_context(nc.sbuf_tensor("arena", [128, total // 4], F32))
        base = (base + 31) // 32 * 32
        at = [0]

        def place(name, shape, dt, off):
            return nc.alloc_sbuf_tensor_at(name, shape, dt, offset=base + off)

        def area(nbytes):
            off = at[0]
            at[0] += (nbytes + 31) // 32 * 32
            assert at[0] <= total, (at[0], total)
            return off

        def sb(name, shape, dt=F32):
            n = 4
            for s in shape[1:]:
                n *= s
            return place(name, shape, dt, area(n))

        raw = [Slot(sb(f"raw{i}", [128, MAXC]), sem(f"s_raw{i}")) for i in range(NRAW)]
        whr = [Slot(sb(f"wh{i}", [128, MAXC], F32R)) for i in range(NW)]
        wlr = [Slot(sb(f"wl{i}", [128, MAXC], F32R)) for i in range(NW)]
        x = sb("x", [128, 8, T])
        hh = Slot(sb("hh", [128, 8, T], F32R))
        hl = Slot(sb("hl", [128, 8, T], F32R))
        ta = Ring([Slot(sb(f"ta{i}", [128, 4, T])) for i in range(2)])
        tb = Ring([Slot(sb(f"tb{i}", [128, 4, T])) for i in range(2)])
        big = area(2 * 22 * T * 4)
        hidh = Slot(place("hidh", [128, 22, T], F32R, big))
        hidl = Slot(place("hidl", [128, 22, T], F32R, big + 22 * T * 4))
        side = area(16384)
        cst = sb("cst", [128, NCST])
        col = sb("col", [128, NCOL])
        mod = sb("mod", [128, 112])
        cact = sb("cact", [128, D])
        ones = sb("ones", [128, 128])[:, :]
        der = sb("der", [128, 10, 8])
        eps = sb("eps", [128, 1])
        root = sb("root", [128, T])
        rsx = Slot(sb("rsx", [128, T]))
        rsy = Slot(sb("rsy", [128, T]))
        e2 = Slot(sb("e2", [1, T]))
        eps2 = sb("eps2", [1, 1])
        warm = sb("warm", [1, 1])
        small = sb("small", [128, 64])

        def C(name):
            o, w = CST[name]
            return cst[:, o:o + w]

        def colat(name, i=0):
            return col[:, COL[name] + i:COL[name] + i + 1]

        ident = C("ident")

        pst = [ctx.enter_context(nc.psum_tensor(f"pp{i}", [128, 2, 512], F32)) for i in range(4)]
        banks = [Slot(pst[i // 2][:, i % 2, :]) for i in range(8)]

        class Pair:
            def __init__(self, i):
                self.t = pst[i]
                self.b = (banks[2 * i], banks[2 * i + 1])
                self.tiles = self.t[:, :, :].rearrange("p b (m t) -> p (b m) t", t=T)
                self.rows = self.t[:, :, :]

            def free(self):
                return [self.b[0].free, self.b[1].free]

            def release(self, tok):
                self.b[0].free = [tok]
                self.b[1].free = [tok]

        pairs = Ring([Pair(0), Pair(1), Pair(2)])
        misc = Ring([banks[6], banks[7]])
        turns = Ring([banks[4], banks[5]])

        sp = Engine("sp", sem("s_sp"))
        act = Engine("act", sem("s_act"))
        dve = Engine("dve", sem("s_dve"))
        pe = Engine("pe", sem("s_pe"))
        pool = Engine("pool", sem("s_pool"))

        load_slot = {}

        def load(name, dst, src, after=(), queue=None):
            s = Slot(None, sem("s_ld_" + name))
            load_slot[name] = (queue or pool).dma(lambda e: e.dma_start(dst, src), s, after)
            return load_slot[name]

        t_ones = pool.op(lambda e: e.memset(ones, 1.0))
        v = place("v", [128, 2, 2048], F32, big)
        wsT = place("wsT", [128, 16, 128], F32, big + 16384)
        bsb = place("bsb", [128, 16, 128], F32, big + 24576)
        binr = place("binr", [128, 2048], F32, big + 32768)
        pool.op(lambda e: e.memset(eps2[:, :], D * EPS * EPS))
        t_eps = pool.op(lambda e: e.memset(eps[:, :], EPS))

        items, _ = stream()
        state = {"dma": 0, "prep": 0, "use": 0, "used": 0, "ahead": 3, "small": misc}
        landed, ready, freed = {}, {}, set()

        def start_loads(upto):
            while state["dma"] < min(upto, len(items)):
                i = state["dma"]
                if i >= NRAW and i - NRAW not in freed:
                    return
                kind, off, parts, k0, kt, n, tag = items[i]
                s = raw[i % NRAW]
                src = w_d[off:off + 128 * kt * n].rearrange("(p f) -> p f", p=128)
                landed[i] = sp.dma(lambda e, d=s.ap[:, 0:kt * n], src=src: e.dma_start(d, src), s, s.free)
                state["dma"] += 1

        mm_index = {}
        count = 0
        for i, it in enumerate(items):
            if it[0] == "mm":
                mm_index[i] = count
                count += 1

        def item_steps(i, parts):
            kind, off, _, k0, kt, n, tag = items[i]
            s = raw[i % NRAW]
            if kind == "mm":
                h, l = whr[mm_index[i] % NW], wlr[mm_index[i] % NW]
                w = kt * n // parts
                for q in range(parts):
                    if q:
                        yield
                    c = slice(q * w, q * w + w)
                    th = act.op(lambda e, o=h.ap[:, c], a=s.ap[:, c]: e.activation(o, a, ACT.Copy), [landed[i], h.free])
                    tl = dve.op(lambda e, o=l.ap[:, c], a=s.ap[:, c], b=h.ap[:, c]:
                                e.tensor_tensor(o, a, b, ALU.subtract), [landed[i], th, l.free])
                s.free = [th, tl]
                ready[i] = (th, tl)
                freed.add(i)
                start_loads(i + NRAW + 1)
            else:
                ada_piece(i)

        def prepare(upto):
            while state["prep"] < min(upto, len(items)):
                drain(state.pop("part", None) or item_steps(state["prep"], 1))
                state["prep"] += 1

        def nibble():
            i = state["prep"]
            if "part" not in state:
                if i >= len(items) or i not in landed or (i in mm_index and mm_index[i] - NW >= state["used"]):
                    return
                state["part"] = item_steps(i, 4)
            if next(state["part"], "end") == "end":
                del state["part"]
                state["prep"] += 1

        def drain(steps):
            while True:
                try:
                    next(steps)
                except StopIteration as e:
                    return e.value

        t_c = load("c", cact[:, :], c_d.partition_broadcast(128), queue=sp)
        t_col = load("col", col[:, :], col_d, queue=sp)
        t_x = load("x", x[:, :, :], x_d.rearrange("(k p) t -> p k t", p=128), queue=sp)
        start_loads(NRAW)

        late = [landed[NRAW - 1]]
        t_cst = [load("cst", cst[:, :], cst_d, late), t_ones]
        t_ws = load("ws", wsT[:, :, :], ws_d.rearrange("s (g t) -> s g t", g=16), late)
        t_bin = load("bin", binr[:, :], row_d.partition_broadcast(128), late)
        t_bs = load("bs", bsb[:, :, :].rearrange("p g t -> p (g t)"), bs_d.partition_broadcast(128), late)

        def mm(out, lhsT, rhs, start, stop, after=(), sig=False, **kw):
            return pe.op(lambda e: e.matmul(out, lhsT, rhs, start=start, stop=stop, skip_group_check=True, **kw),
                         after, sig)

        def transpose(out, in_, idn, after=(), sig=False):
            return pe.op(lambda e: e.transpose(out, in_, idn), after, sig)

        def activation(out, in_, func, after=(), **kw):
            return act.op(lambda e: e.activation(out, in_, func, **kw), after)

        def tt(out, a, b, op, after=()):
            return dve.op(lambda e: e.tensor_tensor(out, a, b, op), after)

        def stt(out, a, s, b, op0, op1, after=()):
            return dve.op(lambda e: e.scalar_tensor_tensor(out=out, in0=a, scalar=s, in1=b, op0=op0, op1=op1), after)

        def ts(out, a, s1, s2, op0, op1=None, after=()):
            if op1 is None:
                return dve.op(lambda e: e.tensor_scalar(out, a, s1, s2, op0), after)
            return dve.op(lambda e: e.tensor_scalar(out, a, s1, s2, op0, op1), after)

        t_cact = activation(cact[:, :], cact[:, :], ACT.Silu, [t_c])
        mod_tok = {}

        def ada_piece(i):
            kind, off, parts, k0, kt, n, c = items[i]
            s = raw[i % NRAW]
            for m in range(2):
                w = s.ap[:, 1024 * m:1024 * m + 1024]
                o = mod[:, 2 * c + m:2 * c + m + 1]
                t = dve.op(lambda e, w=w, o=o: e.tensor_tensor_reduce(w, w, cact[:, :], 1.0, 0.0, ALU.mult, ALU.add, o),
                           [landed[i], t_cact])
            s.free = [t]
            o = mod[:, 2 * c:2 * c + 2]
            bias = col[:, COL["ada_b"] + 2 * c:COL["ada_b"] + 2 * c + 2]
            mod_tok[c // 4] = tt(o, o, bias, ALU.add, [t, t_col])
            freed.add(i)
            start_loads(i + NRAW + 1)

        def next_piece(ahead):
            while items[state["use"]][0] == "ada":
                state["use"] += 1
            i = state["use"]
            j, seen = i, 0
            while j < len(items) and seen < ahead:
                seen += items[j][0] == "mm"
                j += 1
            prepare(j)
            state["use"] += 1
            return i

        def first_piece(steps, xtok):
            while None in xtok[0:4]:
                yield
            for _ in range(4):
                next(steps)
                yield
            while None in xtok:
                yield
            return drain(steps)

        def group(*args, **kw):
            return drain(group_steps(*args, **kw))

        def group_steps(name, gi, xh, xl, xtok, mode, between=None, ahead=None, pair=None):
            pair = pair or pairs.take()
            n_done = 0
            while True:
                if between and n_done == 1:
                    between()
                i = next_piece(ahead if ahead and n_done == 0 else state["ahead"])
                n_done += 1
                kind, off, parts, k0, kt, n, tag = items[i]
                assert tag == (name, gi), (tag, name, gi)
                j = mm_index[i]
                last = i + 1 >= len(items) or all(
                    items[q][6] != tag or items[q][0] != "mm" for q in range(i + 1, min(i + 6, len(items))))
                wh = whr[j % NW].ap[:, 0:kt * n].rearrange("p (k n) -> p k n", k=kt)
                wl = wlr[j % NW].ap[:, 0:kt * n].rearrange("p (k n) -> p k n", k=kt)
                th, tl = ready[i]
                nm = n // 128 if mode == "T" else 2
                first = k0 == 0

                def product(m, k, w, xx, after, stop=False, sig=False):
                    wa, xa = w[:, k, :], xx[:, k0 + k, :]
                    if mode == "T":
                        out, lh, rh = pair.tiles[:, m, :], wa[:, m * 128:(m + 1) * 128], xa
                    else:
                        out, lh, rh = pair.rows[:, m, 0:n], xa[:, m * 128:(m + 1) * 128], wa
                    fresh = first and k == 0 and w is wh and xx is xh and (mode == "N" or m % 2 == 0)
                    return mm(out, lh, rh, fresh, stop, after, sig)

                if last:
                    toks = []
                    for m in range(nm):
                        for k in range(kt):
                            xt = xtok[k0 + k]
                            product(m, k, wh, xh, [th, xt[0], pair.free() if first and k == 0 else None])
                            product(m, k, wh, xl, [xt[1]])
                            t = product(m, k, wl, xh, [tl], k == kt - 1, k == kt - 1)
                        toks.append(t)
                        yield
                    whr[j % NW].free = [t, tl]
                    wlr[j % NW].free = [t]
                    state["used"] += 1
                    pair.toks = [toks[min(m | 1, nm - 1)] for m in range(len(toks))]
                    return pair, t
                for k in range(kt):
                    xt = xtok[k0 + k]
                    for m in range(nm):
                        product(m, k, wh, xh, [th, xt[0], pair.free() if first and k == 0 else None])
                    for m in range(nm):
                        product(m, k, wl, xh, [tl])
                    for m in range(nm):
                        t = product(m, k, wh, xl, [xt[1]], sig=(m == nm - 1 and k == kt - 1))
                    yield
                whr[j % NW].free = [t, tl]
                wlr[j % NW].free = [t]
                state["used"] += 1

        def split(dsth, dstl, src, after, waitfree=()):
            th = activation(dsth, src, ACT.Copy, [after, waitfree])
            tl = tt(dstl, src, dsth, ALU.subtract, [th, after])
            return th, tl

        def root_tables():
            activation(warm[:, :], eps[0:1, :], ACT.Sqrt, [t_eps])

        class Stats:

            def __init__(self, dst, extra=None):
                self.b, self.i, self.dst, self.tm, self.todo = misc.take(), 0, dst, None, []
                if extra:
                    row, t = extra
                    self.tm = mm(self.b.ap[:, 0:T], ones[0:1, :], row, True, False, [t, t_ones, self.b.free], sig=True)
                    e2.free = [self.tm]

            def add(self, src, toks, now=True):
                if self.i % 4 == 0:
                    self.a = ta.take()
                sq = self.a.ap[:, self.i % 4, :]
                t = activation(sq, src, ACT.Square, [toks, self.a.free if self.i % 4 == 0 else None])
                self.todo.append((self.i, self.a, sq, t))
                self.i += 1
                if now:
                    self.sum()

            def sum(self):
                for i, a, sq, t in self.todo:
                    self.tm = mm(self.b.ap[:, 0:T], ones, sq, self.tm is None, i == 7,
                                 [t, t_ones, self.b.free if i == 0 else None], sig=True)
                    if i % 4 == 3:
                        a.free = [self.tm]
                self.todo = []

            def done(self):
                t = activation(root[:, :], self.b.ap[:, 0:T], ACT.Sqrt, [self.tm, t_eps, state.get("root")],
                               bias=eps[:, 0:1], scale=1.0 / D)
                self.b.free = [t]
                t = dve.op(lambda e, o=self.dst.ap[:, :]: e.reciprocal(o, root[:, :]), [t, self.dst.free])
                state["root"] = t
                return t

            def times_eps(self):
                t = activation(e2.ap[:, :], self.b.ap[0:1, 0:T], ACT.Identity, [self.tm, t_eps, e2.free],
                               bias=eps2[:, 0:1], scale=EPS)
                self.b.free = [t]
                return (e2.ap[:, :], t)

        def bc4(ap, n=4):
            return ap.unsqueeze(1).to_broadcast([128, n, ap.shape[-1]])

        x_tok = [t_x] * 8

        def make_h(acols, bcols, t_rs, after, tiles=range(8)):
            toks = []
            for m in tiles:
                if m % 4 == 0 or m == tiles[0]:
                    s = tb.take()
                o = s.ap[:, m % 4, :]
                t = stt(o, x[:, m, :], acols[:, m:m + 1], rsx.ap[:, :], ALU.mult, ALU.mult,
                        [x_tok[m], t_rs, after, s.free if m % 4 == 0 else None])
                th = activation(hh.ap[:, m, :], o, ACT.Identity, [t, hh.free, after], bias=bcols[:, m:m + 1])
                if m != tiles[0]:
                    toks.append((low[2], stt(*low[0], ALU.add, ALU.subtract, low[1])))
                    low[3].free = [toks[-1][1]]
                low = ((hl.ap[:, m, :], o, bcols[:, m:m + 1], hh.ap[:, m, :]), [th, hl.free], th, s)
            tl = stt(*low[0], ALU.add, ALU.subtract, low[1])
            toks.append((th, tl))
            s.free = [tl]
            rsx.free = [tl]
            return toks

        def residual(outs, scols, after, extra=None, nxt=None, more=True):
            y = Stats(rsy, extra)
            for half, (p, _) in enumerate(outs):
                for m in range(4):
                    y.add(p.tiles[:, m, :], p.toks[m])
            t_rs = y.done()
            nx = Stats(rsx) if more else None
            toks = []
            slots = [tb.take(), tb.take()]

            def scaled_y(k):
                (p, _), s, m = outs[k // 4], slots[k // 4], k % 4
                t = stt(s.ap[:, m, :], p.tiles[:, m, :], scols[:, k:k + 1], rsy.ap[:, :],
                        ALU.mult, ALU.mult, [p.toks[m], t_rs, after, s.free if m == 0 else None])
                if m == 3:
                    p.release(t)
                return t

            t = scaled_y(0)
            for k in range(8):
                t_y = t
                if k < 7:
                    t = scaled_y(k + 1)
                s = slots[k // 4]
                x_tok[k] = tt(x[:, k, :], x[:, k, :], s.ap[:, k % 4, :], ALU.add, [t_y, x_tok[k]])
                if nxt is not None:
                    th = activation(hh.ap[:, k, :], x[:, k, :], ACT.Copy, [x_tok[k], hh.free], scale=nxt[:, k:k + 1])
                    toks.append(th)
                    if k:
                        toks[k - 1] = (toks[k - 1], low_part(nxt, k - 1, toks[k - 1]))
                if more:
                    nx.add(x[:, k, :], [x_tok[k]], nxt is None)
                if k % 4 == 3:
                    s.free = [x_tok[k]]
            rsy.free = [t]
            if nxt is not None:
                toks[7] = (toks[7], low_part(nxt, 7, toks[7]))
            state["x"] = nx.done() if more and nxt is None else nx
            return toks

        def late_stats():
            nx = state["x"]
            nx.sum()
            state["x"] = nx.done()
            state["e2"] = nx.times_eps()

        def low_part(nxt, k, th):
            return stt(hl.ap[:, k, :], x[:, k, :], nxt[:, k:k + 1], hh.ap[:, k, :], ALU.mult, ALU.subtract,
                       [th, hl.free])

        def both(name, xh, xl, xtok, mode="T"):
            root_tables()
            return [group(name, g, xh, xl, xtok, mode) for g in range(2)]

        def modcols(sec):
            return mod[:, 8 * sec:8 * sec + 8]

        def pcols(name, i):
            return col[:, COL[name] + 8 * i:COL[name] + 8 * i + 8]

        ndr = [0]

        def scaled(gains, sec, add_one):
            o = der[:, ndr[0] % 10, :]
            ndr[0] += 1
            t = stt(o, modcols(sec), 1.0 if add_one else 0.0, gains, ALU.add, ALU.mult, [mod_tok[sec], t_col])
            return o, t

        def swiglu(tag, toks, late=False):
            name = "gu" + tag
            ht = []
            hidh.free, hidl.free = [hidh.free], [hidl.free]
            for i in range(6):
                nt = 4 if i < 5 else 2
                if i < 5:
                    pg, tg = group(name, 2 * i, hh.ap, hl.ap, toks, "T", late_stats if late and i == 0 else None)
                    g_ps = pg.tiles[:, :, :]
                else:
                    pg, tg = group(name, 10, hh.ap, hl.ap, toks, "T")
                    g_ps = pg.tiles[:, 0:2, :]
                a = ta.take()
                if late:
                    t = tt(a.ap[:, 0:nt, :], g_ps, bc4(rsx.ap[:, :], nt), ALU.mult, [tg, a.free, state["x"]])
                    if i < 5:
                        pg.release(t)
                    rsx.free = [t]
                    t = activation(a.ap[:, 0:nt, :], a.ap[:, 0:nt, :], ACT.Silu, [t])
                else:
                    t = activation(a.ap[:, 0:nt, :], g_ps, ACT.Silu, [tg, a.free])
                    if i < 5:
                        pg.release(t)
                if i < 5:
                    pu, tu = group(name, 2 * i + 1, hh.ap, hl.ap, toks, "T")
                    u_ps = pu.tiles[:, :, :]
                else:
                    pu, tu = pg, tg
                    u_ps = pg.tiles[:, 2:4, :]
                s = tb.take()
                t = tt(s.ap[:, 0:nt, :], a.ap[:, 0:nt, :], u_ps, ALU.mult, [t, tu, s.free])
                pu.release(t)
                a.free = [t]
                th, tl = split(hidh.ap[:, 4 * i:4 * i + nt, :], hidl.ap[:, 4 * i:4 * i + nt, :],
                               s.ap[:, 0:nt, :], t, [hidh.free, hidl.free])
                s.free = [th, tl]
                ht += [(th, tl)] * nt
            hh.free = hl.free = [tu]
            outs = both("dn" + tag, hidh.ap, hidl.ap, ht)
            hidh.free = hidl.free = [outs[1][1]]
            return outs

        root_tables()
        sx = Stats(rsx)
        for k in range(8):
            sx.add(x[:, k, :], [t_x])
        htok = []

        def first_h(j):
            c = slice(2 * j, 2 * j + 2)
            o = der[:, 0, c]
            t = stt(o, modcols(1)[:, c], 1.0, pcols("pre_mix_g", 0)[:, c], ALU.add, ALU.mult, [mod_tok[0], mod_tok[1]])
            htok.extend(make_h(der[:, 0, :], modcols(0), t_rs, [t], range(2 * j, 2 * j + 2)))

        def second_half():
            prepare(9)
            first_h(2)
            first_h(3)

        prepare(2)
        t_rs = sx.done()
        prepare(4)
        first_h(0)
        first_h(1)
        ndr[0] = 1

        bst = small[:, 0:48].rearrange("p (a g s) -> p a g s", a=2, g=4)
        mv = small[:, 48:52].rearrange("p (a s) -> p a s", a=2)
        rstd = small[:, 52:54]
        bias_tok = []

        def spatial_bias():
            wsf = wsT[:, :, :].rearrange("p g t -> p (g t)")
            for q in range(2 * len(bias_tok), 2 * len(bias_tok) + 2):
                b = misc.take()
                t = mm(b.ap[:, :], ones, wsf[:, 512 * q:512 * q + 512], True, True, [t_tri, t_ones, b.free], sig=True)
                for g in range(4):
                    gg = 4 * q + g
                    t = stt(bsb[:, gg, :], b.ap[:, 128 * g:128 * g + 128], colat("a_ln_b", gg), bsb[:, gg, :],
                            ALU.mult, ALU.add, [t, t_bs, t_col])
                b.free = [t]
            bias_tok.append(t)

        v_tok = []
        for g in range(4):
            p, t = group("a_v", g, hh.ap, hl.ap, htok, "N",
                         *((second_half, 1) if g == 0 else (spatial_bias,) if g in (2, 3) else ()))
            s = tb.take()
            bias = binr[:, 512 * g:512 * g + 512]
            t = tt(s.ap[:, :, :].rearrange("p (a b) t -> p a (b t)", a=2), p.rows, bc4(bias, 2), ALU.add,
                   [t, t_bin, s.free])
            p.release(t)
            vg = v[:, :, 512 * g:512 * g + 512]
            t = activation(vg, s.ap[:, :, :].rearrange("p (a b) t -> p a (b t)", a=2), ACT.Gelu_apprx_tanh, [t])
            s.free = [t]
            if g == 0:
                t_tri = tt(wsT[:, :, :], wsT[:, :, :], bc4(C("tri"), 16), ALU.mult, [t_ws, t_cst])
            for a in range(2):
                t = dve.op(lambda e, o=bst[:, a, g, :], i=v[:, a, 512 * g:512 * g + 512]: e.bn_stats(o, i), [t])
        for a in range(2):
            t = dve.op(lambda e, o=mv[:, a, :], i=bst[:, a, :, :].rearrange("p g s -> p (g s)"): e.bn_aggr(o, i), [t])
        t = activation(rstd, mv[:, :, 1], ACT.Sqrt, [t, t_eps], bias=eps[:, 0:1])
        t = dve.op(lambda e: e.reciprocal(rstd, rstd), [t])
        for a in range(2):
            t_v = ts(v[:, a, :], v[:, a, :], mv[:, a, 0:1], rstd[:, a:a + 1], ALU.subtract, ALU.mult, [t])

        spt = place("spt", [128, 16, T], F32, side)

        def gelu_u(g):
            p, tg = group("a_u", g, hh.ap, hl.ap, htok, "T")
            a = ta.take()
            for m in range(4):
                t = activation(a.ap[:, m, :], p.tiles[:, m, :], ACT.Gelu_apprx_tanh, [tg, a.free, t_col],
                               bias=colat("a_b_u", 4 * g + m))
            p.release(t)
            return a, t, tg

        us = [gelu_u(0), gelu_u(1)]
        sp_tok = []
        for q in range(4):
            p = pairs.take()
            for g in range(4):
                for n in range(2):
                    t = mm(p.tiles[:, g, 128 * n:128 * n + 128], v[:, n, 128 * (4 * q + g):128 * (4 * q + g) + 128],
                           wsT[:, 4 * q + g, :], g % 2 == 0 and n == 0, True,
                           [t_v, t_tri, p.free()], sig=(g == 3 and n == 1))
            for g in range(4):
                gg = 4 * q + g
                t2 = stt(spt[:, gg, :].rearrange("p (n t) -> p n t", n=2),
                         p.tiles[:, g, :].rearrange("p (n t) -> p n t", n=2), colat("a_ln_g", gg),
                         bc4(bsb[:, gg, :], 2), ALU.mult, ALU.add, [t, bias_tok])
            p.release(t2)
            sp_tok.append(t2)
            t_sp_pe = t
        hidh.free = [t_sp_pe, sp_tok[-1]]
        hidl.free = [t_sp_pe, sp_tok[-1]]
        ht = []
        for g in range(4):
            a, t, tg = us[g] if g < 2 else gelu_u(g)
            s = tb.take()
            t = tt(s.ap[:, :, :], a.ap[:, :, :], spt[:, 4 * g:4 * g + 4, :], ALU.mult, [t, sp_tok[g], s.free])
            a.free = [t]
            th, tl = split(hidh.ap[:, 4 * g:4 * g + 4, :], hidl.ap[:, 4 * g:4 * g + 4, :], s.ap[:, :, :], t,
                           [hidh.free, hidl.free])
            s.free = [th, tl]
            ht += [(th, tl)] * 4
        t_side = t
        hh.free = hl.free = [tg]
        outs = both("a_out", hidh.ap, hidl.ap, ht)
        hidh.free = hidl.free = [outs[1][1]]

        def after_mix(layer, outs):
            s1, t1 = scaled(pcols("post_mix_g", layer), 6 * layer + 2, False)
            a1, t2 = scaled(pcols("pre_ffn_g", layer), 6 * layer + 4, True)
            residual(outs, s1, [t1])
            return make_h(a1, modcols(6 * layer + 3), state["x"], [t2, mod_tok[6 * layer + 3]])

        htok = after_mix(0, outs)
        outs = swiglu("0", htok)
        s1, t1 = scaled(pcols("post_ffn_g", 0), 5, False)
        a1, t2 = scaled(pcols("kv_norm_g", 0), 13, True)
        residual(outs, s1, [t1])

        t_rs = state["x"]
        htok = make_h(a1, modcols(12), t_rs, [t2, mod_tok[12]])

        Sb = Ring([Slot(place(f"Sb{i}", [128, T], F32, side + 1024 * i)) for i in range(4)])
        Pb = Ring([Slot(place(f"Pb{i}", [128, T], F32, side + 4096 + 1024 * i)) for i in range(6)])
        PT = Ring([Slot(place(f"PT{i}", [128, T], F32, side + 10240 + 1024 * i)) for i in range(4)])
        st = place("st", [128, 64, 4], F32, side + 14336)
        dT = place("dT", [128, T], F32, big + 32768)
        dL = place("dL", [128, T], F32, big + 33792)
        dR = place("dR", [128, 4, T], F32, big + 38912)
        side_free = [t_side, sp_tok]
        for ring in (Sb, Pb, PT):
            for s in ring.slots:
                s.free = [side_free]
        qT = place("qT", [128, 8, T], F32, big)
        kT = place("kT", [128, 8, T], F32, big + 8192)
        vv = place("vv", [128, 2, 1024], F32, big + 16384)
        gT = place("gT", [128, 8, T], F32, big + 24576)
        lf = [place(f"lf{i}", [128, T], F32, big + 34816 + 1024 * i) for i in range(3)]
        big_free = hidh.free

        p, t = group("kv_f", 0, hh.ap, hl.ap, htok, "T")
        t = ts(lf[0][:, :], p.tiles[:, 0, :], colat("b_f"), None, ALU.add, after=[t, big_free, t_col])
        p.release(t)
        t2 = activation(lf[1][:, :], lf[0][:, :], ACT.Abs, [t])
        t2 = activation(lf[1][:, :], lf[1][:, :], ACT.Exp, [t2], scale=-1.0)
        t2 = activation(lf[1][:, :], lf[1][:, :], ACT.Ln, [t2], bias=1.0)
        t = stt(lf[2][:, :], lf[0][:, :], 0.0, lf[1][:, :], ALU.min, ALU.subtract, [t, t2])
        t = dve.op(lambda e: e.tensor_tensor_scan(dT[:, :], ones[:, 0:1].to_broadcast([128, T]), lf[2][:, :], 0.0,
                                                  ALU.mult, ALU.add), [t])
        fc = C("forget")
        t_d = t = ts(dL[:, :], dT[:, :], fc[:, 0:1], fc[:, 1:2], ALU.mult, ALU.add, after=[t, t_cst])
        for j in range(4):
            t_d = ts(dR[:, j, :], dT[:, :], fc[:, 2 + j:3 + j], fc[:, 6 + j:7 + j], ALU.mult, ALU.add, after=[t])

        def head_norm(p, t0, gcol, dst, toks):
            a = ta.take()
            ts_ = [activation(a.ap[:, 2 * n:2 * n + 2, :], p.tiles[:, 2 * n:2 * n + 2, :], ACT.Square, [t0, a.free])
                   for n in range(2)]

            def rest():
                s = tb.take()
                for n in range(2):
                    b = state["small"].take()
                    for m in range(2):
                        tm = mm(b.ap[:, 256 * m:256 * m + 256], C("bd64"), a.ap[:, 2 * n + m, :], m == 0, True,
                                [ts_[n], t_cst, b.free], sig=(m == 1))
                    b.free = [activation(s.ap[:, 2 * n:2 * n + 2, :], b.ap.rearrange("p (m t) -> p m t", m=2), ACT.Ln,
                                         [tm, s.free], bias=eps[:, 0:1], scale=1.0 / 64)]
                t = activation(s.ap[:, :, :], s.ap[:, :, :], ACT.Exp, [b.free], scale=-0.5)
                t = stt(dst, p.tiles, gcol, s.ap[:, :, :], ALU.mult, ALU.mult, [t, t0, big_free, t_col])
                a.free = [tm]
                p.release(t)
                s.free = [t]
                toks.append(t)
            return rest

        qg = small[:, 62:63]
        t_qg = ts(qg, colat("q_norm"), 0.125, None, ALU.mult, after=[t_col])
        qk_tok = [t_qg]
        rest = None
        for g in range(2):
            p, t = group("kv_k", g, hh.ap, hl.ap, htok, "T", rest)
            rest = head_norm(p, t, colat("k_norm"), kT[:, 4 * g:4 * g + 4, :], qk_tok)
        for g in range(2):
            p, t = group("kv_v", g, hh.ap, hl.ap, htok, "N", rest)
            rest = None
            hh.free = hl.free = [t]
            t = activation(vv[:, :, 512 * g:512 * g + 512], p.rows, ACT.Copy, [t, big_free])
            p.release(t)
            t_vv = t
        a1, t1 = scaled(pcols("pre_mix_g", 1), 7, True)
        htok = make_h(a1, modcols(6), t_rs, [t1, mod_tok[6]])
        p, t = group("q", 0, hh.ap, hl.ap, htok, "T")
        rest = head_norm(p, t, qg, qT[:, 0:4, :], qk_tok)

        def gate(g, p, t):
            t_gate[g] = activation(gT[:, 4 * g:4 * g + 4, :], p.tiles, ACT.Sigmoid, [t, big_free])
            p.release(t_gate[g])

        t_gate = {}
        p, t = group("gate", 0, hh.ap, hl.ap, htok, "T", rest)
        gate(0, p, t)
        ho = [None] * 8
        waiting = []

        def split_steps(tile, src, t):
            th = activation(hh.ap[:, tile, :], src, ACT.Copy, [t, hh.free])
            yield
            ho[tile] = (th, tt(hl.ap[:, tile, :], src, hh.ap[:, tile, :], ALU.subtract, [th, t, hl.free]))

        def split_waiting(src):
            for tile, t in waiting:
                drain(split_steps(tile, src[:, tile, :], t))
            del waiting[:]

        def fox_fill():
            P = pairs.slots[0]
            p, t = yield from group_steps("q1", 0, hh.ap, hl.ap, htok, "T", pair=P)
            rest = head_norm(p, t, qg, qT[:, 4:8, :], qk_tok)
            yield
            rest()
            state["second"] = True
            p, t = yield from group_steps("gate1", 0, hh.ap, hl.ap, htok, "T", pair=P)
            gate(1, p, t)
            hh.free = hl.free = [t]
            split_waiting(gT)
            state["own"] = True
            return (yield from first_piece(group_steps("o", 0, hh.ap, hl.ap, ho, "T", pair=P), ho))

        nst = [0]

        def attention(units, finish, fill, rate, keep=False):
            S_r = Ring([banks[2], banks[3]])
            T_r = state["small"] = turns
            state["ahead"] = 1
            O_r = Ring([banks[6], banks[7]])
            live = [dict(u) for u in units]
            later = []
            o_bank = {}

            def scores(u):
                nk = u["nk"]
                u["s"] = []
                for terms in u["subs"]:
                    b = S_r.take()
                    for n, (c0, c1, l, r) in enumerate(terms):
                        t = mm(b.ap[:, c0:c1], l, r, n == 0, n == len(terms) - 1,
                               [u["after"], b.free] if n == 0 else (), sig=(n == len(terms) - 1))
                    sbuf = Sb.take()
                    k = nst[0] % 64
                    nst[0] += 1
                    if u["mask"] is None:
                        t = dve.op(lambda e, o=sbuf.ap[:, 0:nk], i=b.ap[:, 0:nk], m=st[:, k, 0:1]:
                                   e.tensor_scalar(o, i, -1.0, None, ALU.mult, ALU.min, accum_out=m),
                                   [t, sbuf.free])
                    else:
                        t = dve.op(lambda e, o=sbuf.ap[:, 0:nk], i=b.ap[:, 0:nk], m=st[:, k, 0:1], mk=u["mask"]:
                                   e.tensor_tensor_reduce(o, i, mk, -1.0, 3.4e38, ALU.add, ALU.min, m),
                                   [t, sbuf.free, t_cst, u["after"]])
                    b.free = [t]
                    u["s"].append((sbuf, k, t))

            def exps(u):
                nk = u["nk"]
                u["p"] = []
                for sbuf, k, t in u["s"]:
                    pb = Pb.take()
                    t = activation(pb.ap[:, 0:nk], sbuf.ap[:, 0:nk], ACT.Exp, [t, pb.free], scale=-1.0,
                                   bias=st[:, k, 0:1], accum_out=st[:, k, 1:2])
                    sbuf.free = [t]
                    u["p"].append((pb, k, t))

            def normalise(u):
                nk = u["nk"]
                rt = []
                for pb, k, t in u["p"]:
                    rt.append(dve.op(lambda e, o=st[:, k, 2:3], i=st[:, k, 1:2]: e.reciprocal(o, i), [t]))
                if len(rt) == 1:
                    pb, k, t = u["p"][0]
                    u["w"] = (pb, ts(pb.ap[:, 0:nk], pb.ap[:, 0:nk], st[:, k, 2:3], None, ALU.mult, after=[rt[0]]))
                else:
                    (p0, k0, _), (p1, k1, _) = u["p"]
                    t = ts(p1.ap[:, 0:nk], p1.ap[:, 0:nk], st[:, k1, 2:3], nlam, ALU.mult, ALU.mult,
                           after=[rt[1], t_lam])
                    t = stt(p0.ap[:, 0:nk], p0.ap[:, 0:nk], st[:, k0, 2:3], p1.ap[:, 0:nk], ALU.mult, ALU.add,
                            [t, rt[0]])
                    p1.free = [t]
                    u["w"] = (p0, t)

            def turn(u):
                nk = u["nk"]
                pb, t = u["w"]
                b = T_r.take()
                for kb in range(nk // 128):
                    tt_ = transpose(b.ap[:, 128 * kb:128 * kb + 128], pb.ap[:, 128 * kb:128 * kb + 128], ident,
                                    [t, b.free], sig=(kb == nk // 128 - 1))
                pb.free = [tt_]
                pt = PT.take()
                t = activation(pt.ap[:, 0:nk], b.ap[:, 0:nk], ACT.Copy, [tt_, pt.free])
                b.free = [t]
                u["pt"] = (pt, t)

            def values(u):
                pt, t = u["pt"]
                if u["tile"] not in o_bank:
                    o_bank[u["tile"]] = O_r.take()
                b = o_bank[u["tile"]]
                out = b.ap[u["rows"], 128 * u["qb"]:128 * u["qb"] + 128]
                n = u["nk"] // 128
                for kb in range(n):
                    tv = mm(out, u["v"](kb), pt.ap[:, 128 * kb:128 * kb + 128], kb == 0, kb == n - 1,
                            [t, u["vtok"], b.free], sig=(kb == n - 1))
                pt.free = [tv]
                if u["last"]:
                    g = finish(u["tile"], b, tv)
                    next(g)
                    later.append(g)

            for i in range(len(live) + 5):
                for g in later[:]:
                    if next(g, "end") == "end":
                        later.remove(g)
                for stage, lag in ((turn, 4), (values, 5), (normalise, 2), (exps, 1), (scores, 0)):
                    if 0 <= i - lag < len(live):
                        u = live[i - lag]
                        while lag in u.get("need", {}) and u["need"][lag] not in state:
                            next(fill)
                        stage(u)
                for _ in range(rate(i)):
                    nibble()
                    if next(fill, "end") == "end":
                        break
                nibble()
            for g in later:
                drain(g)
            state["small"] = misc
            state["ahead"] = 3
            pairs.i = 1
            if not keep:
                drain(fill)

        def plain_units(qq, kk, vt, mask, after, extra=None, heads=16):
            us = []
            for h in range(heads):
                for qb in range(2):
                    nk = 128 * (qb + 1)
                    r = slice(64 * (h % 2), 64 * (h % 2) + 64)
                    terms = [(0, nk, qq[r, h // 2, 128 * qb:128 * qb + 128], kk[r, h // 2, 0:nk])]
                    if extra:
                        terms += extra(h, qb, nk)
                    us.append(dict(subs=[terms], nk=nk, mask=mask(qb), after=after, rows=r, tile=h // 2, qb=qb,
                                   v=(lambda kb, h=h: vt[:, kb, 64 * h:64 * h + 64]), vtok=after,
                                   last=(h % 2 == 1 and qb == 1)))
            return us

        def cmask(name):
            m = C(name)
            return lambda qb: m[:, 128:256] if qb == 0 else m

        def forget_terms(h, qb, nk):
            r = slice(32 * (h % 4), 32 * (h % 4) + 32)
            return [(0, nk, dL[r, 128 * qb:128 * qb + 128], dR[r, h // 4, 0:nk])]

        def finish_fox(tile, b, t):
            yield
            o = gT[:, tile, :]
            t = tt(o, b.ap[:, 0:T], o, ALU.mult, [t, t_gate[tile // 4]])
            b.free = [t]
            if "own" in state:
                yield
                yield from split_steps(tile, o, t)
            else:
                waiting.append((tile, t))

        us = plain_units(qT, kT, vv, cmask("causal"), [qk_tok, t_vv, t_d], forget_terms)
        for u in us[16:]:
            u["need"] = {0: "second", 5: "own"}
        fill = fox_fill()
        root_tables()
        attention(us, finish_fox, fill, lambda i: i % 5 < 4, True)
        hidh.free = hidl.free = [ho[7][0], ho[7][1], (pe.sem, pe.n)]
        outs = [drain(fill), group("o", 1, hh.ap, hl.ap, ho, "T")]
        hh.free = hl.free = [outs[1][1]]
        half_g = sb("half_g", [128, 4, 8])
        hg = {}
        for n, i in enumerate((1, 5, 7, 11)):
            hg[i] = (half_g[:, n, :], ts(half_g[:, n, :], pcols("norm_g", i), 0.5, None, ALU.mult, after=[t_col]))

        prod = small[0:64, 56:58]
        el = small[:, 58:60]
        nlam = small[:, 60:61]
        lp = col[0:64, COL["lam"]:COL["lam"] + 4].rearrange("p (a b) -> p a b", b=2)
        t = tt(prod, lp[:, :, 0], lp[:, :, 1], ALU.mult, [t_col])
        b = misc.take()
        t = mm(b.ap[:, 0:2], ones[0:64, :], prod, True, True, [t, b.free], sig=True)
        t = activation(el, b.ap[:, 0:2], ACT.Exp, [t])
        b.free = [t]
        t_lam = stt(nlam, el[:, 1:2], LAMBDA_INIT, el[:, 0:1], ALU.subtract, ALU.subtract, [t])
        sub8 = small[:, 61:62]
        t_sub = ts(sub8, colat("subln"), 1.0 - LAMBDA_INIT, None, ALU.mult, after=[t_col])

        htok = after_mix(1, outs)
        outs = swiglu("1", htok)
        s1, t1 = scaled(pcols("post_ffn_g", 1), 11, False)
        htok = residual(outs, s1, [t1], nxt=pcols("norm_g", 0))

        def ffn2(tag, htok, post, nxt):
            outs = swiglu(tag, htok, True)
            return residual(outs, hg[post][0], [hg[post][1]], state["e2"], nxt, nxt is not None)

        rcol = small[:, 62:64]

        def rs_column():
            b = misc.take()
            for n in range(2):
                t = mm(b.ap[:, n:n + 1], rsx.ap[0:1, 128 * n:128 * n + 128], ones[0:1, 0:1], True, True,
                       [state["x"], b.free], sig=(n == 1))
            b.free = [dve.op(lambda e: e.tensor_copy(rcol, b.ap[:, 0:2]), [t])]
            return b.free[0]

        def scaled_rows(dst, p, after):
            for n in range(2):
                t = activation(dst[:, n, :], p.rows[:, n, :], ACT.Copy, after, scale=rcol[:, n:n + 1])
            p.release(t)
            return t

        htok = ffn2("2", htok, 1, pcols("norm_g", 2))

        aq = place("aq", [128, 4, T], F32, big)
        ak = place("ak", [128, 4, T], F32, big + 4096)
        av = place("av", [128, 2, 512], F32, big + 8192)
        bq = place("bq", [128, 4, T], F32, big + 12288)
        bk = place("bk", [128, 4, T], F32, big + 16384)
        bv = place("bv", [128, 2, 512], F32, big + 20480)
        ix = place("ix", [128, 3, T], F32, big + 24576)
        iw = place("iw", [128, 2, 8], F32, big + 27648)
        sc = place("sc", [128, 2, T], F32, big + 28672)
        sel = place("sel", [128, 2, T], F32, big + 30720)
        rl = Ring([Slot(place(f"rl{i}", [128, 512], F32, big + 32768 + 2048 * i)) for i in range(3)])
        oa = place("oa", [128, 4, T], F32, big + 38912)
        turned = cact[:, 0:2 * T].rearrange("p (n t) -> p n t", n=2)
        top8 = place("top8", [128, 2, 8], F32, big + 43008)
        big_free = hidh.free
        for s in rl.slots:
            s.free = [big_free]

        tables = {}
        p, t = group("idx", 0, hh.ap, hl.ap, htok, "T", late_stats)
        for n, name in enumerate(("cos32", "sin32", "cos64", "sin64")):
            o = Sb.slots[n].ap[:, :] if n < 2 else turned[:, n - 2, :]
            tables[name] = (o, tt(o, C(name), rsx.ap[:, :], ALU.mult, [state["x"], Sb.slots[n].free, t_cst]))
        t_rc = rs_column()

        def rope(p, t0, nt, kind, dst, scale, toks, then=None):
            (cos, tc), (sin, tn) = tables["cos" + kind], tables["sin" + kind]
            a = ta.take()
            t = activation(a.ap[:, :, :], p.tiles, ACT.Copy, [t0, a.free])
            p.release(t)

            def rest():
                s = tb.take()
                t1 = stt(dst, a.ap[:, 0:nt, :], scale, bc4(cos, nt), ALU.mult, ALU.mult, [t, tc, big_free])
                for n in range(2):
                    b = state["small"].take()
                    w = min(2, nt - 2 * n)
                    for m in range(w):
                        tm = mm(b.ap[:, 256 * m:256 * m + 256], C("rot" + kind), a.ap[:, 2 * n + m, :], m == 0, True,
                                [t, b.free], sig=(m == w - 1))
                    t2 = stt(s.ap[:, 2 * n:2 * n + w, :], b.ap[:, 0:256 * w].rearrange("p (m t) -> p m t", m=w), scale,
                             bc4(sin, w), ALU.mult, ALU.mult, [tm, tn, s.free])
                    b.free = [t2]
                t3 = tt(dst, dst, s.ap[:, 0:nt, :], ALU.add, [t1, t2])
                s.free = [t3]
                a.free = [t1, tm]
                toks.append(t3)
                if then:
                    then(a, t)
            return rest

        t_ix, t_iw, t_aq, t_ak, t_bq, t_bk = [], [], [], [], [], []

        def index_weights(a, t_raw):
            b = misc.take()
            for n in range(2):
                t = transpose(b.ap[:, 128 * n:128 * n + 128], a.ap[:, 3, 128 * n:128 * n + 128], ident,
                              [t_raw, b.free], sig=(n == 1))
            a.free = [a.free, t]
            for n in range(2):
                b.free = [ts(iw[:, n, :], b.ap[:, 128 * n:128 * n + 8], rcol[:, n:n + 1], 0.0625, ALU.mult, ALU.mult,
                             after=[t, t_rc, big_free])]
            t_iw.append(b.free[0])

        rest = rope(p, t, 3, "32", ix[:, :, :], 1.0, t_ix, index_weights)
        p, t = group("aqkv", 0, hh.ap, hl.ap, htok, "T", rest)
        rest = rope(p, t, 4, "64", aq[:, :, :], 0.125, t_aq)
        p, t = group("aqkv", 1, hh.ap, hl.ap, htok, "T", rest)
        rest = rope(p, t, 4, "64", ak[:, :, :], 1.0, t_ak)

        t_acc = None
        for qb in (1, 0):
            nk = 128 * (qb + 1)
            for jj in (0, 1):
                pp = [pairs.take(), pairs.take()]
                bk4 = [pp[0].b[0], pp[0].b[1], pp[1].b[0], pp[1].b[1]]
                for j in range(4):
                    h = 4 * jj + j
                    r = slice(32 * j, 32 * j + 32)
                    t = mm(bk4[j].ap[:, 0:nk], ix[r, jj, 128 * qb:128 * qb + 128], ix[r, 2, 0:nk], True, True,
                           [t_ix, bk4[j].free], sig=True)
                    s = rl.take()
                    t = activation(s.ap[:, 0:nk], bk4[j].ap[:, 0:nk], ACT.Relu, [t, s.free])
                    bk4[j].free = [t]
                    o = sc[:, qb, 0:nk]
                    if h == 0:
                        t = ts(o, s.ap[:, 0:nk], iw[:, qb, 0:1], None, ALU.mult, after=[t, t_iw])
                    else:
                        t = stt(o, s.ap[:, 0:nk], iw[:, qb, h:h + 1], o, ALU.mult, ALU.add, [t, t_acc])
                    s.free = [t]
                    t_acc = t
            o = sc[:, qb, 0:nk]
            t_acc = tt(o, o, cmask("chunk")(qb), ALU.add, [t_acc, t_cst])
        state["top"] = t_acc

        def top64(qb, rounds=1):
            nk = 128 * (qb + 1)
            s8, o = top8[:, qb, :], sc[:, qb, 0:nk]
            for _ in range(rounds):
                t = dve.op(lambda e, a=s8, b=o: e.max(a, b), [state["top"]])
                state["top"] = dve.op(lambda e, a=s8, b=o: e.match_replace(b, a, b, GONE), [t])

        p, t = group("aqkv", 2, hh.ap, hl.ap, htok, "N", rest)
        t_av = scaled_rows(av, p, [t, t_rc, big_free])
        for o in Sb.slots:
            o.free = [o.free, t_ix, t_iw]
        t_bv, t_sel = [], []

        def a_fill():
            P = pairs.slots[0]
            for g, dst, scale, toks in ((0, bq, 0.125, t_bq), (1, bk, 1.0, t_bk)):
                steps = group_steps("bqkv", g, hh.ap, hl.ap, htok, "T", pair=P)
                for i in range(8):
                    next(steps)
                    top64(i % 2)
                    yield
                p, t = drain(steps)
                rest = rope(p, t, 4, "64", dst[:, :, :], scale, toks)
                yield
                yield
                rest()
            for qb in range(2):
                nk = 128 * (qb + 1)
                o = sel[:, qb, 0:nk]
                t = ts(o, sc[:, qb, 0:nk], -3.15e38, BIG, ALU.is_lt, ALU.mult, after=[state["top"]])
                t_sel.append(ts(o, o, BIG, None, ALU.subtract, after=[t]))
            state["b"] = True
            p, t = yield from group_steps("bqkv", 2, hh.ap, hl.ap, htok, "N", pair=P)
            hh.free = hl.free = [t]
            t_bv.append(scaled_rows(bv, p, [t, t_rc, big_free]))
            rsx.free = [t_rc]
            state["bv"] = True
            while len(oa_tok) < 4:
                yield
            return (yield from b_fill())

        us = []
        for h in range(4):
            for qb in range(2):
                nk = 128 * (qb + 1)
                subs = [[(0, nk, aq[r, h, 128 * qb:128 * qb + 128], ak[r, h, 0:nk])] for r in (slice(0, 64), slice(64, 128))]
                us.append(dict(subs=subs, nk=nk, mask=cmask("chunk")(qb), after=[t_aq, t_ak], rows=slice(0, 128),
                               tile=h, qb=qb, v=(lambda kb, h=h: av[:, kb, 128 * h:128 * h + 128]), vtok=[t_av],
                               last=(qb == 1)))
        oa_tok = []

        def finish_a(tile, b, t):
            yield
            t = dve.op(lambda e, o=oa[:, tile, :], i=b.ap[:, 0:T]: e.tensor_copy(o, i), [t, big_free])
            b.free = [t]
            oa_tok.append(t)

        ho = [None] * 8

        def b_fill():
            a = ta.take()
            t = activation(a.ap[:, :, :], oa[:, :, :], ACT.Square, [oa_tok, a.free])
            s = tb.take()
            yield
            for n in range(2):
                b = state["small"].take()
                for m in range(2):
                    tm = mm(b.ap[:, 256 * m:256 * m + 256], ones, a.ap[:, 2 * n + m, :], m == 0, True, [t, b.free],
                            sig=(m == 1))
                b.free = [activation(s.ap[:, 2 * n:2 * n + 2, :], b.ap.rearrange("p (m t) -> p m t", m=2), ACT.Ln,
                                     [tm, s.free], bias=eps[:, 0:1], scale=1.0 / 128)]
            tn = activation(s.ap[:, :, :], s.ap[:, :, :], ACT.Exp, [b.free], scale=-0.5)
            a.free = [tm]
            yield
            t = stt(oa[:, :, :], oa[:, :, :], sub8, s.ap[:, :, :], ALU.mult, ALU.mult, [tn, oa_tok, t_sub])
            s.free = [t]
            ho[0:4] = [split(hh.ap[:, 0:4, :], hl.ap[:, 0:4, :], oa[:, :, :], t, [hh.free, hl.free])] * 4
            yield
            steps = group_steps("even_out", 0, hh.ap, hl.ap, ho, "T", pair=pairs.slots[0])
            return (yield from first_piece(steps, ho))

        def finish_b(tile, b, t):
            yield
            th = activation(hh.ap[:, tile, :], b.ap[:, 0:T], ACT.Copy, [t, hh.free])
            yield
            tl = tt(hl.ap[:, tile, :], b.ap[:, 0:T], hh.ap[:, tile, :], ALU.subtract, [th, hl.free])
            b.free = [th, tl]
            ho[tile] = (th, tl)

        more = plain_units(bq, bk, bv, lambda qb: sel[:, qb, 0:128 * (qb + 1)], [t_bq, t_bk, t_bv, t_sel], heads=8)
        for u in more:
            u["tile"] += 4
            u["need"] = {0: "b", 5: "bv"}
        fill = a_fill()
        attention(us + more, lambda tile, b, t: (finish_a if tile < 4 else finish_b)(tile, b, t), fill,
                  lambda i: 3 if i < 9 else 1, True)
        hidh.free = hidl.free = [ho[3][0], ho[3][1], ho[7][0], ho[7][1], (pe.sem, pe.n)]
        outs = [drain(fill), group("even_out", 1, hh.ap, hl.ap, ho, "T")]
        hh.free = hl.free = [outs[1][1]]
        htok = residual(outs, pcols("norm_g", 3), [], nxt=pcols("norm_g", 4))
        htok = ffn2("3", htok, 5, pcols("norm_g", 6))
        htok = ffn2("4", htok, 7, pcols("norm_g", 8))

        big_free = hidh.free
        oq = place("oq", [128, 8, T], F32, big)
        ok = place("ok", [128, 8, T], F32, big + 8192)
        ov = place("ov", [128, 2, 1024], F32, big + 16384)
        bT = place("bT", [128, 16, T], F32, big + 24576)
        t_rel = load("rel", bT[:, :, :], rel_d, [big_free])
        t_q, t_k, t_v = [], [], []

        def odd_steps(g, pair=None, first=None):
            tiles = slice(4 * g, 4 * g + 4)
            p, t = yield from group_steps("odd", 3 * g, hh.ap, hl.ap, htok, "T", first, pair=pair)
            if first:
                state["rc"] = rs_column()
            t_q.append(stt(oq[:, tiles, :], p.tiles, 0.125, bc4(rsx.ap[:, :]), ALU.mult, ALU.mult,
                           [t, state["x"], big_free]))
            p.release(t_q[-1])
            yield
            p, t = yield from group_steps("odd", 3 * g + 1, hh.ap, hl.ap, htok, "T", pair=pair)
            t_k.append(tt(ok[:, tiles, :], p.tiles, bc4(rsx.ap[:, :]), ALU.mult, [t, big_free]))
            p.release(t_k[-1])
            if g == 1:
                state["second"] = True
            yield
            p, t = yield from group_steps("odd", 3 * g + 2, hh.ap, hl.ap, htok, "N", pair=pair)
            t_v.append(scaled_rows(ov[:, :, 512 * g:512 * g + 512], p, [t, state["rc"], big_free]))
            return t

        drain(odd_steps(0, None, late_stats))
        ho = [None] * 8

        def odd_fill():
            del state["own"], state["second"]
            hh.free = hl.free = [(yield from odd_steps(1, pairs.slots[0]))]
            rsx.free = [t_k, state["rc"]]
            state["own"] = True
            split_waiting(oq)
            steps = group_steps("odd_out", 0, hh.ap, hl.ap, ho, "T", pair=pairs.slots[0])
            return (yield from first_piece(steps, ho))

        def finish_odd(tile, b, t):
            yield
            o = oq[:, tile, :]
            t = dve.op(lambda e, i=b.ap[:, 0:T]: e.tensor_copy(o, i), [t])
            b.free = [t]
            if "own" in state:
                yield
                yield from split_steps(tile, o, t)
            else:
                waiting.append((tile, t))

        us = plain_units(oq, ok, ov, lambda qb: None, [t_q, t_k, t_v, t_rel])
        for n, u in enumerate(us):
            u["mask"] = bT[:, n // 2, 256 - u["nk"]:256]
            if n >= 16:
                u["need"] = {0: "second", 5: "own"}
        fill = odd_fill()
        next(fill)
        attention(us, finish_odd, fill, lambda i: 1, True)
        hidh.free = hidl.free = [ho[7][0], ho[7][1], (pe.sem, pe.n)]
        outs = [drain(fill), group("odd_out", 1, hh.ap, hl.ap, ho, "T")]
        hh.free = hl.free = [outs[1][1]]
        htok = residual(outs, pcols("norm_g", 9), [], nxt=pcols("norm_g", 10))
        ffn2("5", htok, 11, None)

        s_out = Slot(None, sem("s_out"))
        ov_d = out_d.rearrange("(k p) t -> p k t", p=128)
        for i in range(2):
            t = sp.dma(lambda e, i=i: e.dma_start(ov_d[:, 4 * i:4 * i + 4, :], x[:, 4 * i:4 * i + 4, :]), s_out,
                       [x_tok[4 * i:4 * i + 4]])
        sp.wait([t])
        assert state["use"] == len(items)

        block = ctx.enter_context(nc.Block())

        @block.sync
        def _(e):
            sp.play(e)

        @block.gpsimd
        def _(e):
            pool.play(e)

        @block.scalar
        def _(e):
            act.play(e)

        @block.vector
        def _(e):
            dve.play(e)

        @block.tensor
        def _(e):
            pe.play(e)



def pack_stream(inputs):
    items, total = stream()
    out = np.empty((total,), np.float32)
    for kind, off, parts, k0, kt, n, tag in items:
        blocks = []
        for src, lead, g in parts:
            a = inputs[src]
            for i in lead:
                a = a[i]
            a = a[128 * k0:128 * (k0 + kt)]
            for p in g:
                if p[0] == "zero":
                    blocks.append(np.zeros((128 * kt, p[1]), np.float32))
                else:
                    blocks.append(a[:, p[1]:p[2]])
        w = blocks[0] if len(blocks) == 1 else np.concatenate(blocks, axis=1)
        if kind == "ada":
            w = w.reshape(1024, 2, 128).transpose(2, 1, 0)
        else:
            w = w.reshape(kt, 128, n).transpose(1, 0, 2)
        out[off:off + 128 * kt * n] = w.reshape(-1)
    return out


def pack_columns(inputs):
    def c(a):
        return np.asarray(a).reshape(-1, 128).T

    f16 = inputs["kv_b_f"]
    lam = inputs["even_lambda_2"][0].T
    made = {
        "ada_b": c(inputs["ada_b"]), "kv_ada_b": c(inputs["kv_ada_b"]),
        "pre_mix_g": c(inputs["pre_mix_g"]), "post_mix_g": c(inputs["post_mix_g"]),
        "pre_ffn_g": c(inputs["pre_ffn_g"]), "post_ffn_g": c(inputs["post_ffn_g"]),
        "kv_norm_g": c(inputs["kv_norm_g"]), "a_b_u": c(inputs["a_b_in"][0, :2048]),
        "a_ln_g": c(inputs["a_ln_g"]), "a_ln_b": c(inputs["a_ln_b"]), "norm_g": c(inputs["norm_g_2"]),
        "subln": c(inputs["even_subln_2"]), "q_norm": c(np.tile(inputs["b_q_norm_g"][0], 2)),
        "k_norm": c(np.tile(inputs["k_norm_g"], 2)), "b_f": c(np.tile(f16, 8)),
        "lam": np.concatenate([lam, np.zeros((64, 4), np.float32)], axis=0),
    }
    return np.ascontiguousarray(np.concatenate([made[n] for n, _ in COLS], axis=1))


def lay_out_bias(rel):
    q, k = np.arange(128)[:, None] + 128, np.arange(T)[None, :]
    out = rel[:, np.maximum(q - k + 63, 0)].transpose(1, 0, 2)
    return np.ascontiguousarray(np.where((k // 64 <= q // 64)[:, None, :], out, np.float32(-BIG)))


def kernel(**inputs):
    import concourse.bacc as _bacc
    from concourse.bass_utils import run_bass_kernel_spmd as _run

    inputs = {k: np.asarray(a) for k, a in inputs.items()}
    arrays = {
        "c": np.ascontiguousarray(inputs["c"].reshape(-1)),
        "w": pack_stream(inputs), "cols": pack_columns(inputs), "csts": constants(),
        "xT": np.ascontiguousarray(inputs["x"][0].T),
        "bin": np.ascontiguousarray(inputs["a_b_in"][0, 2048:]),
        "bs": np.ascontiguousarray(inputs["a_b_s"][0].reshape(-1)),
        "ws": np.ascontiguousarray(inputs["a_w_s"][0].transpose(2, 0, 1).reshape(128, 2048)),
        "rel": lay_out_bias(inputs["odd_rel_bias_2"][0]),
    }
    nc = _bacc.Bacc("TRN2", target_bir_lowering=False, num_devices=1)
    aps = {n: nc.dram_tensor("in_" + n, a.shape, F32, kind="ExternalInput").ap() for n, a in arrays.items()}
    out = nc.dram_tensor("out_T", (D, T), F32, kind="ExternalOutput").ap()
    build(nc, aps["c"], aps["w"], aps["cols"], aps["csts"], aps["xT"], aps["bin"], aps["bs"], aps["ws"], aps["rel"], out)
    r = _run(nc, [{"in_" + n: a for n, a in arrays.items()}], core_ids=[0])
    return np.ascontiguousarray(r.results[0]["out_T"].T)[None]
```
